# Optimizing a Trainium2 kernel written in Bass

```python
import jax, jax.numpy as jnp
from jax import lax
import numpy as np
import math

D_MODEL = 2048
BATCH = 1
SEQ = 256
DEPTH = 2

HEAD_DIM = 128
D_MIX = D_MODEL
N_HEADS_A = 10
N_HEADS_B = 6
N_HEADS_C = 8
N_HEADS_D = 8
IDX_HEADS = 16
IDX_DIM = 64
TOPK_MAX = 256
DILATED = ((128, 1), (512, 4), (2048, 16))
BLOCK = 128
ROPE_THETA = 10000.0
EPS = 1e-6

A_Q = N_HEADS_A * HEAD_DIM
IDX_Q = IDX_HEADS * IDX_DIM
B_W = N_HEADS_B * HEAD_DIM
C_W = N_HEADS_C * HEAD_DIM
D_W = N_HEADS_D * HEAD_DIM
SPLIT0 = (A_Q, HEAD_DIM, HEAD_DIM, IDX_Q, IDX_DIM, IDX_HEADS, B_W, B_W, B_W, D_MIX)
SPLIT1 = (C_W, C_W, C_W, D_W, D_W, D_W, N_HEADS_D, D_MIX)
IN0 = sum(SPLIT0)
IN1 = sum(SPLIT1)


F32 = jnp.float32

def rmsnorm(x, g):
    xf = x.astype(F32)
    y = xf * lax.rsqrt(jnp.mean(xf * xf, axis=-1, keepdims=True) + EPS)
    return (y * g.astype(F32)).astype(x.dtype)

def rope(t, pos):
    half = t.shape[-1] // 2
    inv = ROPE_THETA ** (-jnp.arange(half, dtype=F32) / half)
    ang = pos.astype(F32)[:, None] * inv[None, :]
    cos = jnp.cos(ang)[None, :, None, :]
    sin = jnp.sin(ang)[None, :, None, :]
    tf = t.astype(F32)
    t1, t2 = tf[..., :half], tf[..., half:]
    return jnp.concatenate([t1 * cos - t2 * sin, t2 * cos + t1 * sin], axis=-1).astype(t.dtype)

def split_cols(t, sizes):
    offs, acc = [], 0
    for s in sizes[:-1]:
        acc += s
        offs.append(acc)
    return jnp.split(t, offs, axis=-1)

def blocks_to_seq(out):
    nb, bsz, q, h, d = out.shape
    return out.transpose(1, 0, 2, 3, 4).reshape(bsz, nb * q, h, d)

def dsa_attention(q, k, v, iq, ik, iw):
    S = q.shape[1]
    topk = min(TOPK_MAX, S // 4)
    key_pos = jnp.arange(S)
    ikf = ik.astype(F32)

    def block(b):
        start = b * BLOCK
        qb = lax.dynamic_slice_in_dim(q, start, BLOCK, axis=1)
        iqb = lax.dynamic_slice_in_dim(iq, start, BLOCK, axis=1).astype(F32)
        iwb = lax.dynamic_slice_in_dim(iw, start, BLOCK, axis=1).astype(F32)
        qpos = start + jnp.arange(BLOCK)
        dots = jnp.einsum('bqhd,bsd->bqhs', iqb, ikf) * (IDX_DIM ** -0.5)
        score = jnp.einsum('bqh,bqhs->bqs', iwb * (IDX_HEADS ** -0.5), jax.nn.relu(dots))
        causal = key_pos[None, :] <= qpos[:, None]
        score = jnp.where(causal[None], score, -jnp.inf)
        _, sel = lax.top_k(score, topk)
        valid = sel <= qpos[None, :, None]
        ks = jax.vmap(lambda kk, ii: kk[ii])(k, sel)
        vs = jax.vmap(lambda vv, ii: vv[ii])(v, sel)
        logits = jnp.einsum('bqhd,bqkd->bqhk', qb, ks).astype(F32) * (HEAD_DIM ** -0.5)
        logits = jnp.where(valid[:, :, None, :], logits, -jnp.inf)
        p = jax.nn.softmax(logits, axis=-1)
        return jnp.einsum('bqhk,bqkd->bqhd', p.astype(v.dtype), vs)

    return blocks_to_seq(lax.map(block, jnp.arange(S // BLOCK)))

def strided_band(q, k, v, dil, steps):
    bsz, S, H, hd = q.shape
    L = S // dil
    nb = -(-L // BLOCK)
    Lp = nb * BLOCK

    def to_blocks(t):
        t = t.reshape(bsz, L, dil, H, hd).transpose(0, 2, 1, 3, 4)
        t = jnp.pad(t, ((0, 0), (0, 0), (0, Lp - L), (0, 0), (0, 0)))
        return t.reshape(bsz, dil, nb, BLOCK, H, hd)

    def with_prev(t):
        prev = jnp.pad(t, ((0, 0), (0, 0), (1, 0), (0, 0), (0, 0), (0, 0)))[:, :, :-1]
        return jnp.concatenate([prev, t], axis=3)

    qb = to_blocks(q)
    kk = with_prev(to_blocks(k))
    vv = with_prev(to_blocks(v))
    logits = jnp.einsum('brnqhd,brnkhd->brnhqk', qb, kk).astype(F32) * (HEAD_DIM ** -0.5)
    qi = jnp.arange(BLOCK)[:, None] + BLOCK
    ki = jnp.arange(2 * BLOCK)[None, :]
    dist = qi - ki
    band = (dist >= 0) & (dist <= steps)
    blk = jnp.arange(nb)[:, None, None]
    valid = band[None] & ((ki[None] >= BLOCK) | (blk > 0))
    logits = jnp.where(valid[None, None, :, None], logits, -jnp.inf)
    m = jnp.max(logits, axis=-1, keepdims=True)
    p = jnp.exp(logits - m)
    l = jnp.sum(p, axis=-1, keepdims=True)
    o = jnp.einsum('brnhqk,brnkhd->brnhqd', p, vv.astype(F32)) / l
    lse = (m + jnp.log(l))[..., 0]
    o = o.transpose(0, 1, 2, 4, 3, 5).reshape(bsz, dil, Lp, H, hd)[:, :, :L]
    o = o.transpose(0, 2, 1, 3, 4).reshape(bsz, S, H, hd)
    lse = lse.transpose(0, 1, 2, 4, 3).reshape(bsz, dil, Lp, H)[:, :, :L]
    lse = lse.transpose(0, 2, 1, 3).reshape(bsz, S, H)
    return o, lse

def dilated_attention(q, k, v):
    outs, lses = [], []
    for window, dil in DILATED:
        o, lse = strided_band(q, k, v, dil, window // dil)
        outs.append(o)
        lses.append(lse)
    alpha = jax.nn.softmax(jnp.stack(lses, axis=0), axis=0)
    o = jnp.einsum('pbsh,pbshd->bshd', alpha, jnp.stack(outs, axis=0))
    return o.astype(q.dtype)

def stick_breaking_attention(q, k, v):
    S = q.shape[1]
    key_pos = jnp.arange(S)

    def block(b):
        start = b * BLOCK
        qb = lax.dynamic_slice_in_dim(q, start, BLOCK, axis=1)
        qpos = start + jnp.arange(BLOCK)
        z = jnp.einsum('bqhd,bshd->bhqs', qb, k).astype(F32) * (HEAD_DIM ** -0.5)
        before = (key_pos[None, :] < qpos[:, None])[None, None]
        log_1m = jnp.where(before, jax.nn.log_sigmoid(-z), 0.0)
        tail = lax.cumsum(log_1m, axis=3, reverse=True) - log_1m
        w = jnp.where(before, jnp.exp(jax.nn.log_sigmoid(z) + tail), 0.0)
        return jnp.einsum('bhqs,bshd->bqhd', w.astype(v.dtype), v)

    return blocks_to_seq(lax.map(block, jnp.arange(S // BLOCK)))

def forgetting_attention(q, k, v, log_f):
    S = q.shape[1]
    key_pos = jnp.arange(S)
    c = jnp.cumsum(log_f.astype(F32), axis=1).transpose(0, 2, 1)

    def block(b):
        start = b * BLOCK
        qb = lax.dynamic_slice_in_dim(q, start, BLOCK, axis=1)
        cb = lax.dynamic_slice_in_dim(c, start, BLOCK, axis=2)
        qpos = start + jnp.arange(BLOCK)
        logits = jnp.einsum('bqhd,bshd->bhqs', qb, k).astype(F32) * (HEAD_DIM ** -0.5)
        logits = logits + (cb[..., :, None] - c[..., None, :])
        causal = (key_pos[None, :] <= qpos[:, None])[None, None]
        p = jax.nn.softmax(jnp.where(causal, logits, -jnp.inf), axis=-1)
        return jnp.einsum('bhqs,bshd->bqhd', p.astype(v.dtype), v)

    return blocks_to_seq(lax.map(block, jnp.arange(S // BLOCK)))

def layer_even(x, norm_g, w_in, w_out):
    bsz, S, _ = x.shape
    pos = jnp.arange(S)
    h = rmsnorm(x, norm_g)
    qa, ka, va, iq, ik, iw, qb, kb, vb, gate = split_cols(h @ w_in, SPLIT0)
    qa = rope(qa.reshape(bsz, S, N_HEADS_A, HEAD_DIM), pos)
    ka = rope(ka.reshape(bsz, S, 1, HEAD_DIM), pos)[:, :, 0]
    iq = rope(iq.reshape(bsz, S, IDX_HEADS, IDX_DIM), pos)
    ik = rope(ik.reshape(bsz, S, 1, IDX_DIM), pos)[:, :, 0]
    o_a = dsa_attention(qa, ka, va, iq, ik, iw)
    qb = rope(qb.reshape(bsz, S, N_HEADS_B, HEAD_DIM), pos)
    kb = rope(kb.reshape(bsz, S, N_HEADS_B, HEAD_DIM), pos)
    vb = vb.reshape(bsz, S, N_HEADS_B, HEAD_DIM)
    o_b = dilated_attention(qb, kb, vb)
    y = jnp.concatenate([o_a.reshape(bsz, S, A_Q), o_b.reshape(bsz, S, B_W)], axis=-1)
    return x + (y * jax.nn.silu(gate)) @ w_out

def layer_odd(x, norm_g, w_in, b_f, w_out):
    bsz, S, _ = x.shape
    h = rmsnorm(x, norm_g)
    qc, kc, vc, qd, kd, vd, fl, gate = split_cols(h @ w_in, SPLIT1)
    shp_c = (bsz, S, N_HEADS_C, HEAD_DIM)
    shp_d = (bsz, S, N_HEADS_D, HEAD_DIM)
    o_c = stick_breaking_attention(qc.reshape(shp_c), kc.reshape(shp_c), vc.reshape(shp_c))
    log_f = jax.nn.log_sigmoid(fl.astype(F32) + b_f.astype(F32))
    o_d = forgetting_attention(qd.reshape(shp_d), kd.reshape(shp_d), vd.reshape(shp_d), log_f)
    y = jnp.concatenate([o_c.reshape(bsz, S, C_W), o_d.reshape(bsz, S, D_W)], axis=-1)
    return x + (y * jax.nn.silu(gate)) @ w_out

def first_inputs(seed: int = 0) -> dict:
    key = jax.random.key(seed)
    ks = jax.random.split(key, 10)
    nrm = jax.random.normal
    return {
        'x': nrm(ks[0], (BATCH, SEQ, D_MODEL), F32),
        'norm0': 1.0 + 0.02 * nrm(ks[1], (D_MODEL,), F32),
        'w_in0': nrm(ks[2], (D_MODEL, IN0), F32) * D_MODEL ** -0.5,
        'w_out0': nrm(ks[3], (D_MIX, D_MODEL), F32) * D_MIX ** -0.5,
        'norm1': 1.0 + 0.02 * nrm(ks[4], (D_MODEL,), F32),
        'w_in1': nrm(ks[5], (D_MODEL, IN1), F32) * D_MODEL ** -0.5,
        'b_f1': 2.0 + 0.5 * nrm(ks[6], (N_HEADS_D,), F32),
        'w_out1': nrm(ks[7], (D_MIX, D_MODEL), F32) * D_MIX ** -0.5,
        'norm_f': 1.0 + 0.02 * nrm(ks[8], (D_MODEL,), F32),
    }

def first_block(x, norm0, w_in0, w_out0, norm1, w_in1, b_f1, w_out1, norm_f):
    for i in range(DEPTH):
        if i % 2 == 0:
            x = layer_even(x, norm0, w_in0, w_out0)
        else:
            x = layer_odd(x, norm1, w_in1, b_f1, w_out1)
    return rmsnorm(x, norm_f)


DEPTH_2 = 1

GDN_HEADS = 8
GDN_HEAD_DIM = 128
GDN_WIDTH = GDN_HEADS * GDN_HEAD_DIM
GDN_CONV = 4
GDN_CHUNK = 64
RWKV_HEAD_DIM = 64
RWKV_HEADS = 16
RWKV_WIDTH = RWKV_HEADS * RWKV_HEAD_DIM
RWKV_DECAY_LORA = 96
RWKV_ICLR_LORA = 96
RWKV_SHIFT_COLS = 3 * RWKV_WIDTH + RWKV_DECAY_LORA + RWKV_ICLR_LORA
RWKV_LN_EPS = 64e-5
S5_GROUP = 16
S5_WIDTH = 1024
S5_GROUPS = S5_WIDTH // S5_GROUP
S5_STATE = 64
N_BRANCH = 3
BRANCH_WIDTH = 1024
NORM_EPS = 1e-6

SPLIT_SIZES = (3 * GDN_WIDTH, GDN_WIDTH, GDN_HEADS, GDN_HEADS,
               RWKV_SHIFT_COLS, RWKV_WIDTH,
               S5_WIDTH, S5_WIDTH,
               N_BRANCH * D_MODEL)
IN_COLS = sum(SPLIT_SIZES)


def _split_cols(t, sizes):
    out, start = [], 0
    for s in sizes:
        out.append(t[..., start:start + s])
        start += s
    return out

def rms_norm(x, w, eps=NORM_EPS):
    xf = x.astype(jnp.float32)
    y = xf * lax.rsqrt(jnp.mean(xf * xf, axis=-1, keepdims=True) + eps)
    return (y * w.astype(jnp.float32)).astype(x.dtype)

def l2_normalize(x, eps=1e-6):
    return x * lax.rsqrt(jnp.sum(x * x, axis=-1, keepdims=True) + eps)

def causal_depthwise_conv(x, w):
    k_width, ch = w.shape
    return lax.conv_general_dilated(x, w[:, None, :].astype(x.dtype), window_strides=(1,),
                                    padding=[(k_width - 1, 0)],
                                    dimension_numbers=('NWC', 'WIO', 'NWC'),
                                    feature_group_count=ch)

def _to_chunks(t, n):
    bsz, _, h = t.shape[:3]
    t = t.reshape((bsz, n, GDN_CHUNK, h) + t.shape[3:])
    return t.transpose((1, 0, 3, 2) + tuple(range(4, t.ndim)))

def gated_delta_rule_chunked(q, k, v, beta, g):
    bsz, seq, h, dk = q.shape
    dv = v.shape[-1]
    n = seq // GDN_CHUNK
    q, k, v, beta, g = (_to_chunks(t, n) for t in (q, k, v, beta, g))
    g_cum = jnp.cumsum(g, axis=-1)
    idx = jnp.arange(GDN_CHUNK)
    strict = idx[:, None] > idx[None, :]
    incl = idx[:, None] >= idx[None, :]
    diff = g_cum[..., :, None] - g_cum[..., None, :]
    decay_strict = jnp.exp(jnp.where(strict, diff, -jnp.inf))
    decay_incl = jnp.exp(jnp.where(incl, diff, -jnp.inf))
    k_beta = k * beta[..., None]
    lower = jnp.einsum('nbhcd,nbhsd->nbhcs', k_beta, k) * decay_strict
    eye = jnp.eye(GDN_CHUNK, dtype=q.dtype)
    t_mat = lax.linalg.triangular_solve(eye + lower, jnp.broadcast_to(eye, lower.shape),
                                        left_side=True, lower=True)
    u = jnp.einsum('nbhcs,nbhse->nbhce', t_mat, v * beta[..., None])
    w = jnp.einsum('nbhcs,nbhsd->nbhcd', t_mat, k_beta * jnp.exp(g_cum)[..., None])
    attn = jnp.einsum('nbhcd,nbhsd->nbhcs', q, k) * decay_incl
    q_dec = q * jnp.exp(g_cum)[..., None]
    g_last = g_cum[..., -1]
    k_dec = k * jnp.exp(g_last[..., None] - g_cum)[..., None]

    def step(state, xs):
        q_i, k_i, u_i, w_i, a_i, gl_i = xs
        v_new = u_i - jnp.einsum('bhcd,bhde->bhce', w_i, state)
        o_i = (jnp.einsum('bhcd,bhde->bhce', q_i, state)
               + jnp.einsum('bhcs,bhse->bhce', a_i, v_new))
        state = state * jnp.exp(gl_i)[..., None, None] + jnp.einsum('bhcd,bhce->bhde', k_i, v_new)
        return state, o_i

    s0 = jnp.zeros((bsz, h, dk, dv), jnp.float32)
    _, o = lax.scan(step, s0, (q_dec, k_dec, u, w, attn, g_last))
    return o.transpose(1, 0, 3, 2, 4).reshape(bsz, seq, h, dv)

def gdn_branch(qkv, z, b_logit, a_logit, conv_w, a_log, dt_bias, norm_w):
    bsz, seq, _ = qkv.shape
    qkv = jax.nn.silu(causal_depthwise_conv(qkv, conv_w)).astype(jnp.float32)
    q, k, v = jnp.split(qkv, 3, axis=-1)
    hs = (bsz, seq, GDN_HEADS, GDN_HEAD_DIM)
    q = l2_normalize(q.reshape(hs)) * (GDN_HEAD_DIM ** -0.5)
    k = l2_normalize(k.reshape(hs))
    v = v.reshape(hs)
    beta = jax.nn.sigmoid(b_logit.astype(jnp.float32))
    g = -jnp.exp(a_log.astype(jnp.float32)) * jax.nn.softplus(
        a_logit.astype(jnp.float32) + dt_bias.astype(jnp.float32))
    o = gated_delta_rule_chunked(q, k, v, beta, g)
    o = rms_norm(o, norm_w) * jax.nn.silu(z.astype(jnp.float32).reshape(hs))
    return o.reshape(bsz, seq, GDN_WIDTH)

def rwkv7_scan(r, w, k, v, kk, a):
    bsz, seq, h, n = r.shape

    def step(state, xs):
        r_t, w_t, k_t, v_t, kk_t, a_t = xs
        sa = jnp.einsum('bhvk,bhk->bhv', state, -kk_t)
        state = (state * w_t[:, :, None, :] + sa[..., None] * (kk_t * a_t)[:, :, None, :]
                 + v_t[..., None] * k_t[:, :, None, :])
        return state, jnp.einsum('bhvk,bhk->bhv', state, r_t)

    xs = tuple(t.transpose(1, 0, 2, 3) for t in (r, w, k, v, kk, a))
    s0 = jnp.zeros((bsz, h, n, n), jnp.float32)
    _, y = lax.scan(step, s0, xs)
    return y.transpose(1, 0, 2, 3)

def rwkv7_branch(feat, z, mu, w0, w_up, a0, a_up, k_k, k_a, r_k, lnx_w, lnx_b):
    bsz, seq, _ = feat.shape
    f32 = jnp.float32
    feat = feat.astype(f32)
    prev = jnp.pad(feat[:, :-1], ((0, 0), (1, 0), (0, 0)))
    feat = feat + (prev - feat) * mu.astype(f32)
    r, k, v, wl, al = _split_cols(feat, (RWKV_WIDTH,) * 3 + (RWKV_DECAY_LORA, RWKV_ICLR_LORA))
    w_pre = w0.astype(f32) + jnp.tanh(wl) @ w_up.astype(f32)
    decay = jnp.exp(-jnp.exp(-jax.nn.softplus(-w_pre) - 0.5))
    a = jax.nn.sigmoid(a0.astype(f32) + al @ a_up.astype(f32))
    hs = (bsz, seq, RWKV_HEADS, RWKV_HEAD_DIM)
    kk = l2_normalize((k * k_k.astype(f32)).reshape(hs))
    k = k * (1.0 + (a - 1.0) * k_a.astype(f32))
    r, k, v, a, decay = (t.reshape(hs) for t in (r, k, v, a, decay))
    y = rwkv7_scan(r, decay, k, v, kk, a)
    mean = jnp.mean(y, axis=-1, keepdims=True)
    var = jnp.mean(jnp.square(y - mean), axis=-1, keepdims=True)
    y = ((y - mean) * lax.rsqrt(var + RWKV_LN_EPS) * lnx_w.astype(f32).reshape(RWKV_HEADS, RWKV_HEAD_DIM)
         + lnx_b.astype(f32).reshape(RWKV_HEADS, RWKV_HEAD_DIM))
    y = y + jnp.sum(r * k * r_k.astype(f32), axis=-1, keepdims=True) * v
    y = y * jax.nn.silu(z.astype(f32).reshape(hs))
    return y.reshape(bsz, seq, RWKV_WIDTH)

def s5_branch(u, z, a_re, a_im, log_dt, b_re, b_im, c_re, c_im, d_skip, glu_w, glu_b):
    bsz, seq, _ = u.shape
    f32 = jnp.float32
    u = u.astype(f32)
    ug = u.reshape(bsz, seq, S5_GROUPS, S5_GROUP)
    a_re, a_im, b_re, b_im, c_re, c_im = (t.astype(f32) for t in (a_re, a_im, b_re, b_im, c_re, c_im))
    dt = jnp.exp(log_dt.astype(f32))[:, None]
    mag = jnp.exp(a_re * dt)
    ab_re, ab_im = mag * jnp.cos(a_im * dt), mag * jnp.sin(a_im * dt)
    den = a_re * a_re + a_im * a_im
    coef_re = ((ab_re - 1.0) * a_re + ab_im * a_im) / den
    coef_im = (ab_im * a_re - (ab_re - 1.0) * a_im) / den
    bb_re = coef_re[..., None] * b_re - coef_im[..., None] * b_im
    bb_im = coef_re[..., None] * b_im + coef_im[..., None] * b_re
    bu_re = jnp.einsum('gpc,blgc->blgp', bb_re, ug)
    bu_im = jnp.einsum('gpc,blgc->blgp', bb_im, ug)
    shp = (1, seq, S5_GROUPS, S5_STATE)
    a_re_t = jnp.broadcast_to(ab_re, shp)
    a_im_t = jnp.broadcast_to(ab_im, shp)

    def combine(e1, e2):
        a1r, a1i, b1r, b1i = e1
        a2r, a2i, b2r, b2i = e2
        return (a1r * a2r - a1i * a2i, a1r * a2i + a1i * a2r,
                a2r * b1r - a2i * b1i + b2r, a2r * b1i + a2i * b1r + b2i)

    _, _, s_re, s_im = lax.associative_scan(combine, (a_re_t, a_im_t, bu_re, bu_im), axis=1)
    y = jnp.einsum('gcp,blgp->blgc', c_re, s_re) - jnp.einsum('gcp,blgp->blgc', c_im, s_im)
    y = y.reshape(bsz, seq, S5_WIDTH) + d_skip.astype(f32) * u
    y = jax.nn.gelu(y)
    y = y * jax.nn.sigmoid(y @ glu_w.astype(f32) + glu_b.astype(f32))
    return y * jax.nn.silu(z.astype(f32))

def second_inputs(seed: int = 0) -> dict:
    key = jax.random.key(seed)
    ks = iter(jax.random.split(key, 40))
    f32 = jnp.float32

    def nrm(shape, s):
        return s * jax.random.normal(next(ks), shape, f32)

    def unif(shape, lo, hi):
        return jax.random.uniform(next(ks), shape, f32, lo, hi)

    gdn_dt = jnp.exp(unif((DEPTH_2, GDN_HEADS), math.log(1e-3), math.log(1e-1)))
    return {
        "x": nrm((BATCH, SEQ, D_MODEL), 1.0),
        "norm_w": 1.0 + nrm((DEPTH_2, D_MODEL), 0.02),
        "w_in": nrm((DEPTH_2, D_MODEL, IN_COLS), D_MODEL ** -0.5),
        "gdn_conv_w": nrm((DEPTH_2, GDN_CONV, 3 * GDN_WIDTH), GDN_CONV ** -0.5),
        "gdn_a_log": jnp.log(unif((DEPTH_2, GDN_HEADS), 1.0, 16.0)),
        "gdn_dt_bias": jnp.log(jnp.expm1(gdn_dt)),
        "gdn_norm_w": 1.0 + nrm((DEPTH_2, GDN_HEAD_DIM), 0.02),
        "rwkv_mu": unif((DEPTH_2, RWKV_SHIFT_COLS), 0.0, 1.0),
        "rwkv_w0": unif((DEPTH_2, RWKV_WIDTH), -6.5, -1.5),
        "rwkv_w_up": nrm((DEPTH_2, RWKV_DECAY_LORA, RWKV_WIDTH), 0.5 * RWKV_DECAY_LORA ** -0.5),
        "rwkv_a0": nrm((DEPTH_2, RWKV_WIDTH), 0.1),
        "rwkv_a_up": nrm((DEPTH_2, RWKV_ICLR_LORA, RWKV_WIDTH), 0.5 * RWKV_ICLR_LORA ** -0.5),
        "rwkv_k_k": 0.85 + nrm((DEPTH_2, RWKV_WIDTH), 0.05),
        "rwkv_k_a": 1.0 + nrm((DEPTH_2, RWKV_WIDTH), 0.05),
        "rwkv_r_k": nrm((DEPTH_2, RWKV_HEADS, RWKV_HEAD_DIM), 0.1),
        "rwkv_lnx_w": 1.0 + nrm((DEPTH_2, RWKV_WIDTH), 0.02),
        "rwkv_lnx_b": nrm((DEPTH_2, RWKV_WIDTH), 0.02),
        "s5_a_re": -0.5 + nrm((DEPTH_2, S5_GROUPS, S5_STATE), 0.01),
        "s5_a_im": jnp.pi * jnp.arange(S5_STATE, dtype=f32)[None, None, :] + nrm((DEPTH_2, S5_GROUPS, S5_STATE), 0.01),
        "s5_log_dt": unif((DEPTH_2, S5_GROUPS), math.log(1e-3), math.log(1e-1)),
        "s5_b_re": nrm((DEPTH_2, S5_GROUPS, S5_STATE, S5_GROUP), (2 * S5_GROUP) ** -0.5),
        "s5_b_im": nrm((DEPTH_2, S5_GROUPS, S5_STATE, S5_GROUP), (2 * S5_GROUP) ** -0.5),
        "s5_c_re": nrm((DEPTH_2, S5_GROUPS, S5_GROUP, S5_STATE), (2 * S5_STATE) ** -0.5),
        "s5_c_im": nrm((DEPTH_2, S5_GROUPS, S5_GROUP, S5_STATE), (2 * S5_STATE) ** -0.5),
        "s5_d": nrm((DEPTH_2, S5_WIDTH), 1.0),
        "s5_glu_w": nrm((DEPTH_2, S5_WIDTH, S5_WIDTH), S5_WIDTH ** -0.5),
        "s5_glu_b": nrm((DEPTH_2, S5_WIDTH), 0.02),
        "gate_b": nrm((DEPTH_2, N_BRANCH, D_MODEL), 0.02),
        "w_branch": nrm((DEPTH_2, N_BRANCH, BRANCH_WIDTH, D_MODEL), BRANCH_WIDTH ** -0.5),
        "w_out": nrm((DEPTH_2, D_MODEL, D_MODEL), D_MODEL ** -0.5),
        "final_norm_w": 1.0 + nrm((D_MODEL,), 0.02),
    }

def second_block(x, norm_w, w_in, gdn_conv_w, gdn_a_log, gdn_dt_bias, gdn_norm_w,
              rwkv_mu, rwkv_w0, rwkv_w_up, rwkv_a0, rwkv_a_up, rwkv_k_k, rwkv_k_a, rwkv_r_k,
              rwkv_lnx_w, rwkv_lnx_b,
              s5_a_re, s5_a_im, s5_log_dt, s5_b_re, s5_b_im, s5_c_re, s5_c_im, s5_d,
              s5_glu_w, s5_glu_b,
              gate_b, w_branch, w_out, final_norm_w):
    bsz, seq, _ = x.shape
    for i in range(DEPTH_2):
        h = rms_norm(x, norm_w[i])
        proj = h @ w_in[i]
        (g_qkv, g_z, g_b, g_a, r_feat, r_z, s_u, s_z, gate_logits) = _split_cols(proj, SPLIT_SIZES)
        o_a = gdn_branch(g_qkv, g_z, g_b, g_a, gdn_conv_w[i], gdn_a_log[i], gdn_dt_bias[i], gdn_norm_w[i])
        o_b = rwkv7_branch(r_feat, r_z, rwkv_mu[i], rwkv_w0[i], rwkv_w_up[i], rwkv_a0[i], rwkv_a_up[i],
                           rwkv_k_k[i], rwkv_k_a[i], rwkv_r_k[i], rwkv_lnx_w[i], rwkv_lnx_b[i])
        o_c = s5_branch(s_u, s_z, s5_a_re[i], s5_a_im[i], s5_log_dt[i], s5_b_re[i], s5_b_im[i],
                        s5_c_re[i], s5_c_im[i], s5_d[i], s5_glu_w[i], s5_glu_b[i])
        branches = jnp.stack([o_a, o_b, o_c], axis=2)
        branch_proj = jnp.einsum('blnc,ncd->blnd', branches, w_branch[i].astype(jnp.float32))
        gates = jax.nn.sigmoid(gate_logits.astype(jnp.float32).reshape(bsz, seq, N_BRANCH, D_MODEL)
                               + gate_b[i].astype(jnp.float32))
        merged = jnp.sum(gates * branch_proj, axis=2)
        x = x + (merged @ w_out[i].astype(jnp.float32)).astype(x.dtype)
    return rms_norm(x, final_norm_w)


_first_inputs = second_inputs


def second_inputs(seed=0):
    import zlib

    import numpy as np

    out = dict(_first_inputs(seed))
    spreads = {}
    factors = {'norm_w': 3.342,
     'gdn_norm_w': 53.831,
     'rwkv_w_up': 8.0,
     'rwkv_a0': 4.667,
     'rwkv_k_k': 35.556,
     'rwkv_k_a': 3.541,
     'rwkv_lnx_w': 58.75,
     'rwkv_lnx_b': 59.231,
     's5_a_re': 64.0,
     's5_a_im': 64.0,
     's5_log_dt': 64.0,
     's5_b_re': 64.0,
     's5_b_im': 64.0,
     's5_c_re': 64.0,
     's5_c_im': 64.0,
     's5_glu_b': 64.0,
     'gate_b': 8.0,
     'final_norm_w': 7.639}
    for name, (base, spread) in spreads.items():
        noise = np.random.default_rng([zlib.crc32(name.encode()), seed]).standard_normal(out[name].shape)
        drawn = base * np.exp(spread * noise) if base else spread * noise
        out[name] = __import__('jax').numpy.asarray(drawn.astype(out[name].dtype))
    for name, factor in factors.items():
        out[name] = (out[name] * factor).astype(out[name].dtype)
    return out


_narrow_inputs = second_inputs


def second_inputs(seed=0):
    out = dict(_narrow_inputs(seed))
    wider = {'gdn_norm_w': 4.51,
     'rwkv_k_k': 4.43,
     'rwkv_lnx_w': 4.48,
     'rwkv_lnx_b': 4.46,
     's5_d': 4.14,
     's5_glu_w': 7.09,
     's5_glu_b': 12.0,
     'final_norm_w': 3.11}
    for name, times in wider.items():
        mean = out[name].mean()
        out[name] = (mean + times * (out[name] - mean)).astype(out[name].dtype)
    return out


def setup_inputs(seed=0):
    out = dict(first_inputs(seed))
    for name, value in second_inputs(seed + 1).items():
        if name != "x":
            out[name + "_2"] = value
    return out


def reference(
    x, norm0, w_in0, w_out0, norm1, w_in1, b_f1, w_out1, norm_f, norm_w_2, w_in_2, gdn_conv_w_2,
    gdn_a_log_2, gdn_dt_bias_2, gdn_norm_w_2, rwkv_mu_2, rwkv_w0_2, rwkv_w_up_2, rwkv_a0_2,
    rwkv_a_up_2, rwkv_k_k_2, rwkv_k_a_2, rwkv_r_k_2, rwkv_lnx_w_2, rwkv_lnx_b_2, s5_a_re_2,
    s5_a_im_2, s5_log_dt_2, s5_b_re_2, s5_b_im_2, s5_c_re_2, s5_c_im_2, s5_d_2, s5_glu_w_2,
    s5_glu_b_2, gate_b_2, w_branch_2, w_out_2, final_norm_w_2,
):
    x = first_block(
        x, norm0, w_in0, w_out0, norm1, w_in1, b_f1, w_out1, norm_f,
    )
    return second_block(
        x, norm_w_2, w_in_2, gdn_conv_w_2, gdn_a_log_2, gdn_dt_bias_2, gdn_norm_w_2, rwkv_mu_2,
        rwkv_w0_2, rwkv_w_up_2, rwkv_a0_2, rwkv_a_up_2, rwkv_k_k_2, rwkv_k_a_2, rwkv_r_k_2,
        rwkv_lnx_w_2, rwkv_lnx_b_2, s5_a_re_2, s5_a_im_2, s5_log_dt_2, s5_b_re_2, s5_b_im_2,
        s5_c_re_2, s5_c_im_2, s5_d_2, s5_glu_w_2, s5_glu_b_2, gate_b_2, w_branch_2, w_out_2,
        final_norm_w_2,
    )


_drawn_inputs = setup_inputs


def setup_inputs(seed=0):
    import zlib

    import numpy as np

    out = dict(_drawn_inputs(seed))
    spreads = {}
    factors = {}
    for name, (base, spread) in spreads.items():
        noise = np.random.default_rng([zlib.crc32(name.encode()), seed]).standard_normal(out[name].shape)
        drawn = base * np.exp(spread * noise) if base else spread * noise
        out[name] = __import__('jax').numpy.asarray(drawn.astype(out[name].dtype))
    for name, factor in factors.items():
        out[name] = (out[name] * factor).astype(out[name].dtype)
    return out
```

```python
from contextlib import ExitStack

import numpy as np

import concourse.bass as bass
from concourse import mybir

F32 = mybir.dt.float32
F32R = mybir.dt.float32r
ALU = mybir.AluOpType
ACT = mybir.ActivationFunctionType
AX_X = mybir.AxisListType.X
P = 128
SEQ = 256
MT = SEQ // P
D = 2048
EPS = 1e-6
NEG = -1.0e30


class Phase:

    def __init__(self, nc, name):
        self.nc, self.name = nc, name

    def __enter__(self):
        self.stack = ExitStack()
        self.sems = []
        return self

    def sb(self, name, shape, dt=F32):
        return self.stack.enter_context(self.nc.sbuf_tensor(f"{self.name}_{name}", shape, dt))

    def ps(self, name, shape):
        bank = self.stack.enter_context(self.nc.psum_tensor(f"{self.name}_{name}", [P, 512], F32))
        n = int(np.prod(shape[1:]))
        v = bank[0:shape[0], 0:n]
        return v if len(shape) == 2 else v.rearrange("p (a b) -> p a b", a=shape[1])

    def sem(self, name):
        s = self.nc.alloc_semaphore(f"{self.name}_{name}")
        self.sems.append(s)
        return s

    def __exit__(self, *e):
        if e[0] is None:
            self.nc.clear_and_free_semaphores(self.sems)
            self.nc.all_engine_barrier()
        self.stack.close()
        return False


class Chain:

    def __init__(self, eng, sem):
        self.eng, self.sem, self.last = eng, sem, 0

    def step(self, ins):
        self.last += 1
        ins.then_inc(self.sem, 1)
        return self.last

    def settle(self):
        if self.last:
            self.eng.wait_ge(self.sem, self.last)


def bcast_rows(ap, n=P):
    return ap.rearrange("(a w) -> a w", a=1).broadcast_to([n, ap.shape[0]])


def gemm(nc, ph, W, out, residual=None):
    K, N = W.shape
    KT = K // P
    TN, Q = 512, 4
    KQ = KT // Q
    tiles = -(-N // TN)
    pairs = (N // TN - 1) // 2 if tiles > 4 else 0
    wid = lambda t: min(TN, N - t * TN)
    Wv = W.rearrange("(k p) n -> p k n", p=P)
    outv = out.rearrange("(m p) n -> p m n", p=P)
    raw = ph.sb("raw", [P, 2 * Q, KQ, TN])
    hi = ph.sb("hi", [P, Q, KQ, TN], F32R)
    lo = ph.sb("lo", [P, Q, KQ, TN], F32R)
    aT_hi = ph.sb("aT_hi", [P, KT, SEQ], F32R)
    aT_lo = ph.sb("aT_lo", [P, KT, SEQ], F32R)
    stage = ph.sb("stage", [P, 2, MT, TN])
    acc = [[ph.ps(f"acc{s}{m}", [P, TN]) for m in range(MT)] for s in range(2)]
    raw_full = [ph.sem(f"raw_full{r}") for r in range(2 * Q)]
    hi_done = [ph.sem(f"hi_done{q}") for q in range(Q)]
    lo_done = [ph.sem(f"lo_done{q}") for q in range(Q)]
    used = [ph.sem(f"used{q}") for q in range(Q)]
    act_staged = [ph.sem(f"act_staged{s}") for s in range(2)]
    dve_staged = [ph.sem(f"dve_staged{s}") for s in range(2)]
    stored = [ph.sem(f"stored{s}") for s in range(2)]

    def walk(eng, one):
        tile = lambda t: (t % 2, t // 2, t * TN, wid(t))
        one(tile(0), None)
        if pairs > 0:
            with eng.Fori(0, pairs) as i:
                one((1, i, i * (2 * TN) + TN, TN), (0, i, i * (2 * TN), TN))
                one((0, i + 1, i * (2 * TN) + 2 * TN, TN), (1, i, i * (2 * TN) + TN, TN))
        for t in range(1 + 2 * max(pairs, 0), tiles):
            one(tile(t), tile(t - 1))
        one(None, tile(tiles - 1))

    def load(sp):
        def one(cur, prev):
            if cur is None:
                return
            s, n, c0, w = cur
            for q in range(Q):
                sp.wait_ge(lo_done[q], n * 2 + (s + 1))
                sp.dma_start(raw[:, s * Q + q, :, 0:w], Wv[:, q * KQ:(q + 1) * KQ, bass.ds(c0, w)]).then_inc(raw_full[s * Q + q], 16)
        walk(sp, one)

    def products(pe):
        def one(cur, prev):
            if cur is None:
                return
            s, n, c0, w = cur
            pe.wait_ge(dve_staged[s], n + 1)
            if residual is None:
                pe.wait_ge(act_staged[s], n + 1)
            for q in range(Q):
                pe.wait_ge(lo_done[q], n * 2 + (s + 3))
                for k in range(q * KQ, (q + 1) * KQ):
                    for m in range(MT):
                        for a, b, first, end in ((aT_hi, hi, True, False), (aT_hi, lo, False, False), (aT_lo, hi, False, True)):
                            last = nc.tensor.matmul(acc[s][m][:, 0:w], a[:, k, m * P:(m + 1) * P], b[:, q, k - q * KQ, 0:w],
                                                    start=(k == 0 and first), stop=(k == KT - 1 and end))
                last.then_inc(used[q], 1)
        for q in range(Q):
            pe.sem_inc(used[q], 1)
        walk(pe, one)

    def scalar(act):
        def one(cur, prev):
            if cur is not None:
                s, n, c0, w = cur
                for q in range(Q):
                    act.wait_ge(raw_full[s * Q + q], (n + 1) * 16)
                    act.wait_ge(used[q], n * 2 + (s + 1))
                    nc.scalar.copy(hi[:, q, :, 0:w], raw[:, s * Q + q, :, 0:w]).then_inc(hi_done[q], 1)
            if prev is not None:
                s, n, c0, w = prev
                if residual is None:
                    act.wait_ge(used[Q - 1], n * 2 + (s + 2))
                    act.wait_ge(stored[s], (n + 1) * 16)
                    nc.scalar.copy(stage[:, s, 0, 0:w], acc[s][0][:, 0:w]).then_inc(act_staged[s], 1)
                    act.wait_ge(act_staged[s], n + 2)
                act.wait_ge(dve_staged[s], n + 2)
                act.dma_start(outv[:, :, bass.ds(c0, w)], stage[:, s, :, 0:w]).then_inc(stored[s], 16)
        for s in range(2):
            act.sem_inc(stored[s], 16)
            act.sem_inc(act_staged[s], 1)
        walk(act, one)
        for s in range(2):
            act.wait_ge(stored[s], 16 * (1 + (tiles + 1 - s) // 2))

    def vector(dve):
        def one(cur, prev):
            if cur is not None:
                s, n, c0, w = cur
                for q in range(Q):
                    dve.wait_ge(hi_done[q], n * 2 + (s + 1))
                    nc.vector.tensor_tensor(lo[:, q, :, 0:w], raw[:, s * Q + q, :, 0:w],
                                            hi[:, q, :, 0:w].bitcast(F32), ALU.subtract).then_inc(lo_done[q], 1)
            if prev is not None:
                s, n, c0, w = prev
                dve.wait_ge(used[Q - 1], n * 2 + (s + 2))
                dve.wait_ge(stored[s], (n + 1) * 16)
                if residual is None:
                    nc.vector.tensor_copy(stage[:, s, 1, 0:w], acc[s][1][:, 0:w]).then_inc(dve_staged[s], 1)
                else:
                    rows, sem, value = residual
                    dve.wait_ge(sem, value)
                    for m in range(MT):
                        last = nc.vector.tensor_tensor(stage[:, s, m, 0:w], acc[s][m][:, 0:w], rows[:, m, c0:c0 + w], ALU.add)
                    last.then_inc(dve_staged[s], 1)
        walk(dve, one)

    def start(dve):
        for q in range(Q):
            dve.sem_inc(lo_done[q], 2)
        for s in range(2):
            dve.sem_inc(dve_staged[s], 1)

    return dict(load=load, products=products, scalar=scalar, vector=vector, start=start, aT=(aT_hi, aT_lo), stage=stage)


class Steps:

    def __init__(self, eng, sem):
        self.eng, self.own, self.count = eng, sem, {}

    def link(self, ins):
        self.tell(ins, self.own)

    def tell(self, ins, sem, wait=True):
        n = self.count.get(id(sem), 0) + 1
        self.count[id(sem)] = n
        ins.then_inc(sem, 1)
        if wait:
            self.eng.wait_ge(sem, n)


class Turner:

    def __init__(self, nc, ph, ident, name="turn"):
        self.nc, self.ident = nc, ident
        self.bank = [ph.ps(f"{name}{b}", [P, 4, P]) for b in range(2)]
        self.turned = ph.sem(f"{name}_turned")
        self.copied = ph.sem(f"{name}_copied")
        self.hi_copied = ph.sem(f"{name}_hi_copied")
        self.n_pe = self.n_copy = 0

    def turn(self, pe, jobs):
        for srcs, dst, ready in jobs:
            if ready:
                pe.wait_ge(*ready)
            if self.n_pe >= 2:
                pe.wait_ge(self.copied, self.n_pe - 1)
            for j, s in enumerate(srcs):
                rows, cols = s.shape[0], s.free_size()
                last = self.nc.tensor.transpose(self.bank[self.n_pe % 2][0:cols, j, 0:rows], s,
                                                self.ident[0:rows, 0:rows])
            last.then_inc(self.turned, 1)
            self.n_pe += 1

    def copy(self, eng, jobs):
        for srcs, dst, ready in jobs:
            eng.wait_ge(self.turned, self.n_copy + 1)
            rows, cols = srcs[0].shape[0], srcs[0].free_size()
            src = self.bank[self.n_copy % 2][0:cols, 0:len(srcs), 0:rows]
            if eng is self.nc.scalar:
                self.nc.scalar.copy(dst, src).then_inc(self.copied, 1)
            else:
                self.nc.vector.tensor_copy(dst, src).then_inc(self.copied, 1)
            self.n_copy += 1

    def copy_hi(self, act, jobs):
        for j, (srcs, (hi, lo), ready) in enumerate(jobs):
            act.wait_ge(self.turned, j + 1)
            self.nc.scalar.copy(hi, self.bank[j % 2]).then_inc(self.hi_copied, 1)

    def copy_lo(self, dve, jobs):
        for j, (srcs, (hi, lo), ready) in enumerate(jobs):
            dve.wait_ge(self.hi_copied, j + 1)
            self.nc.vector.tensor_tensor(lo, self.bank[j % 2], hi.bitcast(F32), ALU.subtract).then_inc(self.copied, 1)

    def all_copied(self, eng, n):
        eng.wait_ge(self.copied, n)


class SoftmaxHeads:

    def __init__(self, nc, ph, ident, units):
        self.nc, self.ident, self.units = nc, ident, units
        self.lg_ps = [ph.ps(f"lg_ps{b}", [P, SEQ]) for b in range(2)]
        self.pT_ps = [ph.ps(f"pT_ps{b}", [P, MT, P]) for b in range(2)]
        self.o_ps = [ph.ps(f"o_ps{b}", [P, P]) for b in range(2)]
        self.lg = ph.sb("lg", [P, 2, SEQ])
        self.p = ph.sb("p", [P, 3, SEQ])
        self.pT = ph.sb("pT", [P, 2, MT, P])
        self.nmx = ph.sb("nmx", [P, 4])
        self.sm = ph.sb("sm", [P, 4])
        self.rs = ph.sb("rs", [P, 4])
        (self.lg_full, self.lg_masked, self.lg_max, self.p_exp, self.p_counted, self.pT_full, self.pT_copied,
         self.o_full, self.o_recip, self.o_done) = (ph.sem(s) for s in (
             "lg_full", "lg_masked", "lg_max", "p_exp", "p_counted", "pT_full", "pT_copied", "o_full",
             "o_recip", "o_done"))
        self.counted = [sum(1 for x in units[:i + 1] if x.get("count") is not None) for i in range(len(units))]

    def p_ready(self, eng, u):
        if self.units[u].get("count") is not None:
            eng.wait_ge(self.p_counted, self.counted[u])
        else:
            eng.wait_ge(self.p_exp, u + 1)

    def tensor(self, pe):
        nc, U = self.nc, self.units
        for u in range(len(U) + 3):
            if u < len(U):
                x = U[u]
                if x.get("ready"):
                    pe.wait_ge(*x["ready"])
                if u >= 2:
                    pe.wait_ge(self.lg_masked, u - 1)
                more = x.get("extra")
                last = nc.tensor.matmul(self.lg_ps[u % 2][:, 0:x["ns"]], x["q"], x["k"], start=True, stop=not more)
                if more:
                    last = nc.tensor.matmul(self.lg_ps[u % 2][:, 0:x["ns"]], more[0], more[1], start=False, stop=True)
                last.then_inc(self.lg_full, 1)
            v = u - 2
            if 0 <= v < len(U):
                self.p_ready(pe, v)
                if v >= 2:
                    pe.wait_ge(self.pT_copied, v - 1)
                for j in range(U[v]["ns"] // P):
                    last = nc.tensor.transpose(self.pT_ps[v % 2][:, j, :], self.p[:, v % 3, j * P:(j + 1) * P],
                                               self.ident[:, :])
                last.then_inc(self.pT_full, 1)
            w = u - 3
            if 0 <= w < len(U):
                pe.wait_ge(self.pT_copied, w + 1)
                if w >= 2:
                    pe.wait_ge(self.o_done, w - 1)
                n = U[w]["ns"] // P
                for j in range(n):
                    last = nc.tensor.matmul(self.o_ps[w % 2][:, :], self.pT[:, w % 2, j, :], U[w]["v"][j],
                                            start=(j == 0), stop=(j == n - 1))
                last.then_inc(self.o_full, 1)

    def scalar(self, act):
        nc, U = self.nc, self.units
        for u in range(len(U) + 2):
            if u < len(U):
                ns = U[u]["ns"]
                act.wait_ge(self.lg_max, u + 1)
                if u >= 3:
                    act.wait_ge(self.pT_full, u - 2)
                if u >= 4:
                    act.wait_ge(self.o_recip, u - 3)
                nc.scalar.activation(self.p[:, u % 3, 0:ns], self.lg[:, u % 2, 0:ns], ACT.Exp,
                                     bias=self.nmx[:, u % 4:u % 4 + 1],
                                     accum_out=self.sm[:, u % 4:u % 4 + 1]).then_inc(self.p_exp, 1)
            v = u - 2
            if 0 <= v < len(U):
                n = U[v]["ns"] // P
                act.wait_ge(self.pT_full, v + 1)
                if v >= 2:
                    act.wait_ge(self.o_full, v - 1)
                nc.scalar.copy(self.pT[:, v % 2, 0:n, :], self.pT_ps[v % 2][:, 0:n, :]).then_inc(self.pT_copied, 1)

    def vector(self, dve):
        nc, U = self.nc, self.units
        for u in range(len(U) + 3):
            if u < len(U):
                x = U[u]
                ns = x["ns"]
                dve.wait_ge(self.lg_full, u + 1)
                if u >= 2:
                    dve.wait_ge(self.p_exp, u - 1)
                nc.vector.scalar_tensor_tensor(self.lg[:, u % 2, 0:ns], self.lg_ps[u % 2][:, 0:ns], x["scale"],
                                               x["mask"], x.get("op", ALU.mult), ALU.add).then_inc(self.lg_masked, 1)
                dve.wait_ge(self.lg_masked, u + 1)
                nc.vector.tensor_reduce(self.nmx[:, u % 4:u % 4 + 1], self.lg[:, u % 2, 0:ns], AX_X, ALU.max,
                                        negate=True).then_inc(self.lg_max, 1)
            v = u - 1
            if 0 <= v < len(U) and U[v].get("count") is not None:
                ns = U[v]["ns"]
                dve.wait_ge(self.p_exp, v + 1)
                p = self.p[:, v % 3, 0:ns]
                nc.vector.tensor_tensor_reduce(p, p, U[v]["count"], 1.0, 0.0, ALU.mult, ALU.add,
                                               self.sm[:, v % 4:v % 4 + 1]).then_inc(self.p_counted, 1)
            w = u - 3
            if 0 <= w < len(U):
                self.p_ready(dve, w)
                nc.vector.reciprocal(self.rs[:, w % 4:w % 4 + 1], self.sm[:, w % 4:w % 4 + 1]).then_inc(self.o_recip, 1)
                dve.wait_ge(self.o_recip, w + 1)
                dve.wait_ge(self.o_full, w + 1)
                nc.vector.tensor_scalar(U[w]["out"], self.o_ps[w % 2][:, :], self.rs[:, w % 4:w % 4 + 1], None,
                                        ALU.mult).then_inc(self.o_done, 1)


def turn_operand(aT, rows, ready):
    return [([rows[:, m, (4 * g + j) * P:(4 * g + j + 1) * P] for j in range(4)],
             tuple(t[:, 4 * g:4 * g + 4, m * P:(m + 1) * P] for t in aT), (ready, m + 1))
            for m in range(MT) for g in range(aT[0].shape[1] // 4)]


def norm_project(nc, name, C, x, g, W, out):
    with Phase(nc, name) as ph:
        xt = ph.sb("xt", [P, MT, D])
        gt = ph.sb("gt", [P, D])
        ss = ph.sb("ss", [P, MT])
        rs = ph.sb("rs", [P, MT])
        ident = ph.sb("ident", [P, P])
        x_in, squares, root, mean, scaled, recip = (ph.sem(s) for s in (
            "x_in", "squares", "root", "mean", "scaled", "recip"))
        turner = Turner(nc, ph, ident)
        mm = gemm(nc, ph, W, out)
        jobs = turn_operand(mm["aT"], xt, scaled)
        sq = mm["stage"][:, :, :, :].rearrange("p a b c -> p (a b c)")

        with nc.Block() as block:
            @block.sync
            def _(sp):
                sp.dma_start(xt[:, :, :], x.rearrange("(m p) d -> p m d", p=P)).then_inc(x_in, 16)
                sp.dma_start(gt[:, :], bcast_rows(g)).then_inc(x_in, 16)
                sp.dma_start(ident[:, :], C["ident"]).then_inc(x_in, 16)
                mm["load"](sp)

            @block.tensor
            def _(pe):
                pe.wait_ge(x_in, 48)
                turner.turn(pe, jobs)
                turner.all_copied(pe, len(jobs))
                mm["products"](pe)

            @block.scalar
            def _(act):
                act.wait_ge(x_in, 48)
                for m in range(MT):
                    if m:
                        act.wait_ge(squares, m)
                    nc.scalar.activation(sq, xt[:, m, :], ACT.Square, accum_out=ss[:, m:m + 1]).then_inc(squares, 1)
                act.wait_ge(squares, MT)
                act.wait_ge(mean, 1)
                nc.scalar.activation(ss[:, :], rs[:, :], ACT.Sqrt).then_inc(root, 1)
                turner.copy_hi(act, jobs)
                mm["scalar"](act)

            @block.vector
            def _(dve):
                mm["start"](dve)
                dve.wait_ge(squares, MT)
                nc.vector.tensor_scalar(rs[:, :], ss[:, :], 1.0 / D, EPS, ALU.mult, ALU.add).then_inc(mean, 1)
                dve.wait_ge(root, 1)
                nc.vector.reciprocal(rs[:, :], ss[:, :]).then_inc(recip, 1)
                dve.wait_ge(recip, 1)
                for m in range(MT):
                    nc.vector.scalar_tensor_tensor(xt[:, m, :], xt[:, m, :], rs[:, m:m + 1], gt[:, :],
                                                   ALU.mult, ALU.mult).then_inc(scaled, 1)
                turner.copy_lo(dve, jobs)
                mm["vector"](dve)


def gated_project(nc, name, C, a, gate, W, x, out):
    K, N = W.shape
    with Phase(nc, name) as ph:
        at = ph.sb("at", [P, MT, K])
        gt = ph.sb("gt", [P, MT, D])
        ident = ph.sb("ident", [P, P])
        x_in, silu, gated, res_in = (ph.sem(s) for s in ("x_in", "silu", "gated", "res_in"))
        turner = Turner(nc, ph, ident)
        loads = 3 if gate is not None else 2
        mm = gemm(nc, ph, W, out, residual=(gt, res_in, 16))
        jobs = turn_operand(mm["aT"], at, gated)

        with nc.Block() as block:
            @block.sync
            def _(sp):
                sp.dma_start(at[:, :, :], a.rearrange("(m p) d -> p m d", p=P)).then_inc(x_in, 16)
                if gate is not None:
                    sp.dma_start(gt[:, :, :], gate.rearrange("(m p) d -> p m d", p=P)).then_inc(x_in, 16)
                sp.dma_start(ident[:, :], C["ident"]).then_inc(x_in, 16)
                mm["load"](sp)

            @block.gpsimd
            def _(pool):
                pool.wait_ge(gated, MT)
                pool.dma_start(gt[:, :, :], x.rearrange("(m p) d -> p m d", p=P)).then_inc(res_in, 16)

            @block.tensor
            def _(pe):
                pe.wait_ge(x_in, 16 * loads)
                turner.turn(pe, jobs)
                turner.all_copied(pe, len(jobs))
                mm["products"](pe)

            @block.scalar
            def _(act):
                if gate is not None:
                    act.wait_ge(x_in, 16 * loads)
                    for m in range(MT):
                        nc.scalar.activation(gt[:, m, :], gt[:, m, :], ACT.Silu).then_inc(silu, 1)
                turner.copy_hi(act, jobs)
                mm["scalar"](act)

            @block.vector
            def _(dve):
                mm["start"](dve)
                dve.wait_ge(x_in, 16 * loads)
                for m in range(MT):
                    if gate is None:
                        dve.sem_inc(gated, 1)
                    else:
                        dve.wait_ge(silu, m + 1)
                        nc.vector.tensor_tensor(at[:, m, :], at[:, m, :], gt[:, m, :], ALU.mult).then_inc(gated, 1)
                turner.copy_lo(dve, jobs)
                mm["vector"](dve)


HD = 128
N_A, N_B, N_I, DI = 10, 6, 16, 64
TOPK = min(256, SEQ // 4)
EVEN_MIX = (N_A + 2) * HD + N_I * DI + DI + N_I + 3 * N_B * HD
C_KA = N_A * HD
C_VA = C_KA + HD
C_IQ = C_VA + HD
C_IK = C_IQ + N_I * DI
C_IW = C_IK + DI
C_QB = C_IW + N_I
C_KB = C_QB + N_B * HD
C_VB = C_KB + N_B * HD
TAKEN = -3.0e38


def even_mix(nc, name, C, proj, y):
    SC = float(HD) ** -0.5
    with Phase(nc, name) as ph:
        pr = ph.sb("pr", [P, MT, EVEN_MIX])
        cos = ph.sb("cos", [P, MT, HD // 2])
        sin = ph.sb("sin", [P, MT, HD // 2])
        cosi = ph.sb("cosi", [P, MT, DI // 2])
        sini = ph.sb("sini", [P, MT, DI // 2])
        causal = ph.sb("causal", [P, MT, SEQ])
        band = ph.sb("band", [P, MT, SEQ])
        count = ph.sb("count", [P, MT, SEQ])
        ident = ph.sb("ident", [P, P])
        W = 2 * N_B * HD
        t1 = ph.sb("t1", [P, W // 2])
        t2 = ph.sb("t2", [P, W // 2])
        t3 = ph.sb("t3", [P, W // 2])
        t4 = ph.sb("t4", [P, W // 2])
        ikk = ph.sb("ikk", [P, MT, 2 * DI])
        qkT = ph.sb("qkT", [P, N_A + 1 + 2 * N_B, SEQ])
        iT = ph.sb("iT", [P, N_I // 2 + 1, SEQ])
        relu = ph.sb("relu", [P, 4, SEQ])
        iw = ph.sb("iw", [P, MT, N_I])
        score = ph.sb("score", [P, MT, SEQ])
        top8 = ph.sb("top8", [P, 8])
        sel = ph.sb("sel", [P, MT, SEQ])
        yo = ph.sb("yo", [P, MT, D])
        x_in, const_in, roped, dots_full, dots_relu, added, chosen, own_v, stored = (ph.sem(s) for s in (
            "x_in", "const_in", "roped", "dots_full", "dots_relu", "added", "chosen", "own_v", "stored"))
        turner = Turner(nc, ph, ident)
        prv = proj.rearrange("(m p) n -> p m n", p=P)

        def heads(m, c0, n, w=HD):
            return [pr[:, m, c0 + i * w:c0 + (i + 1) * w] for i in range(n)]

        jobs = []
        for m in range(MT):
            cols = slice(m * P, (m + 1) * P)
            srcs = heads(m, 0, N_A + 1) + heads(m, C_QB, 2 * N_B)
            for g in range(0, len(srcs), 4):
                part = srcs[g:g + 4]
                jobs.append((part, qkT[:, g:g + len(part), cols], (roped, m + 1)))
            srcs = heads(m, C_IQ, N_I // 2) + [ikk[:, m, :]]
            for g in range(0, len(srcs), 4):
                part = srcs[g:g + 4]
                jobs.append((part, iT[:, g:g + len(part), cols], (roped, m + 1)))

        units = []
        for m in range(MT):
            ns = (m + 1) * P
            cols = slice(m * P, (m + 1) * P)
            for h in range(N_B):
                units.append(dict(q=qkT[:, N_A + 1 + h, cols], k=qkT[:, N_A + 1 + N_B + h, 0:ns], ns=ns, scale=SC,
                                  mask=band[:, m, 0:ns], count=count[:, m, 0:ns],
                                  v=[pr[:, j, C_VB + h * HD:C_VB + (h + 1) * HD] for j in range(m + 1)],
                                  out=yo[:, m, (N_A + h) * HD:(N_A + h + 1) * HD]))
        for m in range(MT):
            ns = (m + 1) * P
            cols = slice(m * P, (m + 1) * P)
            for h in range(N_A):
                units.append(dict(q=qkT[:, h, cols], k=qkT[:, N_A, 0:ns], ns=ns, scale=SC,
                                  mask=sel[:, m, 0:ns],
                                  v=[pr[:, j, C_VA:C_VA + HD] for j in range(m + 1)],
                                  out=yo[:, m, h * HD:(h + 1) * HD]))
        soft = SoftmaxHeads(nc, ph, ident, units)
        dots = [(m, h) for m in range(MT) for h in range(N_I)]

        with nc.Block() as block:
            @block.sync
            def _(sp):
                for m in range(MT):
                    sp.dma_start(pr[:, m, :], prv[:, m, 0:EVEN_MIX]).then_inc(x_in, 16)
                for t, c in ((cos, "cos"), (sin, "sin"), (cosi, "cosi"), (sini, "sini"), (causal, "causal"),
                             (band, "band"), (count, "count")):
                    sp.dma_start(t[:, :, :], C[c].rearrange("(m p) n -> p m n", p=P)).then_inc(const_in, 16)
                sp.dma_start(ident[:, :], C["ident"]).then_inc(const_in, 16)
                sp.wait_ge(soft.o_done, len(units))
                sp.dma_start(y.rearrange("(m p) n -> p m n", p=P), yo[:, :, :]).then_inc(stored, 16)
                sp.wait_ge(stored, 16)

            @block.tensor
            def _(pe):
                pe.wait_ge(const_in, 128)
                turner.turn(pe, jobs)
                turner.all_copied(pe, len(jobs))
                for n, (m, h) in enumerate(dots):
                    ns = (m + 1) * P
                    r = slice((h % 2) * DI, (h % 2 + 1) * DI)
                    if n >= 2:
                        pe.wait_ge(dots_relu, n - 1)
                    nc.tensor.matmul(soft.lg_ps[n % 2][:, 0:ns], iT[r, h // 2, m * P:(m + 1) * P],
                                     iT[r, N_I // 2, 0:ns], start=True, stop=True).then_inc(dots_full, 1)
                pe.wait_ge(dots_relu, len(dots))
                pe.wait_ge(chosen, 1)
                soft.tensor(pe)

            @block.scalar
            def _(act):
                turner.copy(act, jobs)
                for n, (m, h) in enumerate(dots):
                    ns = (m + 1) * P
                    act.wait_ge(dots_full, n + 1)
                    if n >= 4:
                        act.wait_ge(added, n - 3)
                    nc.scalar.activation(relu[:, n % 4, 0:ns], soft.lg_ps[n % 2][:, 0:ns], ACT.Relu,
                                         scale=float(DI) ** -0.5).then_inc(dots_relu, 1)
                soft.scalar(act)

            @block.vector
            def _(dve):
                st = Steps(dve, own_v)
                V = nc.vector
                dve.wait_ge(x_in, 16 * MT)
                dve.wait_ge(const_in, 128)
                for m in range(MT):
                    for c0, n, w, co, si in ((0, N_A + 1, HD, cos, sin), (C_QB, 2 * N_B, HD, cos, sin),
                                             (C_IQ, N_I + 1, DI, cosi, sini)):
                        hw = w // 2
                        x = pr[:, m, c0:c0 + n * w].rearrange("p (h d) -> p h d", h=n)
                        a, b = x[:, :, 0:hw], x[:, :, hw:w]
                        cb = co[:, m, :].unsqueeze(1).broadcast_to([P, n, hw])
                        sb_ = si[:, m, :].unsqueeze(1).broadcast_to([P, n, hw])
                        tv = [t[:, 0:n * hw].rearrange("p (h d) -> p h d", h=n) for t in (t1, t2, t3, t4)]
                        V.tensor_tensor(tv[0], a, cb, ALU.mult)
                        V.tensor_tensor(tv[1], b, sb_, ALU.mult)
                        V.tensor_tensor(tv[2], b, cb, ALU.mult)
                        st.link(V.tensor_tensor(tv[3], a, sb_, ALU.mult))
                        V.tensor_tensor(a, tv[0], tv[1], ALU.subtract)
                        st.link(V.tensor_tensor(b, tv[2], tv[3], ALU.add))
                    V.tensor_scalar(iw[:, m, :], pr[:, m, C_IW:C_IW + N_I], float(N_I) ** -0.5, None, ALU.mult)
                    st.tell(V.tensor_copy(ikk[:, m, :].rearrange("p (a d) -> p a d", a=2),
                                          pr[:, m, C_IK:C_IK + DI].unsqueeze(1).broadcast_to([P, 2, DI])), roped)
                for n, (m, h) in enumerate(dots):
                    ns = (m + 1) * P
                    dve.wait_ge(dots_relu, n + 1)
                    if h == 0:
                        i = V.tensor_scalar(score[:, m, 0:ns], relu[:, n % 4, 0:ns], iw[:, m, 0:1], None, ALU.mult)
                    else:
                        i = V.scalar_tensor_tensor(score[:, m, 0:ns], relu[:, n % 4, 0:ns], iw[:, m, h:h + 1],
                                                   score[:, m, 0:ns], ALU.mult, ALU.add)
                    st.tell(i, added)
                for m in range(MT):
                    ns = (m + 1) * P
                    s = score[:, m, 0:ns]
                    st.link(V.tensor_tensor(s, s, causal[:, m, 0:ns], ALU.add))
                    for _ in range(TOPK // 8):
                        st.link(V.max(top8[:, :], s))
                        st.link(V.match_replace(s, top8[:, :], s, TAKEN))
                    st.link(V.tensor_scalar(s, s, TAKEN / 2, None, ALU.is_lt))
                    st.link(V.tensor_scalar(s, s, -NEG, NEG, ALU.mult, ALU.add))
                    st.link(V.tensor_tensor(sel[:, m, 0:ns], s, causal[:, m, 0:ns], ALU.add))
                dve.sem_inc(chosen, 1)
                soft.vector(dve)


N_C, N_D = 8, 8
C_QC, C_KC, C_VC = 0, N_C * HD, 2 * N_C * HD
C_QD, C_KD, C_VD = 3 * N_C * HD, 3 * N_C * HD + N_D * HD, 3 * N_C * HD + 2 * N_D * HD
C_FL = 3 * (N_C + N_D) * HD
ODD_MIX = C_FL + N_D


def odd_mix(nc, name, C, proj, b_f, y):
    SC = float(HD) ** -0.5
    ZW = SEQ + P
    NB = 2
    with Phase(nc, name) as ph:
        pr = ph.sb("pr", [P, MT, ODD_MIX])
        qkT = ph.sb("qkT", [P, 2 * N_C + 2 * N_D, SEQ])
        causal = ph.sb("causal", [P, MT, SEQ])
        before = ph.sb("before", [P, P])
        upto = ph.sb("upto", [P, P])
        after = ph.sb("after", [P, P])
        ones = ph.sb("ones", [P, P])
        pick = ph.sb("pick", [N_D, N_D, P])
        ident = ph.sb("ident", [P, P])
        bf = ph.sb("bf", [P, N_D])
        lf = ph.sb("lf", [P, MT, N_D])
        e1 = ph.sb("e1", [P, MT, N_D])
        cum = ph.sb("cum", [P, MT, N_D])
        ncT = ph.sb("ncT", [N_D, SEQ])
        z = ph.sb("z", [P, 2, ZW])
        az = ph.sb("az", [P, 2, ZW])
        ez = ph.sb("ez", [P, 2, ZW])
        ls = ph.sb("ls", [P, 2, ZW])
        w = ph.sb("w", [P, 2, ZW])
        yo = ph.sb("yo", [P, MT, D])
        (x_in, const_in, ready, pre, abs_, exp_, cum_full, cum_done, z_full, z_out, l_abs, l_exp, l_ln, l_done,
         r_full, w_arg, w_exp, w_done, oc_full, oc_done, own_v, stored, scaled, z_copied) = (ph.sem(s) for s in (
             "x_in", "const_in", "ready", "pre", "abs", "exp", "cum_full", "cum_done", "z_full", "z_out", "l_abs",
             "l_exp", "l_ln", "l_done", "r_full", "w_arg", "w_exp", "w_done", "oc_full", "oc_done", "own_v",
             "stored", "scaled", "z_copied"))
        turner = Turner(nc, ph, ident)
        srcs0 = [C_QC + i * HD for i in range(2 * N_C)] + [C_QD + i * HD for i in range(2 * N_D)]
        jobs = []
        for m in range(MT):
            for g in range(0, len(srcs0), 4):
                jobs.append(([pr[:, m, c:c + HD] for c in srcs0[g:g + 4]],
                             qkT[:, g:g + 4, m * P:(m + 1) * P], (scaled, m + 1)))
        units = []
        for m in range(MT):
            ns = (m + 1) * P
            for h in range(N_D):
                units.append(dict(q=qkT[:, 2 * N_C + h, m * P:(m + 1) * P], k=qkT[:, 2 * N_C + N_D + h, 0:ns],
                                  ns=ns, scale=cum[:, m, h:h + 1], op=ALU.add, mask=causal[:, m, 0:ns],
                                  extra=(pick[:, h, :], ncT[:, 0:ns]),
                                  v=[pr[:, j, C_VD + h * HD:C_VD + (h + 1) * HD] for j in range(m + 1)],
                                  out=yo[:, m, (N_C + h) * HD:(N_C + h + 1) * HD]))
        soft = SoftmaxHeads(nc, ph, ident, units)
        zb, rb, ob = soft.lg_ps, soft.pT_ps, soft.o_ps
        with nc.Block() as block:
            @block.sync
            def _(sp):
                for m in range(MT):
                    sp.dma_start(pr[:, m, :], proj.rearrange("(m p) n -> p m n", p=P)[:, m, 0:ODD_MIX]).then_inc(x_in, 16)
                sp.dma_start(bf[:, :], bcast_rows(b_f)).then_inc(const_in, 16)
                sp.dma_start(causal[:, :, :], C["causal"].rearrange("(m p) n -> p m n", p=P)).then_inc(const_in, 16)
                for t, c in ((before, "before"), (upto, "upto"), (after, "after"), (ones, "ones"), (ident, "ident")):
                    sp.dma_start(t[:, :], C[c]).then_inc(const_in, 16)
                sp.dma_start(pick[:, :, :], C["pick"].rearrange("a (b c) -> a b c", b=N_D)).then_inc(const_in, 16)
                sp.wait_ge(soft.o_done, len(units))
                sp.wait_ge(oc_done, MT * N_C)
                sp.dma_start(y.rearrange("(m p) n -> p m n", p=P), yo[:, :, :]).then_inc(stored, 16)
                sp.wait_ge(stored, 16)

            @block.tensor
            def _(pe):
                pe.wait_ge(const_in, 128)
                turner.turn(pe, jobs)
                turner.all_copied(pe, len(jobs))
                pe.wait_ge(ready, 1)
                nc.tensor.matmul(rb[0][:, 0, 0:N_D], upto[:, :], lf[:, 0, :], start=True, stop=True)
                nc.tensor.matmul(rb[0][:, 1, 0:N_D], ones[:, :], lf[:, 0, :], start=True, stop=False)
                nc.tensor.matmul(rb[0][:, 1, 0:N_D], upto[:, :], lf[:, 1, :], start=False, stop=True).then_inc(cum_full, 1)
                pe.wait_ge(cum_done, 1)
                for m in range(MT):
                    last = nc.tensor.transpose(ob[0].tensor[0:N_D, m * P:(m + 1) * P], cum[:, m, :], ident[:, :])
                last.then_inc(cum_full, 1)
                pe.wait_ge(cum_done, 2)
                for i in range(N_C + 2):
                    h = i
                    if h < N_C:
                        q, k = qkT[:, h, :], qkT[:, N_C + h, :]
                        b = zb[h % 2].tensor
                        if h >= 2:
                            pe.wait_ge(z_copied, h - 1)
                        nc.tensor.matmul(b[:, 0:SEQ], k[:, 0:P], q, start=True, stop=True)
                        nc.tensor.matmul(b[:, SEQ:ZW], k[:, P:SEQ], q[:, P:SEQ], start=True, stop=True).then_inc(z_full, 1)
                    h = i - 1
                    if 0 <= h < N_C:
                        pe.wait_ge(l_done, h + 1)
                        b = rb[h % 2].tensor
                        if h >= 2:
                            pe.wait_ge(w_arg, h - 1)
                        l = ls[:, h % 2, :]
                        nc.tensor.matmul(b[:, 0:P], after[:, :], l[:, 0:P], start=True, stop=True)
                        nc.tensor.matmul(b[:, P:SEQ], after[:, :], l[:, P:SEQ], start=True, stop=False)
                        nc.tensor.matmul(b[:, P:SEQ], ones[:, :], l[:, SEQ:ZW], start=False, stop=True)
                        nc.tensor.matmul(b[:, SEQ:ZW], after[:, :], l[:, SEQ:ZW], start=True, stop=True).then_inc(r_full, 1)
                    h = i - 2
                    if 0 <= h < N_C:
                        pe.wait_ge(w_done, h + 1)
                        b = ob[h % 2].tensor
                        if h >= 2:
                            pe.wait_ge(oc_done, MT * (h - 1))
                        ww = w[:, h % 2, :]
                        v = [pr[:, j, C_VC + h * HD:C_VC + (h + 1) * HD] for j in range(MT)]
                        nc.tensor.matmul(b[:, 0:HD], ww[:, 0:P], v[0], start=True, stop=True)
                        nc.tensor.matmul(b[:, HD:2 * HD], ww[:, P:SEQ], v[0], start=True, stop=False)
                        nc.tensor.matmul(b[:, HD:2 * HD], ww[:, SEQ:ZW], v[1], start=False, stop=True).then_inc(oc_full, 1)
                pe.wait_ge(oc_done, MT * N_C)
                pe.wait_ge(w_arg, N_C)
                soft.tensor(pe)

            @block.scalar
            def _(act):
                A = nc.scalar.activation
                turner.copy(act, jobs)
                act.wait_ge(pre, 1)
                A(e1[:, :, :], lf[:, :, :], ACT.Abs).then_inc(abs_, 1)
                act.wait_ge(abs_, 1)
                A(e1[:, :, :], e1[:, :, :], ACT.Exp, scale=-1.0).then_inc(exp_, 1)
                act.wait_ge(exp_, 1)
                A(e1[:, :, :], e1[:, :, :], ACT.Ln, bias=1.0).then_inc(abs_, 1)
                for i in range(N_C + 1):
                    h = i
                    if h < N_C:
                        s = h % 2
                        act.wait_ge(z_full, h + 1)
                        act.wait_ge(z_copied, h + 1)
                        if h >= 2:
                            act.wait_ge(l_done, h - 1)
                        A(az[:, s, :], z[:, s, :], ACT.Abs).then_inc(l_abs, 1)
                        act.wait_ge(l_abs, h + 1)
                        A(ez[:, s, :], az[:, s, :], ACT.Exp, scale=-1.0).then_inc(l_exp, 1)
                        act.wait_ge(l_exp, h + 1)
                        A(ez[:, s, :], ez[:, s, :], ACT.Ln, bias=1.0).then_inc(l_ln, 1)
                    h = i - 1
                    if 0 <= h < N_C:
                        s = h % 2
                        act.wait_ge(w_arg, h + 1)
                        A(w[:, s, :], w[:, s, :], ACT.Exp).then_inc(w_exp, 1)
                soft.scalar(act)

            @block.vector
            def _(dve):
                st = Steps(dve, own_v)
                V = nc.vector
                dve.wait_ge(x_in, 16 * MT)
                dve.wait_ge(const_in, 128)
                for m in range(MT):
                    c = pr[:, m, C_QC:C_QC + N_C * HD]
                    V.tensor_scalar(c, c, SC, None, ALU.mult)
                    c = pr[:, m, C_QD:C_QD + N_D * HD]
                    st.tell(V.tensor_scalar(c, c, SC, None, ALU.mult), scaled)
                st.tell(V.tensor_tensor(lf[:, :, :], pr[:, :, C_FL:C_FL + N_D], bf[:, :].unsqueeze(1).broadcast_to([P, MT, N_D]), ALU.add), pre)
                dve.wait_ge(abs_, 2)
                st.tell(V.scalar_tensor_tensor(lf[:, :, :], lf[:, :, :], 0.0, e1[:, :, :], ALU.min, ALU.subtract), ready)
                dve.wait_ge(cum_full, 1)
                st.tell(V.tensor_copy(cum[:, :, :], rb[0][:, :, 0:N_D]), cum_done)
                dve.wait_ge(cum_full, 2)
                st.tell(V.tensor_scalar(ncT[:, :], ob[0].tensor[0:N_D, 0:SEQ], -1.0, None, ALU.mult), cum_done)
                for i in range(N_C + 3):
                    h = i
                    if h < N_C:
                        s = h % 2
                        dve.wait_ge(z_full, h + 1)
                        if h >= 2:
                            dve.wait_ge(w_exp, h - 1)
                        st.tell(V.tensor_copy(z[:, s, :], zb[s].tensor[:, 0:ZW]), z_copied)
                        if h >= 2:
                            dve.wait_ge(r_full, h - 1)
                        st.link(V.tensor_scalar(ls[:, s, :], z[:, s, :], -1.0, 0.0, ALU.mult, ALU.min))
                        dve.wait_ge(l_ln, h + 1)
                        st.link(V.tensor_tensor(ls[:, s, :], ls[:, s, :], ez[:, s, :], ALU.subtract))
                        d0, d1 = ls[:, s, 0:P], ls[:, s, SEQ:ZW]
                        V.tensor_tensor(d0, d0, before[:, :], ALU.mult)
                        st.tell(V.tensor_tensor(d1, d1, before[:, :], ALU.mult), l_done)
                    h = i - 1
                    if 0 <= h < N_C:
                        s = h % 2
                        dve.wait_ge(r_full, h + 1)
                        if h >= 2:
                            dve.wait_ge(oc_full, h - 1)
                        st.tell(V.tensor_tensor(w[:, s, :], rb[s].tensor[:, 0:ZW], z[:, s, :], ALU.add), w_arg)
                        dve.wait_ge(w_exp, h + 1)
                        d0, d1 = w[:, s, 0:P], w[:, s, SEQ:ZW]
                        V.tensor_tensor(d0, d0, before[:, :], ALU.mult)
                        st.tell(V.tensor_tensor(d1, d1, before[:, :], ALU.mult), w_done)
                    h = i - 2
                    if 0 <= h < N_C:
                        dve.wait_ge(oc_full, h + 1)
                        for m in range(MT):
                            st.tell(V.tensor_copy(yo[:, m, h * HD:(h + 1) * HD], ob[h % 2].tensor[:, m * HD:(m + 1) * HD]), oc_done)
                soft.vector(dve)


G_H, G_W = 8, 1024
R_H, R_D, R_W, R_LORA = 16, 64, 1024, 96
R_FEAT = 3 * R_W + 2 * R_LORA
S_W, S_G, S_C, S_N = 1024, 64, 16, 64
O_GZ = 3 * G_W
O_GB = O_GZ + G_W
O_GA = O_GB + G_H
O_RF = O_GA + G_H
O_RZ = O_RF + R_FEAT
O_SU = O_RZ + R_W
O_SZ = O_SU + S_W
O_GL = O_SZ + S_W
N_IN = O_GL + 3 * D
QUAD = 4
LEVELS = (2, 4, 8, 16, 32, 64)


class Inverter:

    def __init__(self, nc, ph, joins, banks):
        self.nc, self.joins = nc, joins
        self.xb, self.yb, self.tb = banks[0:2], banks[2:4], banks[4:6]
        self.x = ph.sb("inv_x", [P, 2, QUAD * P // 2])
        self.x_full, self.x_done, self.y_full, self.y_done, self.t_full, self.t_done = (ph.sem(s) for s in (
            "inv_x_full", "inv_x_done", "inv_y_full", "inv_y_done", "inv_t_full", "inv_t_done"))

    def tensor(self, pe, rnd, lT, m, mT, ident):
        nc, L, HW = self.nc, len(LEVELS), P // 2
        for l, b in enumerate(LEVELS):
            step = lambda i: (rnd * L + l) * 2 + i
            for i in range(2):
                n = step(i)
                if l:
                    pe.wait_ge(self.y_done, n - 1)
                for h in range(QUAD):
                    c = slice(h * P, (h + 1) * P)
                    even = m[i][:, c].rearrange("p (n two b) -> p n two b", two=2, b=b)[:, :, 0, :]
                    last = nc.tensor.matmul(self.xb[i][:, h * HW:(h + 1) * HW].rearrange("p (n b) -> p n b", b=b),
                                            lT[i][:, c], even, start=True, stop=True)
                last.then_inc(self.x_full, 1)
            for i in range(2):
                n = step(i)
                pe.wait_ge(self.x_done, n + 1)
                if l:
                    pe.wait_ge(self.t_done, n - 1)
                for h in range(QUAD):
                    hc = slice(h * HW, (h + 1) * HW)
                    last = nc.tensor.matmul(self.yb[i][:, hc], mT[i][:, h * P:(h + 1) * P], self.x[:, i, hc], start=True, stop=True)
                last.then_inc(self.y_full, 1)
            for i in range(2):
                pe.wait_ge(self.y_done, step(i) + 1)
                for h in range(QUAD):
                    c = slice(h * P, (h + 1) * P)
                    last = nc.tensor.transpose(self.tb[i][:, c], m[i][:, c], ident)
                last.then_inc(self.t_full, 1)

    def vector(self, dve, rnd, m):
        V, L, HW = self.nc.vector, len(LEVELS), P // 2
        for l, b in enumerate(LEVELS):
            for i in range(2):
                dve.wait_ge(self.x_full, (rnd * L + l) * 2 + i + 1)
                j = self.joins[:, l, :].unsqueeze(1).broadcast_to([P, QUAD, HW])
                V.tensor_tensor(self.x[:, i, :].rearrange("p (h s) -> p h s", h=QUAD),
                                self.xb[i][:, 0:QUAD * HW].rearrange("p (h s) -> p h s", h=QUAD), j, ALU.mult).then_inc(self.x_done, 1)
            for i in range(2):
                dve.wait_ge(self.y_full, (rnd * L + l) * 2 + i + 1)
                even = m[i].rearrange("p (n two b) -> p n two b", two=2, b=b)[:, :, 0, :]
                V.tensor_tensor(even, even, self.yb[i][:, 0:QUAD * HW].rearrange("p (n b) -> p n b", b=b),
                                ALU.subtract).then_inc(self.y_done, 1)

    def scalar(self, act, rnd, mT):
        for l in range(len(LEVELS)):
            for i in range(2):
                act.wait_ge(self.t_full, (rnd * len(LEVELS) + l) * 2 + i + 1)
                self.nc.scalar.copy(mT[i], self.tb[i]).then_inc(self.t_done, 1)

    def finished(self, eng, rnd):
        eng.wait_ge(self.t_done, 2 * len(LEVELS) * (rnd + 1))


def heads4(ap):
    return ap.rearrange("p (h s) -> p h s", h=QUAD)


def gdn(nc, name, C, proj, conv_w, a_log, dt_bias, norm_w, out):
    H, CH = G_H, MT
    NQ = H // QUAD
    with Phase(nc, name) as ph:
        sh = ph.sb("sh", [P, 2, 4, G_W])
        cw = ph.sb("cw", [P, 2, 4, G_W])
        tmp = ph.sb("tmp", [P, G_W])
        qkv = ph.sb("qkv", [P, 3, MT, G_W])
        z = ph.sb("z", [P, MT, G_W])
        ba = ph.sb("ba", [P, MT, 2 * H])
        par = ph.sb("par", [P, 2 * H])
        nw = ph.sb("nw", [P, HD])
        ss = ph.sb("ss", [P, 2 * MT, H])
        rt = ph.sb("rt", [P, 2 * MT, H])
        beta = ph.sb("beta", [P, MT, H])
        g = ph.sb("g", [P, MT, H])
        gt = ph.sb("gt", [P, MT, H])
        gc = ph.sb("gc", [P, MT, H])
        eg = ph.sb("eg", [P, MT, H])
        kd = ph.sb("kd", [P, MT, H])
        gcT = ph.sb("gcT", [H, MT, P])
        ident = ph.sb("ident", [P, P])
        upto = ph.sb("upto", [P, P])
        ones = ph.sb("ones", [P, P])
        low = ph.sb("low", [P, P])
        upi = ph.sb("upi", [P, P])
        join1 = ph.sb("join1", [P, P])
        joins = ph.sb("joins", [P, len(LEVELS), P // 2])
        join1T = ph.sb("join1T", [P, P])
        pick = ph.sb("pick", [H, H, P])
        qT = ph.sb("qT", [P, H, SEQ])
        kT = ph.sb("kT", [P, H, SEQ])
        Q4 = QUAD * P
        el = ph.sb("el", [P, 2, Q4])
        eu = ph.sb("eu", [P, 2, Q4])
        L = ph.sb("L", [P, 2, Q4])
        LT = ph.sb("LT", [P, 2, Q4])
        AT = ph.sb("AT", [P, 2, Q4])
        M = ph.sb("M", [P, 2, Q4])
        MTt = ph.sb("MTt", [P, 2, Q4])
        S = ph.sb("S", [P, Q4])
        X = ph.sb("X", [P, Q4])
        vn = ph.sb("vn", [P, Q4])
        y = ph.sb("y", [P, MT, G_W])
        names = ("tap_in", "x_in", "const_in", "pooled", "conv", "silu", "squared", "ssum", "root", "unit", "own_v",
                 "own_a", "g_in", "g_a", "g_ready", "gc_full", "gc_done", "gcT_full", "gcT_done", "gb_full", "diff",
                 "decay", "kk_full", "kq_full", "l_done", "lT_full", "lT_done", "at_done", "ks_full", "x_done",
                 "vn_full", "vn_done", "o_full", "o_done", "s_full", "s_done", "y_rt", "y_rt_a", "stored", "e_in",
                 "e_a", "tap_used", "zs", "y_ready")
        s = {n: ph.sem(n) for n in names}
        bank = [ph.ps(f"bank{i}", [P, 512]) for i in range(6)]
        turner = Turner(nc, ph, ident)
        inv = Inverter(nc, ph, joins, bank)
        parts = [(m, p) for m in range(MT) for p in range(3)]
        jobs = []
        for m in range(MT):
            for src, dst in ((0, qT), (1, kT)):
                for a in range(0, H, 4):
                    jobs.append(([qkv[:, src, m, (a + i) * P:(a + i + 1) * P] for i in range(4)],
                                 dst[:, a:a + 4, m * P:(m + 1) * P], (s["unit"], 1)))
        CONSTS = ((ident, "ident"), (upto, "upto"), (ones, "ones"), (low, "low"), (upi, "upi"), (join1, "join1"), (join1T, "join1T"))

        with nc.Block() as block:
            @block.sync
            def _(sp):
                sp.dma_start(ba[:, :, :], proj.rearrange("(m p) n -> p m n", p=P)[:, :, O_GB:O_GB + 2 * H]).then_inc(s["x_in"], 16)
                sp.dma_start(par[:, 0:H], bcast_rows(a_log)).then_inc(s["x_in"], 16)
                sp.dma_start(par[:, H:2 * H], bcast_rows(dt_bias)).then_inc(s["x_in"], 16)
                sp.dma_start(nw[:, :], bcast_rows(norm_w)).then_inc(s["x_in"], 16)
                sp.dma_start(z[:, :, :], proj.rearrange("(m p) n -> p m n", p=P)[:, :, O_GZ:O_GZ + G_W]).then_inc(s["x_in"], 16)
                for t, c in CONSTS:
                    sp.dma_start(t[:, :], C[c]).then_inc(s["const_in"], 16)
                sp.dma_start(joins[:, :, :], C["joins"].rearrange("p (a b) -> p a b", b=P // 2)).then_inc(s["const_in"], 16)
                sp.dma_start(pick[:, :, :], C["pick"].rearrange("a (b c) -> a b c", b=H)).then_inc(s["const_in"], 16)
                sp.wait_ge(s["pooled"], 1)
                for n, (m, p) in enumerate(parts):
                    if n >= 2:
                        sp.wait_ge(s["conv"], n - 1)
                        sp.wait_ge(s["tap_used"], n - 1)
                    c = slice(p * G_W, (p + 1) * G_W)
                    for j in range(4):
                        back = 3 - j
                        skip = back if m == 0 else 0
                        sp.dma_start(sh[skip:P, n % 2, j, :], proj[m * P + skip - back:(m + 1) * P - back, c]).then_inc(s["tap_in"], 16)
                        sp.dma_start(cw[:, n % 2, j, :], bcast_rows(conv_w[j, c])).then_inc(s["tap_in"], 16)
                    sp.wait_ge(s["tap_in"], 128 * (n + 1))
                sp.wait_ge(s["y_ready"], 1)
                sp.dma_start(out.rearrange("(m p) n -> p m n", p=P), y[:, :, :]).then_inc(s["stored"], 16)
                sp.wait_ge(s["stored"], 16)

            @block.gpsimd
            def _(pool):
                G = nc.gpsimd
                for j in range(3):
                    for n in range(2):
                        last = G.memset(sh[0:4, n, j, :], 0.0)
                last.then_inc(s["pooled"], 1)
                for n, (m, p) in enumerate(parts):
                    pool.wait_ge(s["tap_in"], 128 * (n + 1))
                    a, b = sh[:, n % 2, 0, :], sh[:, n % 2, 1, :]
                    k = 3 * n + 1
                    G.tensor_tensor(a, a, cw[:, n % 2, 0, :], ALU.mult).then_inc(s["pooled"], 1)
                    G.tensor_tensor(b, b, cw[:, n % 2, 1, :], ALU.mult).then_inc(s["pooled"], 1)
                    pool.wait_ge(s["pooled"], k + 2)
                    G.tensor_tensor(b, a, b, ALU.add).then_inc(s["pooled"], 1)

            @block.scalar
            def _(act):
                A = nc.scalar.activation
                own = Steps(act, s["own_a"])
                act.wait_ge(s["g_in"], 1)
                own.link(A(gt[:, :, :], g[:, :, :], ACT.Abs))
                own.link(A(gt[:, :, :], gt[:, :, :], ACT.Exp, scale=-1.0))
                own.link(A(par[:, 0:H], par[:, 0:H], ACT.Exp))
                own.link(A(beta[:, :, :], ba[:, :, 0:H], ACT.Exp, scale=-1.0))
                own.tell(A(gt[:, :, :], gt[:, :, :], ACT.Ln, bias=1.0), s["g_a"])
                for n, (m, p) in enumerate(parts):
                    act.wait_ge(s["conv"], n + 1)
                    c = qkv[:, p, m, :]
                    A(c, c, ACT.Silu).then_inc(s["silu"], 1)
                A(z[:, :, :], z[:, :, :], ACT.Silu).then_inc(s["zs"], 1)
                act.wait_ge(s["ssum"], 1)
                A(rt[:, :, :], ss[:, :, :], ACT.Sqrt).then_inc(s["root"], 1)
                act.wait_ge(s["e_in"], 1)
                own.link(A(eg[:, :, :], gc[:, :, :], ACT.Exp))
                A(kd[:, :, :], kd[:, :, :], ACT.Exp).then_inc(s["e_a"], 1)
                turner.copy(act, jobs)
                for q in range(NQ):
                    for m in range(MT):
                        n = q * MT + m
                        act.wait_ge(s["diff"], 2 * n + 1)
                        A(el[:, m, :], el[:, m, :], ACT.Exp).then_inc(s["decay"], 1)
                        act.wait_ge(s["diff"], 2 * n + 2)
                        A(eu[:, m, :], eu[:, m, :], ACT.Exp).then_inc(s["decay"], 1)
                    inv.scalar(act, q, [MTt[:, m, :] for m in range(MT)])
                act.wait_ge(s["y_rt"], 1)
                A(rt[:, 0:MT, :], ss[:, 0:MT, :], ACT.Sqrt).then_inc(s["y_rt_a"], 1)

            @block.tensor
            def _(pe):
                T = nc.tensor
                pe.wait_ge(s["const_in"], 144)
                pe.wait_ge(s["g_ready"], 1)
                for m in range(MT):
                    T.matmul(bank[0][:, m * H:(m + 1) * H], upto[:, :], g[:, m, :], start=True, stop=True)
                    last = T.matmul(bank[0][:, (MT + m) * H:(MT + m + 1) * H], ones[:, :], g[:, m, :], start=True, stop=True)
                last.then_inc(s["gc_full"], 1)
                pe.wait_ge(s["gc_done"], 1)
                for m in range(MT):
                    last = T.transpose(bank[1][0:H, m * P:(m + 1) * P], gc[:, m, :], ident[:, :])
                last.then_inc(s["gcT_full"], 1)
                turner.turn(pe, jobs)
                turner.all_copied(pe, len(jobs))
                pe.wait_ge(s["gcT_done"], 1)
                for q in range(NQ):
                    for m in range(MT):
                        n = q * MT + m
                        c = slice(m * P, (m + 1) * P)
                        if n:
                            pe.wait_ge(s["diff"], 2 * n)
                        for h in range(QUAD):
                            last = T.matmul(bank[0][:, h * P:(h + 1) * P], pick[:, q * QUAD + h, :], gcT[:, m, :], start=True, stop=True)
                        last.then_inc(s["gb_full"], 1)
                        if q and m == 0:
                            inv.finished(pe, q - 1)
                            pe.wait_ge(s["o_done"], q * MT)
                            pe.wait_ge(s["s_done"], q)
                        if n:
                            pe.wait_ge(s["l_done"], n)
                            pe.wait_ge(s["at_done"], n)
                            pe.wait_ge(s["lT_done"], n)
                        for h in range(QUAD):
                            k = kT[:, q * QUAD + h, c]
                            last = T.matmul(bank[1][:, h * P:(h + 1) * P], k, k, start=True, stop=True)
                        last.then_inc(s["kk_full"], 1)
                        for h in range(QUAD):
                            last = T.matmul(bank[2][:, h * P:(h + 1) * P], kT[:, q * QUAD + h, c], qT[:, q * QUAD + h, c], start=True, stop=True)
                        last.then_inc(s["kq_full"], 1)
                        pe.wait_ge(s["l_done"], n + 1)
                        for h in range(QUAD):
                            last = T.transpose(bank[3][:, h * P:(h + 1) * P], L[:, m, h * P:(h + 1) * P], ident[:, :])
                        last.then_inc(s["lT_full"], 1)
                    pe.wait_ge(s["lT_done"], (q + 1) * MT)
                    pe.wait_ge(s["at_done"], (q + 1) * MT)
                    sets = [[t[:, m, :] for m in range(MT)] for t in (LT, M, MTt)]
                    inv.tensor(pe, q, *sets, ident[:, :])
                    inv.finished(pe, q)
                    for m in range(MT):
                        n = q * MT + m
                        c = slice(m * P, (m + 1) * P)
                        if m:
                            pe.wait_ge(s["s_done"], q + 1)
                            for h in range(QUAD):
                                last = T.matmul(bank[0][:, h * P:(h + 1) * P], kT[:, q * QUAD + h, c], S[:, h * P:(h + 1) * P], start=True, stop=True)
                            last.then_inc(s["ks_full"], 1)
                        pe.wait_ge(s["x_done"], n + 1)
                        for h in range(QUAD):
                            hc = slice(h * P, (h + 1) * P)
                            last = T.matmul(bank[1][:, hc], MTt[:, m, hc], X[:, hc], start=True, stop=True)
                        last.then_inc(s["vn_full"], 1)
                        pe.wait_ge(s["vn_done"], n + 1)
                        if m == 0:
                            for h in range(QUAD):
                                hc = slice(h * P, (h + 1) * P)
                                last = T.matmul(bank[2][:, hc], qkv[:, 1, m, (q * QUAD + h) * P:(q * QUAD + h + 1) * P], vn[:, hc], start=True, stop=True)
                            last.then_inc(s["s_full"], 1)
                        else:
                            for h in range(QUAD):
                                hc = slice(h * P, (h + 1) * P)
                                T.matmul(bank[3][:, hc], qT[:, q * QUAD + h, c], S[:, hc], start=True, stop=True)
                        for h in range(QUAD):
                            hc = slice(h * P, (h + 1) * P)
                            last = T.matmul(bank[4][:, hc], AT[:, m, hc], vn[:, hc], start=True, stop=True)
                        last.then_inc(s["o_full"], 1)

            @block.vector
            def _(dve):
                V = nc.vector
                st = Steps(dve, s["own_v"])
                W = G_W
                dve.wait_ge(s["x_in"], 80)
                dve.wait_ge(s["const_in"], 144)
                dt = par[:, H:2 * H].unsqueeze(1).broadcast_to([P, MT, H])
                ea = par[:, 0:H].unsqueeze(1).broadcast_to([P, MT, H])
                st.tell(V.tensor_tensor(g[:, :, :], ba[:, :, H:2 * H], dt, ALU.add), s["g_in"])
                dve.wait_ge(s["g_a"], 1)
                st.link(V.scalar_tensor_tensor(g[:, :, :], g[:, :, :], 0.0, gt[:, :, :], ALU.max, ALU.add))
                st.tell(V.scalar_tensor_tensor(g[:, :, :], g[:, :, :], -1.0, ea, ALU.mult, ALU.mult), s["g_ready"])
                st.link(V.tensor_scalar(beta[:, :, :], beta[:, :, :], 1.0, None, ALU.add))
                st.link(V.reciprocal(beta[:, :, :], beta[:, :, :]))
                dve.wait_ge(s["gc_full"], 1)
                st.tell(V.tensor_copy(gc[:, :, :], bank[0][:, 0:MT * H].rearrange("p (m h) -> p m h", m=MT)), s["gc_done"])
                st.tell(V.tensor_tensor(kd[:, :, :], bank[0][:, MT * H:2 * MT * H].rearrange("p (m h) -> p m h", m=MT), gc[:, :, :], ALU.subtract), s["e_in"])
                dve.wait_ge(s["gcT_full"], 1)
                st.tell(V.tensor_copy(gcT[:, :, :], bank[1][0:H, 0:SEQ].rearrange("p (m t) -> p m t", m=MT)), s["gcT_done"])
                for n, (m, p) in enumerate(parts):
                    dve.wait_ge(s["tap_in"], 128 * (n + 1))
                    b = n % 2
                    V.tensor_tensor(tmp[:, :], sh[:, b, 2, :], cw[:, b, 2, :], ALU.mult)
                    st.link(V.tensor_tensor(qkv[:, p, m, :], sh[:, b, 3, :], cw[:, b, 3, :], ALU.mult))
                    st.link(V.tensor_tensor(tmp[:, :], tmp[:, :], qkv[:, p, m, :], ALU.add))
                    dve.wait_ge(s["pooled"], 3 * n + 4)
                    st.tell(V.tensor_tensor(qkv[:, p, m, :], tmp[:, :], sh[:, b, 1, :], ALU.add), s["conv"])
                    dve.sem_inc(s["tap_used"], 1)
                for m in range(MT):
                    for p in range(2):
                        dve.wait_ge(s["silu"], m * 3 + p + 1)
                        c = qkv[:, p, m, :]
                        st.link(V.tensor_tensor(tmp[:, :], c, c, ALU.mult))
                        st.link(V.tensor_reduce(ss[:, 2 * m + p, :], tmp[:, :].rearrange("p (h d) -> p h d", h=H), AX_X, ALU.add))
                st.tell(V.tensor_scalar(ss[:, :, :], ss[:, :, :], 1e-6, None, ALU.add), s["ssum"])
                dve.wait_ge(s["root"], 1)
                st.link(V.reciprocal(rt[:, :, :], rt[:, :, :]))
                for m in range(MT):
                    r = rt[:, 2 * m, :]
                    st.link(V.tensor_scalar(r, r, float(HD) ** -0.5, None, ALU.mult))
                    for p in range(2):
                        c = qkv[:, p, m, :].rearrange("p (h d) -> p h d", h=H)
                        last = V.tensor_tensor(c, c, rt[:, 2 * m + p, :].unsqueeze(2).broadcast_to([P, H, HD]), ALU.mult)
                        st.link(last)
                dve.sem_inc(s["unit"], 1)
                dve.wait_ge(s["silu"], 6)
                turner.all_copied(dve, len(jobs))
                dve.wait_ge(s["e_a"], 1)
                c = qkv[:, 1, 0, :].rearrange("p (h d) -> p h d", h=H)
                st.link(V.tensor_tensor(c, c, kd[:, 0, :].unsqueeze(2).broadcast_to([P, H, HD]), ALU.mult))
                for q in range(NQ):
                    hs = slice(q * QUAD, (q + 1) * QUAD)
                    for m in range(MT):
                        n = q * MT + m
                        col = gc[:, m, hs].unsqueeze(2).broadcast_to([P, QUAD, P])
                        lo, up, lm, am = heads4(el[:, m, :]), heads4(eu[:, m, :]), heads4(L[:, m, :]), heads4(AT[:, m, :])
                        bc = lambda t: t.unsqueeze(1).broadcast_to([P, QUAD, P])
                        dve.wait_ge(s["gb_full"], n + 1)
                        b0 = heads4(bank[0])
                        st.link(V.tensor_tensor(lo, col, b0, ALU.subtract))
                        st.link(V.tensor_tensor(up, b0, col, ALU.subtract))
                        st.tell(V.tensor_tensor(lo, lo, bc(low[:, :]), ALU.add), s["diff"])
                        st.tell(V.tensor_tensor(up, up, bc(upi[:, :]), ALU.add), s["diff"])
                        dve.wait_ge(s["decay"], 2 * n + 1)
                        st.link(V.tensor_tensor(lo, lo, beta[:, m, hs].unsqueeze(2).broadcast_to([P, QUAD, P]), ALU.mult))
                        dve.wait_ge(s["kk_full"], n + 1)
                        if q:
                            inv.finished(dve, q - 1)
                        st.tell(V.tensor_tensor(lm, heads4(bank[1]), lo, ALU.mult), s["l_done"])
                        dve.wait_ge(s["decay"], 2 * n + 2)
                        dve.wait_ge(s["kq_full"], n + 1)
                        st.tell(V.tensor_tensor(am, heads4(bank[2]), up, ALU.mult), s["at_done"])
                        mm, mt, lt = heads4(M[:, m, :]), heads4(MTt[:, m, :]), heads4(LT[:, m, :])
                        st.link(V.tensor_tensor(mm, lm, bc(join1[:, :]), ALU.mult))
                        st.link(V.tensor_tensor(mm, bc(ident[:, :]), mm, ALU.subtract))
                        dve.wait_ge(s["lT_full"], n + 1)
                        st.link(V.tensor_copy(lt, heads4(bank[3])))
                        st.link(V.tensor_tensor(mt, lt, bc(join1T[:, :]), ALU.mult))
                        st.tell(V.tensor_tensor(mt, bc(ident[:, :]), mt, ALU.subtract), s["lT_done"])
                    inv.vector(dve, q, [M[:, m, :] for m in range(MT)])
                    inv.finished(dve, q)
                    for m in range(MT):
                        n = q * MT + m
                        hb = lambda t: t[:, m, hs].unsqueeze(2).broadcast_to([P, QUAD, HD])
                        v = heads4(qkv[:, 2, m, q * QUAD * HD:(q + 1) * QUAD * HD])
                        x = heads4(X[:, :])
                        if m:
                            dve.wait_ge(s["ks_full"], q + 1)
                            st.link(V.tensor_tensor(x, heads4(bank[0]), hb(eg), ALU.mult))
                            st.link(V.tensor_tensor(x, v, x, ALU.subtract))
                            st.tell(V.tensor_tensor(x, x, hb(beta), ALU.mult), s["x_done"])
                        else:
                            st.tell(V.tensor_tensor(x, v, hb(beta), ALU.mult), s["x_done"])
                        dve.wait_ge(s["vn_full"], n + 1)
                        if n:
                            dve.wait_ge(s["o_full"], n)
                        st.tell(V.tensor_copy(vn[:, :], bank[1]), s["vn_done"])
                        yy = heads4(y[:, m, q * QUAD * HD:(q + 1) * QUAD * HD])
                        if m == 0:
                            dve.wait_ge(s["s_full"], q + 1)
                            st.tell(V.tensor_copy(S[:, :], bank[2]), s["s_done"])
                            dve.wait_ge(s["o_full"], n + 1)
                            st.tell(V.tensor_copy(yy, heads4(bank[4])), s["o_done"])
                        else:
                            dve.wait_ge(s["o_full"], n + 1)
                            st.link(V.tensor_tensor(x, heads4(bank[3]), hb(eg), ALU.mult))
                            st.tell(V.tensor_tensor(yy, x, heads4(bank[4]), ALU.add), s["o_done"])
                for m in range(MT):
                    st.link(V.tensor_tensor(tmp[:, :], y[:, m, :], y[:, m, :], ALU.mult))
                    st.link(V.tensor_reduce(ss[:, m, :], tmp[:, :].rearrange("p (h d) -> p h d", h=H), AX_X, ALU.add))
                st.tell(V.tensor_scalar(ss[:, 0:MT, :], ss[:, 0:MT, :], 1.0 / HD, EPS, ALU.mult, ALU.add), s["y_rt"])
                dve.wait_ge(s["y_rt_a"], 1)
                st.link(V.reciprocal(rt[:, 0:MT, :], rt[:, 0:MT, :]))
                dve.wait_ge(s["zs"], 1)
                for m in range(MT):
                    yv = y[:, m, :].rearrange("p (h d) -> p h d", h=H)
                    st.link(V.tensor_tensor(yv, yv, rt[:, m, :].unsqueeze(2).broadcast_to([P, H, HD]), ALU.mult))
                    st.link(V.tensor_tensor(yv, yv, nw[:, :].unsqueeze(1).broadcast_to([P, H, HD]), ALU.mult))
                    st.link(V.tensor_tensor(y[:, m, :], y[:, m, :], z[:, m, :], ALU.mult))
                dve.sem_inc(s["y_ready"], 1)


def rwkv_prepare(nc, name, C, proj, mu, w0, w_up, a0, a_up, k_k, k_a, r_k, al, be, ka, rh, vv, bonus, carry):
    NF = R_FEAT
    W = R_W
    HB = [(0, 512), (512, 1024)]
    with Phase(nc, name) as ph:
        ft = ph.sb("ft", [P, MT, NF])
        pv = ph.sb("pv", [P, MT, NF])
        mub = ph.sb("mub", [P, NF])
        prm = ph.sb("prm", [P, 5, W])
        ups = ph.sb("ups", [R_LORA, 2, W])
        ident = ph.sb("ident", [P, P])
        mid_in = ph.sb("mid_in", [P, P])
        mid_ex = ph.sb("mid_ex", [P, P])
        half = ph.sb("half", [P, 1])
        lw = ph.sb("lw", [P, MT, W])
        a = ph.sb("a", [P, W])
        kk = ph.sb("kk", [P, W])
        t1 = ph.sb("t1", [P, W])
        t2 = ph.sb("t2", [P, W])
        ei = ph.sb("ei", [P, W])
        ni = ph.sb("ni", [P, W])
        ee = ph.sb("ee", [P, W])
        outs = ph.sb("outs", [P, 5, W])
        lT = ph.sb("lT", [R_LORA, MT, 2, P])
        ss = ph.sb("ss", [P, R_H])
        rt = ph.sb("rt", [P, R_H])
        cr = ph.sb("cr", [P, W // P])
        names = ("x_in", "const_in", "zeroed", "mixed_r", "mixed", "tanh", "pre_full", "w_pre", "a_pre", "w_sig",
                 "a_sig", "lw_ready", "c_full", "c_read", "cr_full", "cr_done", "sumsq", "root", "own_v", "own_a",
                 "outs_ready", "stored", "v_stored", "own_p")
        s = {n: ph.sem(n) for n in names}
        bank = [ph.ps(f"bank{i}", [P, 512]) for i in range(6)]
        turner = Turner(nc, ph, ident)
        jobs = [([ft[:, m, 3 * W:3 * W + R_LORA], ft[:, m, 3 * W + R_LORA:NF]], lT[:, m, :, :], (s["tanh"], m + 1))
                for m in range(MT)]
        PR = proj[:, O_RF:O_RF + NF]
        with nc.Block() as block:
            @block.sync
            def _(sp):
                sp.dma_start(ft[:, :, :], PR.rearrange("(m p) n -> p m n", p=P)).then_inc(s["x_in"], 16)
                sp.dma_start(pv[1:P, 0, :], PR[0:P - 1, :]).then_inc(s["x_in"], 16)
                sp.dma_start(pv[:, 1, :], PR[P - 1:SEQ - 1, :]).then_inc(s["x_in"], 16)
                sp.dma_start(mub[:, :], bcast_rows(mu)).then_inc(s["x_in"], 16)
                for t, c in ((ident, "ident"), (mid_in, "mid_in"), (mid_ex, "mid_ex"), (half, "half")):
                    sp.dma_start(t[:, :], C[c]).then_inc(s["const_in"], 16)
                for i, w in enumerate((w0, a0, k_k, k_a, r_k)):
                    sp.dma_start(prm[:, i, :], bcast_rows(w)).then_inc(s["const_in"], 16)
                sp.dma_start(ups[:, 0, :], w_up).then_inc(s["const_in"], 16)
                sp.dma_start(ups[:, 1, :], a_up).then_inc(s["const_in"], 16)
                for m in range(MT):
                    sp.wait_ge(s["outs_ready"], m + 1)
                    for i, o in enumerate((al, be, ka, rh, bonus)):
                        sp.dma_start(o[m * P:(m + 1) * P, :], outs[:, i, :]).then_inc(s["stored"], 16)
                    sp.wait_ge(s["stored"], 80 * (m + 1))
                    sp.dma_start(vv[m * P:(m + 1) * P, :], ft[:, m, 2 * W:3 * W]).then_inc(s["v_stored"], 16)
                sp.wait_ge(s["cr_done"], 1)
                sp.dma_start(carry, cr[:, :]).then_inc(s["v_stored"], 16)
                sp.wait_ge(s["v_stored"], 48)

            @block.gpsimd
            def _(pool):
                G = nc.gpsimd
                st = Steps(pool, s["own_p"])
                G.memset(pv[0:1, 0, :], 0.0).then_inc(s["zeroed"], 1)
                pool.wait_ge(s["zeroed"], 1)
                pool.wait_ge(s["x_in"], 64)
                for m in range(MT):
                    f, p_ = ft[:, m, 0:W], pv[:, m, 0:W]
                    st.link(G.tensor_tensor(p_, p_, f, ALU.subtract))
                    st.link(G.tensor_tensor(p_, p_, mub[:, 0:W], ALU.mult))
                    st.tell(G.tensor_tensor(f, f, p_, ALU.add), s["mixed_r"])

            @block.scalar
            def _(act):
                A = nc.scalar.activation
                st = Steps(act, s["own_a"])
                for m in range(MT):
                    act.wait_ge(s["mixed"], m + 1)
                    w = ft[:, m, 3 * W:3 * W + R_LORA]
                    A(w, w, ACT.Tanh).then_inc(s["tanh"], 1)
                turner.copy(act, jobs)
                for m in range(MT):
                    act.wait_ge(s["w_pre"], m + 1)
                    A(lw[:, m, :], lw[:, m, :], ACT.Sigmoid).then_inc(s["w_sig"], 1)
                    act.wait_ge(s["a_pre"], m + 1)
                    A(a[:, :], a[:, :], ACT.Sigmoid).then_inc(s["a_sig"], 1)
                    act.wait_ge(s["sumsq"], m + 1)
                    A(rt[:, :], ss[:, :], ACT.Sqrt).then_inc(s["root"], 1)
                    act.wait_ge(s["c_full"], m + 1)
                    if m:
                        act.wait_ge(s["outs_ready"], m)
                    for i, (c0, c1) in enumerate(HB):
                        A(ei[:, c0:c1], bank[i], ACT.Exp)
                        A(ni[:, c0:c1], bank[i], ACT.Exp, scale=-1.0)
                        last = A(ee[:, c0:c1], bank[2 + i], ACT.Exp)
                    st.tell(last, s["c_read"])
                act.wait_ge(s["cr_full"], 1)
                A(cr[:, :], bank[4][:, 0:W // P], ACT.Exp).then_inc(s["cr_done"], 1)

            @block.tensor
            def _(pe):
                T = nc.tensor
                pe.wait_ge(s["const_in"], 16 * 11)
                turner.turn(pe, jobs)
                turner.all_copied(pe, len(jobs))
                for m in range(MT):
                    if m:
                        pe.wait_ge(s["c_read"], m)
                    for i, (c0, c1) in enumerate(HB):
                        T.matmul(bank[i], lT[:, m, 0, :], ups[:, 0, c0:c1], start=True, stop=True)
                        last = T.matmul(bank[2 + i], lT[:, m, 1, :], ups[:, 1, c0:c1], start=True, stop=True)
                    last.then_inc(s["pre_full"], 1)
                    pe.wait_ge(s["a_pre"], m + 1)
                    pe.wait_ge(s["lw_ready"], m + 1)
                    for i, (c0, c1) in enumerate(HB):
                        T.matmul(bank[i], mid_in[:, :], lw[:, m, c0:c1], start=True, stop=True)
                        last = T.matmul(bank[2 + i], mid_ex[:, :], lw[:, m, c0:c1], start=True, stop=True)
                    last.then_inc(s["c_full"], 1)
                for p_ in range(W // P):
                    for m in range(MT):
                        last = T.matmul(bank[4][:, p_:p_ + 1], lw[:, m, p_ * P:(p_ + 1) * P], half[:, :],
                                        start=(m == 0), stop=(m == MT - 1))
                last.then_inc(s["cr_full"], 1)

            @block.vector
            def _(dve):
                V = nc.vector
                st = Steps(dve, s["own_v"])
                dve.wait_ge(s["x_in"], 64)
                dve.wait_ge(s["zeroed"], 1)
                for m in range(MT):
                    f, p_ = ft[:, m, W:NF], pv[:, m, W:NF]
                    st.link(V.tensor_tensor(p_, p_, f, ALU.subtract))
                    st.link(V.tensor_tensor(p_, p_, mub[:, W:NF], ALU.mult))
                    st.tell(V.tensor_tensor(f, f, p_, ALU.add), s["mixed"])
                dve.wait_ge(s["const_in"], 16 * 11)
                byh = lambda t: t.rearrange("p (h d) -> p h d", h=R_H)
                each = lambda t: t.unsqueeze(2).broadcast_to([P, R_H, R_D])
                for m in range(MT):
                    r, k, v = (ft[:, m, i * W:(i + 1) * W] for i in range(3))
                    dve.wait_ge(s["pre_full"], m + 1)
                    for i, (c0, c1) in enumerate(HB):
                        last = V.tensor_tensor(lw[:, m, c0:c1], bank[i], prm[:, 0, c0:c1], ALU.add)
                    st.tell(last, s["w_pre"])
                    for i, (c0, c1) in enumerate(HB):
                        last = V.tensor_tensor(a[:, c0:c1], bank[2 + i], prm[:, 1, c0:c1], ALU.add)
                    st.tell(last, s["a_pre"])
                    dve.wait_ge(s["w_sig"], m + 1)
                    st.tell(V.tensor_scalar(lw[:, m, :], lw[:, m, :], -float(np.exp(-0.5)), None, ALU.mult), s["lw_ready"])
                    st.link(V.tensor_tensor(kk[:, :], k, prm[:, 2, :], ALU.mult))
                    st.link(V.tensor_tensor(t1[:, :], kk[:, :], kk[:, :], ALU.mult))
                    st.link(V.tensor_reduce(ss[:, :], byh(t1[:, :]), AX_X, ALU.add))
                    st.tell(V.tensor_scalar(ss[:, :], ss[:, :], 1e-6, None, ALU.add), s["sumsq"])
                    dve.wait_ge(s["a_sig"], m + 1)
                    st.link(V.scalar_tensor_tensor(t1[:, :], a[:, :], 1.0, prm[:, 3, :], ALU.subtract, ALU.mult))
                    st.link(V.scalar_tensor_tensor(k, t1[:, :], 1.0, k, ALU.add, ALU.mult))
                    dve.wait_ge(s["root"], m + 1)
                    st.link(V.reciprocal(rt[:, :], rt[:, :]))
                    st.link(V.tensor_tensor(byh(kk[:, :]), byh(kk[:, :]), each(rt[:, :]), ALU.mult))
                    st.link(V.tensor_tensor(t1[:, :], kk[:, :], a[:, :], ALU.mult))
                    dve.wait_ge(s["mixed_r"], m + 1)
                    if m:
                        dve.wait_ge(s["stored"], 80 * m)
                    st.link(V.tensor_tensor(t2[:, :], r, k, ALU.mult))
                    st.link(V.tensor_tensor(t2[:, :], t2[:, :], prm[:, 4, :], ALU.mult))
                    st.link(V.tensor_reduce(ss[:, :], byh(t2[:, :]), AX_X, ALU.add))
                    st.link(V.tensor_tensor(byh(outs[:, 4, :]), byh(v), each(ss[:, :]), ALU.mult))
                    dve.wait_ge(s["c_read"], m + 1)
                    V.tensor_tensor(outs[:, 0, :], kk[:, :], ee[:, :], ALU.mult)
                    V.tensor_tensor(outs[:, 1, :], t1[:, :], ni[:, :], ALU.mult)
                    V.tensor_tensor(outs[:, 2, :], k, ni[:, :], ALU.mult)
                    st.tell(V.tensor_tensor(outs[:, 3, :], r, ei[:, :], ALU.mult), s["outs_ready"])


def rwkv(nc, name, C, proj, al, be, ka, rh, vv, bonus, carry, lnx_w, lnx_b, out):
    W, CH = R_W, MT
    NQ = R_H // QUAD
    Q4 = QUAD * P
    VC = QUAD * R_D
    with Phase(nc, name) as ph:
        tok = {n: ph.sb(n, [P, MT, W]) for n in ("be", "ka", "vv")}
        src = ph.sb("src", [P, 2, W])
        tT = {n: ph.sb(n + "T", [P, W // P, SEQ]) for n in ("al", "be", "ka", "rh")}
        z = ph.sb("z", [P, MT, W])
        bn = ph.sb("bn", [P, MT, W])
        lnw = ph.sb("lnw", [P, 2, W])
        cr = ph.sb("cr", [P, W // P])
        ident = ph.sb("ident", [P, P])
        low1 = ph.sb("low1", [P, P])
        up1 = ph.sb("up1", [P, P])
        upi1 = ph.sb("upi1", [P, P])
        join1 = ph.sb("join1", [P, P])
        joins = ph.sb("joins", [P, len(LEVELS), P // 2])
        join1T = ph.sb("join1T", [P, P])
        NT = ph.sb("NT", [P, 2, Q4])
        PT = ph.sb("PT", [P, 2, Q4])
        QT = ph.sb("QT", [P, 2, Q4])
        RT = ph.sb("RT", [P, 2, Q4])
        M = ph.sb("M", [P, 2, Q4])
        MTt = ph.sb("MTt", [P, 2, Q4])
        Hs = ph.sb("Hs", [P, QUAD // 2, P])
        X = ph.sb("X", [P, VC])
        nS = ph.sb("nS", [P, VC])
        y = ph.sb("y", [P, MT, W])
        sm = ph.sb("sm", [P, 2, R_H])
        rt = ph.sb("rt", [P, R_H])
        names = ("x_in", "src_in", "const_in", "turned", "n_full", "t_full", "m_done", "mT_done", "nT_done", "r_done", "p_done",
                 "q_done", "x_full", "x_done", "s_full", "s_done", "y_full", "y_done", "h_full", "h_done", "own_v",
                 "var", "root", "zs", "y_ready", "stored")
        s = {n: ph.sem(n) for n in names}
        bank = [ph.ps(f"bank{i}", [P, 512]) for i in range(6)]
        turner = Turner(nc, ph, ident)
        inv = Inverter(nc, ph, joins, bank)
        jobs = []
        for m in range(MT):
            for n, t, ready in (("be", tok["be"][:, m, :], None), ("ka", tok["ka"][:, m, :], None),
                                ("al", src[:, 0, :], (s["src_in"], 32 * (m + 1))), ("rh", src[:, 1, :], None)):
                for g in range(0, W // P, 4):
                    jobs.append(([t[:, (g + i) * P:(g + i + 1) * P] for i in range(4)],
                                 tT[n][:, g:g + 4, m * P:(m + 1) * P], ready))
        CONSTS = ((ident, "ident"), (low1, "low1"), (up1, "before"), (upi1, "upto"), (join1, "join1"), (join1T, "join1T"))
        row = lambda e: slice(e * R_D, (e + 1) * R_D)

        with nc.Block() as block:
            @block.sync
            def _(sp):
                for t, c in CONSTS:
                    sp.dma_start(t[:, :], C[c]).then_inc(s["const_in"], 16)
                sp.dma_start(joins[:, :, :], C["joins"].rearrange("p (a b) -> p a b", b=P // 2)).then_inc(s["const_in"], 16)
                for n, d in (("be", be), ("ka", ka), ("vv", vv)):
                    sp.dma_start(tok[n][:, :, :], d.rearrange("(m p) n -> p m n", p=P)).then_inc(s["x_in"], 16)
                sp.dma_start(cr[:, :], carry).then_inc(s["x_in"], 16)
                sp.dma_start(bn[:, :, :], bonus.rearrange("(m p) n -> p m n", p=P)).then_inc(s["x_in"], 16)
                sp.dma_start(z[:, :, :], proj.rearrange("(m p) n -> p m n", p=P)[:, :, O_RZ:O_RZ + W]).then_inc(s["x_in"], 16)
                sp.dma_start(lnw[:, 0, :], bcast_rows(lnx_w)).then_inc(s["x_in"], 16)
                sp.dma_start(lnw[:, 1, :], bcast_rows(lnx_b)).then_inc(s["x_in"], 16)
                for m in range(MT):
                    if m:
                        sp.wait_ge(turner.turned, len(jobs) // MT)
                    sp.dma_start(src[:, 0, :], al[m * P:(m + 1) * P, :]).then_inc(s["src_in"], 16)
                    sp.dma_start(src[:, 1, :], rh[m * P:(m + 1) * P, :]).then_inc(s["src_in"], 16)
                sp.wait_ge(s["y_ready"], 1)
                sp.dma_start(out.rearrange("(m p) n -> p m n", p=P), y[:, :, :]).then_inc(s["stored"], 16)
                sp.wait_ge(s["stored"], 16)

            @block.scalar
            def _(act):
                A = nc.scalar.activation
                turner.copy(act, jobs)
                act.wait_ge(s["x_in"], 128)
                A(z[:, :, :], z[:, :, :], ACT.Silu).then_inc(s["zs"], 1)
                for q in range(NQ):
                    inv.scalar(act, q, [MTt[:, m, :] for m in range(MT)])
                for m in range(MT):
                    act.wait_ge(s["var"], m + 1)
                    A(rt[:, :], sm[:, 1, :], ACT.Sqrt).then_inc(s["root"], 1)

            @block.tensor
            def _(pe):
                T = nc.tensor
                pe.wait_ge(s["const_in"], 112)
                pe.wait_ge(s["x_in"], 128)
                turner.turn(pe, jobs)
                turner.all_copied(pe, len(jobs))
                for q in range(NQ):
                    def products(b, lhs, rhss, m):
                        for j, rhs in enumerate(rhss):
                            for g in range(QUAD // 2):
                                for e in range(2):
                                    pair = q * QUAD // 2 + g
                                    c = slice(m * P, (m + 1) * P)
                                    o = (2 * j + g) * P
                                    last = T.matmul(bank[b + e][:, o:o + P], tT[lhs][row(e), pair, c],
                                                    tT[rhs][row(e), pair, c], start=True, stop=True)
                        last.then_inc(s["n_full"], 1)
                    for m in range(MT):
                        n = q * MT + m
                        if m:
                            for d in ("m_done", "mT_done", "nT_done", "r_done", "p_done", "q_done"):
                                pe.wait_ge(s[d], n)
                        products(0, "al", ("be",), m)
                        products(2, "be", ("al", "rh"), m)
                        products(4, "ka", ("al", "rh"), m)
                    for d in ("m_done", "mT_done", "nT_done", "r_done", "p_done", "q_done"):
                        pe.wait_ge(s[d], (q + 1) * MT)
                    inv.tensor(pe, q, *[[t[:, m, :] for m in range(MT)] for t in (NT, M, MTt)], ident[:, :])
                    inv.finished(pe, q)
                    for m in range(MT):
                        n = q * MT + m
                        c = slice(m * P, (m + 1) * P)
                        vr = lambda h: slice(h * R_D, (h + 1) * R_D)
                        vq = lambda h: tok["vv"][:, m, (q * QUAD + h) * R_D:(q * QUAD + h + 1) * R_D]
                        if m:
                            pe.wait_ge(s["h_done"], q + 1)
                        def from_state(b, t, g):
                            T.matmul(bank[b][:, g * P:(g + 1) * P], tT[t][:, q * QUAD // 2 + g, c], Hs[:, g, :], start=True, stop=False)

                        for g in range(QUAD // 2):
                            if m:
                                from_state(0, "al", g)
                            for h in (2 * g, 2 * g + 1):
                                last = T.matmul(bank[0][:, vr(h)], PT[:, m, h * P:(h + 1) * P], vq(h), start=(m == 0), stop=(m == 0 or h % 2 == 1))
                        last.then_inc(s["x_full"], 1)
                        pe.wait_ge(s["x_done"], n + 1)
                        for h in range(QUAD):
                            last = T.matmul(bank[1][:, vr(h)], MTt[:, m, h * P:(h + 1) * P], X[:, vr(h)], start=True, stop=True)
                        last.then_inc(s["s_full"], 1)
                        pe.wait_ge(s["s_done"], n + 1)
                        for g in range(QUAD // 2):
                            if m:
                                from_state(2, "rh", g)
                            for h in (2 * g, 2 * g + 1):
                                hc = slice(h * P, (h + 1) * P)
                                T.matmul(bank[2][:, vr(h)], QT[:, m, hc], vq(h), start=(m == 0), stop=False)
                                last = T.matmul(bank[2][:, vr(h)], RT[:, m, hc], nS[:, vr(h)], start=False, stop=(m == 0 or h % 2 == 1))
                        last.then_inc(s["y_full"], 1)
                        if m == 0:
                            for g in range(QUAD // 2):
                                pair = q * QUAD // 2 + g
                                pc = slice(pair * P, (pair + 1) * P)
                                T.matmul(bank[3][:, g * P:(g + 1) * P], tok["ka"][:, m, pc], tok["vv"][:, m, pc], start=True, stop=False)
                                last = T.matmul(bank[3][:, g * P:(g + 1) * P], tok["be"][:, m, pc], nS[:, g * P:(g + 1) * P], start=False, stop=True)
                            last.then_inc(s["h_full"], 1)
                    pe.wait_ge(s["y_done"], (q + 1) * MT)

            @block.vector
            def _(dve):
                V = nc.vector
                st = Steps(dve, s["own_v"])
                dve.wait_ge(s["x_in"], 128)
                dve.wait_ge(s["const_in"], 112)
                bc = lambda t: t.unsqueeze(1).broadcast_to([P, QUAD, P])
                st.link(V.memset(Hs[:, :, :], 0.0))
                for q in range(NQ):
                    for m in range(MT):
                        n = q * MT + m
                        mm, mt = heads4(M[:, m, :]), heads4(MTt[:, m, :])
                        half = lambda b, j: bank[b][:, 2 * j * P:2 * (j + 1) * P].rearrange("p (h s) -> p h s", h=2)
                        two = lambda t: t.unsqueeze(1).broadcast_to([P, 2, P])
                        dve.wait_ge(s["n_full"], 3 * n + 1)
                        for e in range(2):
                            last = V.tensor_tensor(mm[:, e::2, :], half(e, 0), two(join1[:, :]), ALU.mult)
                        st.link(last)
                        st.tell(V.tensor_tensor(mm, bc(ident[:, :]), mm, ALU.subtract), s["m_done"])
                        for b, parts in ((2, ((NT, up1, "nT_done"), (RT, upi1, "r_done"))), (4, ((PT, up1, "p_done"), (QT, upi1, "q_done")))):
                            dve.wait_ge(s["n_full"], 3 * n + 1 + b // 2)
                            for j, (dst, mask, done) in enumerate(parts):
                                for e in range(2):
                                    last = V.tensor_tensor(heads4(dst[:, m, :])[:, e::2, :], half(b + e, j), two(mask[:, :]), ALU.mult)
                                st.tell(last, s[done])
                        st.link(V.tensor_tensor(mt, heads4(NT[:, m, :]), bc(join1T[:, :]), ALU.mult))
                        st.tell(V.tensor_tensor(mt, bc(ident[:, :]), mt, ALU.subtract), s["mT_done"])
                    inv.vector(dve, q, [M[:, m, :] for m in range(MT)])
                    for m in range(MT):
                        n = q * MT + m
                        dve.wait_ge(s["x_full"], n + 1)
                        st.tell(V.tensor_copy(X[:, :], bank[0][:, 0:VC]), s["x_done"])
                        dve.wait_ge(s["s_full"], n + 1)
                        st.tell(V.tensor_scalar(nS[:, :], bank[1][:, 0:VC], -1.0, None, ALU.mult), s["s_done"])
                        dve.wait_ge(s["y_full"], n + 1)
                        st.tell(V.tensor_copy(y[:, m, q * VC:(q + 1) * VC], bank[2][:, 0:VC]), s["y_done"])
                        if m == 0:
                            dve.wait_ge(s["h_full"], q + 1)
                            for g in range(QUAD // 2):
                                pair = q * QUAD // 2 + g
                                for e in range(2):
                                    st.link(V.tensor_scalar(Hs[row(e), g, row(e)], bank[3][row(e), g * P + e * R_D:g * P + (e + 1) * R_D],
                                                            cr[row(e), pair:pair + 1], None, ALU.mult))
                            dve.sem_inc(s["h_done"], 1)
                dve.wait_ge(s["zs"], 1)
                for m in range(MT):
                    byh = lambda t: t.rearrange("p (h d) -> p h d", h=R_H)
                    each = lambda t: t.unsqueeze(2).broadcast_to([P, R_H, R_D])
                    ym, sq = y[:, m, :], src[:, 0, :]
                    st.link(V.tensor_reduce(sm[:, 0, :], byh(ym), AX_X, ALU.add))
                    st.link(V.tensor_scalar(sm[:, 0, :], sm[:, 0, :], 1.0 / R_D, None, ALU.mult))
                    st.link(V.tensor_tensor(byh(ym), byh(ym), each(sm[:, 0, :]), ALU.subtract))
                    st.link(V.tensor_tensor(sq, ym, ym, ALU.mult))
                    st.link(V.tensor_reduce(sm[:, 1, :], byh(sq), AX_X, ALU.add))
                    st.tell(V.tensor_scalar(sm[:, 1, :], sm[:, 1, :], 1.0 / R_D, 64e-5, ALU.mult, ALU.add), s["var"])
                    dve.wait_ge(s["root"], m + 1)
                    st.link(V.reciprocal(rt[:, :], rt[:, :]))
                    st.link(V.tensor_tensor(byh(ym), byh(ym), each(rt[:, :]), ALU.mult))
                    st.link(V.tensor_tensor(ym, ym, lnw[:, 0, :], ALU.mult))
                    st.link(V.tensor_tensor(ym, ym, lnw[:, 1, :], ALU.add))
                    st.link(V.tensor_tensor(ym, ym, bn[:, m, :], ALU.add))
                    st.link(V.tensor_tensor(ym, ym, z[:, m, :], ALU.mult))
                dve.sem_inc(s["y_ready"], 1)


TWO_PI = 2.0 * np.pi
PI_1 = 6.28125
PI_2 = float(np.float32(TWO_PI - PI_1))
PI_3 = float(TWO_PI - PI_1 - PI_2)
ROUND = 1.5 * 2.0 ** 23


def s5_scan(nc, name, C, proj, a_re, a_im, log_dt, b_re, b_im, c_re, c_im, d, out):
    NJ = S_G // 2
    JJ = S_W // P
    PC = 2 * S_C
    with Phase(nc, name) as ph:
        are = ph.sb("are", [NJ, 2, S_N])
        aim = ph.sb("aim", [NJ, 2, S_N])
        ldt = ph.sb("ldt", [NJ, 2])
        prm = ph.sb("prm", [NJ, 5, P])
        w1 = ph.sb("w1", [NJ, P])
        w2 = ph.sb("w2", [NJ, P])
        w3 = ph.sb("w3", [NJ, P])
        w4 = ph.sb("w4", [NJ, P])
        par = ph.sb("par", [P, 5, NJ])
        pw = ph.sb("pw", [P, 2, NJ])
        pw2 = ph.sb("pw2", [P, 2, NJ])
        bre = ph.sb("bre", [P, NJ, S_C])
        bim = ph.sb("bim", [P, NJ, S_C])
        bt = ph.sb("bt", [P, 2, NJ, S_C])
        bp = ph.sb("bp", [P, 2, NJ, PC])
        BT = ph.sb("BT", [P, 2, JJ, P])
        cc = ph.sb("cc", [P, 2, JJ, S_N])
        cp = ph.sb("cp", [P, 3, JJ, P])
        CT = ph.sb("CT", [P, 3, JJ, P])
        parity = ph.sb("parity", [P, 4])
        ident = ph.sb("ident", [P, P])
        u = ph.sb("u", [P, MT, S_W])
        dd = ph.sb("dd", [P, S_W])
        uT = ph.sb("uT", [P, JJ, SEQ])
        tab = ph.sb("tab", [P, NJ, 2, SEQ])
        ta = ph.sb("ta", [P, 2, NJ * P // 4])
        tb = ph.sb("tb", [P, 2, NJ * P // 4])
        b = ph.sb("b", [P, 2, 2, SEQ])
        p1 = ph.sb("p1", [P, 2, SEQ])
        p2 = ph.sb("p2", [P, 2, 2, SEQ])
        v = ph.sb("v", [P, 2, SEQ])
        r = ph.sb("r", [P, 2, 2, SEQ])
        q1 = ph.sb("q1", [P, 2, 2, SEQ])
        q2 = ph.sb("q2", [P, 2, 2, SEQ])
        names = ("par_in", "x_in", "const_in", "own_v", "own_a", "own_p", "dt", "wdt", "mag", "angle", "sines", "prm_ready",
                 "bc_ready", "level", "table_v", "table_p", "bu_full", "b_ready", "p1_done", "p2_done", "r_ready",
                 "q1_done", "q2_done", "y_step", "y_pre", "y_out", "stored", "power")
        s = {n: ph.sem(n) for n in names}
        bu = [ph.ps(f"bu{i}", [P, 2, SEQ]) for i in range(2)]
        yb = [[ph.ps(f"y{m}{i}", [P, 512]) for i in range(2)] for m in range(MT)]
        turner = Turner(nc, ph, ident)
        jobs_u = [([u[:, m, (g + i) * P:(g + i + 1) * P] for i in range(4)], uT[:, g:g + 4, m * P:(m + 1) * P], None)
                  for m in range(MT) for g in range(0, JJ, 4)]
        jobs_p = [([prm[:, i, :] for i in g], par[:, g[0]:g[-1] + 1, :], (s["prm_ready"], 1)) for g in ((0, 1, 2, 3), (4,))]
        jobs_c = [([cp[:, k, g + i, :] for i in range(4)], CT[:, k, g:g + 4, :], (s["bc_ready"], 1)) for k in range(3) for g in range(0, JJ, 4)]
        flat = lambda k: bp[:, k, :, :].rearrange("p j c -> p (j c)")
        jobs_b = [([flat(k)[:, (g + i) * P:(g + i + 1) * P] for i in range(4)], BT[:, k, g:g + 4, :], (s["bc_ready"], 2)) for k in range(2) for g in range(0, JJ, 4)]
        early, late = jobs_u + jobs_p, jobs_c + jobs_b
        levels = [1, 2, 4, 8, 16, 32, 64, 128]
        swap = lambda t: t[:, ::-1, :]

        def double(eng, G, st, n, which, scratch_a, scratch_b):
            for h0 in range(0, NJ, NJ // 4 if n > 32 else NJ):
                h1 = h0 + (NJ // 4 if n > 32 else NJ)
                nj = h1 - h0
                A, B = (t[:, 0:nj * n].rearrange("p (j n) -> p j n", j=nj) for t in (scratch_a, scratch_b))
                co, si = (tab[:, h0:h1, k, 0:n] for k in range(2))
                pc, ps_ = (pw[:, k, h0:h1].unsqueeze(2).broadcast_to([P, nj, n]) for k in range(2))
                x, y_ = (co, si) if which == 0 else (si, co)
                st.link(G.tensor_tensor(A, x, pc, ALU.mult))
                st.link(G.tensor_tensor(B, y_, ps_, ALU.mult))
                st.link(G.tensor_tensor(tab[:, h0:h1, which, n:2 * n], A, B, ALU.subtract if which == 0 else ALU.add))

        with nc.Block() as block:
            @block.sync
            def _(sp):
                sp.dma_start(are[:, :, :], a_re.rearrange("(j e) n -> j e n", e=2)).then_inc(s["par_in"], 16)
                sp.dma_start(aim[:, :, :], a_im.rearrange("(j e) n -> j e n", e=2)).then_inc(s["par_in"], 16)
                sp.dma_start(ldt[:, :], log_dt.rearrange("(j e) -> j e", e=2)).then_inc(s["par_in"], 16)
                sp.dma_start(ident[:, :], C["ident"]).then_inc(s["const_in"], 16)
                sp.dma_start(u[:, :, :], proj.rearrange("(m p) n -> p m n", p=P)[:, :, O_SU:O_SU + S_W]).then_inc(s["const_in"], 16)
                sp.dma_start(parity[:, :], C["parity"]).then_inc(s["x_in"], 16)
                sp.dma_start(bre[:, :, :], b_re.rearrange("(j e) n c -> (e n) j c", e=2)).then_inc(s["x_in"], 16)
                sp.dma_start(bim[:, :, :], b_im.rearrange("(j e) n c -> (e n) j c", e=2)).then_inc(s["x_in"], 16)
                sp.dma_start(cc[:, 0, :, :], c_re.rearrange("(j r) c n -> (r c) j n", r=8)).then_inc(s["x_in"], 16)
                sp.dma_start(cc[:, 1, :, :], c_im.rearrange("(j r) c n -> (r c) j n", r=8)).then_inc(s["x_in"], 16)
                sp.dma_start(dd[:, :], bcast_rows(d)).then_inc(s["x_in"], 16)
                for m in range(MT):
                    sp.wait_ge(s["y_out"], m + 1)
                    sp.dma_start(out[m * P:(m + 1) * P, :], u[:, m, :]).then_inc(s["stored"], 16)
                sp.wait_ge(s["stored"], 16 * MT)

            @block.tensor
            def _(pe):
                T = nc.tensor
                pe.wait_ge(s["const_in"], 32)
                turner.turn(pe, early)
                turner.turn(pe, late)
                turner.all_copied(pe, len(early) + len(late))
                for i in range(NJ + 2):
                    j = i
                    if j < NJ:
                        if j >= 2:
                            pe.wait_ge(s["b_ready"], j - 1)
                        rw = slice((j % 4) * PC, (j % 4 + 1) * PC)
                        for k in range(2):
                            last = T.matmul(bu[j % 2][:, k, :], BT[rw, k, j // 4, :], uT[rw, j // 4, :], start=True, stop=True,
                                            tile_position=((j % 4) * PC, 0))
                        last.then_inc(s["bu_full"], 1)
                    j = i - 2
                    if j >= 0:
                        pe.wait_ge(s["q1_done"], j + 1)
                        pe.wait_ge(s["q2_done"], j + 1)
                        w = slice((j % 4) * PC, (j % 4 + 1) * PC)
                        for m in range(MT):
                            o = yb[m][j // 16][:, (j % 16) * PC:(j % 16 + 1) * PC]
                            terms = ((q1, 0, 0), (q1, 1, 1), (q2, 0, 2), (q2, 1, 2))
                            for k, (q, part, c) in enumerate(terms):
                                last = T.matmul(o, q[:, j % 2, part, m * P:(m + 1) * P], CT[:, c, j // 4, w],
                                                start=(k == 0), stop=(k == 3))
                        last.then_inc(s["y_step"], 1)

            @block.scalar
            def _(act):
                A = nc.scalar.activation
                act.wait_ge(s["par_in"], 48)
                A(ldt[:, :], ldt[:, :], ACT.Exp).then_inc(s["dt"], 1)
                act.wait_ge(s["wdt"], 1)
                A(prm[:, 0, :], w1[:, :], ACT.Exp).then_inc(s["mag"], 1)
                act.wait_ge(s["angle"], 1)
                A(prm[:, 2, :], w3[:, :], ACT.Sin).then_inc(s["sines"], 1)
                A(prm[:, 1, :], w4[:, :], ACT.Sin).then_inc(s["sines"], 1)
                turner.copy(act, early)
                turner.copy(act, late)
                for j in range(NJ):
                    act.wait_ge(s["bu_full"], j + 1)
                    if j >= 2:
                        act.wait_ge(s["p1_done"], j - 1)
                        act.wait_ge(s["p2_done"], j - 1)
                    nc.scalar.copy(b[:, j % 2, :, :], bu[j % 2]).then_inc(s["b_ready"], 1)
                for m in range(MT):
                    act.wait_ge(s["y_pre"], m + 1)
                    A(u[:, m, :], u[:, m, :], ACT.Gelu_apprx_tanh).then_inc(s["y_out"], 1)

            @block.gpsimd
            def _(pool):
                G = nc.gpsimd
                st = Steps(pool, s["own_p"])
                for i, n in enumerate(levels):
                    pool.wait_ge(s["level"], i + 1)
                    double(pool, G, st, n, 1, tb[:, 0, :], tb[:, 1, :])
                    pool.sem_inc(s["table_p"], 1)
                pool.wait_ge(s["table_v"], len(levels))
                for i in range(NJ + 1):
                    j = i
                    if j < NJ:
                        pool.wait_ge(s["b_ready"], j + 1)
                        if j >= 2:
                            pool.wait_ge(s["r_ready"], j - 1)
                        G.tensor_tensor(p2[:, j % 2, :, :], swap(b[:, j % 2, :, :]), tab[:, j, :, :], ALU.mult).then_inc(s["p2_done"], 1)
                    j = i - 1
                    if j >= 0:
                        pool.wait_ge(s["r_ready"], j + 1)
                        if j >= 2:
                            pool.wait_ge(s["y_step"], j - 1)
                        G.tensor_tensor(q2[:, j % 2, :, :], swap(r[:, j % 2, :, :]), tab[:, j, :, :], ALU.mult).then_inc(s["q2_done"], 1)

            @block.vector
            def _(dve):
                V = nc.vector
                st = Steps(dve, s["own_v"])
                L = st.link
                TT, TS = V.tensor_tensor, V.tensor_scalar
                two = lambda t: t.rearrange("j (e n) -> j e n", e=2)
                dtb = ldt[:, :].unsqueeze(2).broadcast_to([NJ, 2, S_N])
                dve.wait_ge(s["dt"], 1)
                st.tell(TT(two(w1[:, :]), are[:, :, :], dtb, ALU.mult), s["wdt"])
                L(TT(two(w2[:, :]), aim[:, :, :], dtb, ALU.mult))
                L(TS(w4[:, :], w2[:, :], 1.0 / TWO_PI, ROUND, ALU.mult, ALU.add))
                L(TS(w4[:, :], w4[:, :], -ROUND, None, ALU.add))
                L(V.scalar_tensor_tensor(w3[:, :], w4[:, :], -PI_1, w2[:, :], ALU.mult, ALU.add))
                L(V.scalar_tensor_tensor(w3[:, :], w4[:, :], -PI_2, w3[:, :], ALU.mult, ALU.add))
                L(V.scalar_tensor_tensor(w3[:, :], w4[:, :], -PI_3, w3[:, :], ALU.mult, ALU.add))
                L(TS(w3[:, :], w3[:, :], 3.1415925, -3.1415925, ALU.min, ALU.max))
                L(V.scalar_tensor_tensor(w4[:, :], w3[:, :], -1.0, w3[:, :], ALU.mult, ALU.max))
                st.tell(TS(w4[:, :], w4[:, :], -1.0, float(np.pi / 2), ALU.mult, ALU.add), s["angle"])
                dve.wait_ge(s["mag"], 1)
                dve.wait_ge(s["sines"], 2)
                ar, ai = are[:, :, :].rearrange("j e n -> j (e n)"), aim[:, :, :].rearrange("j e n -> j (e n)")
                x, y_, den, t = w1[:, :], w2[:, :], w3[:, :], w4[:, :]
                L(TT(x, prm[:, 0, :], prm[:, 1, :], ALU.mult))
                L(TS(x, x, -1.0, None, ALU.add))
                L(TT(y_, prm[:, 0, :], prm[:, 2, :], ALU.mult))
                L(TT(den, ar, ar, ALU.mult))
                L(TT(t, ai, ai, ALU.mult))
                L(TT(den, den, t, ALU.add))
                L(V.reciprocal(den, den))
                for k, (m1, m2, op) in enumerate(((ar, ai, ALU.add), (ai, ar, ALU.subtract))):
                    o = prm[:, 3 + k, :]
                    L(TT(t, x, m1, ALU.mult))
                    L(TT(o, y_, m2, ALU.mult))
                    L(TT(o, o, t, op))
                    last = TT(o, o, den, ALU.mult)
                    L(last)
                dve.sem_inc(s["prm_ready"], 1)
                dve.wait_ge(s["x_in"], 96)
                for k, (src, sign) in enumerate(((0, 0), (0, 2), (1, 2))):
                    for e in range(2):
                        last = TS(cp[:, k, :, e * S_N:(e + 1) * S_N], cc[:, src, :, :], parity[:, sign + e:sign + e + 1], None, ALU.mult)
                        L(last)
                dve.sem_inc(s["bc_ready"], 1)
                turner.all_copied(dve, len(early))
                cr, ci = (par[:, 3 + k, :].unsqueeze(2).broadcast_to([P, NJ, S_C]) for k in range(2))
                L(V.memset(bp[:, :, :, :], 0.0))
                for k, (m1, m2, op) in enumerate(((bre, bim, ALU.subtract), (bim, bre, ALU.add))):
                    L(TT(bt[:, 0, :, :], m1[:, :, :], cr, ALU.mult))
                    L(TT(bt[:, 1, :, :], m2[:, :, :], ci, ALU.mult))
                    for e in range(2):
                        rw = slice(e * S_N, (e + 1) * S_N)
                        L(TT(bp[rw, k, :, e * S_C:(e + 1) * S_C], bt[rw, 0, :, :], bt[rw, 1, :, :], op))
                dve.sem_inc(s["bc_ready"], 1)
                V.memset(tab[:, :, 0, 0:1], 1.0)
                V.memset(tab[:, :, 1, 0:1], 0.0)
                L(V.tensor_copy(pw[:, :, :], par[:, 1:3, :]))
                for i, n in enumerate(levels):
                    dve.sem_inc(s["level"], 1)
                    double(dve, V, st, n, 0, ta[:, 0, :], ta[:, 1, :])
                    dve.wait_ge(s["table_p"], i + 1)
                    if i < len(levels) - 1:
                        L(TT(pw2[:, :, :], pw[:, :, :], pw[:, :, :], ALU.mult))
                        L(TT(pw[:, 1, :], pw[:, 0, :], pw[:, 1, :], ALU.mult))
                        L(TS(pw[:, 1, :], pw[:, 1, :], 2.0, None, ALU.mult))
                        L(TT(pw[:, 0, :], pw2[:, 0, :], pw2[:, 1, :], ALU.subtract))
                    dve.sem_inc(s["table_v"], 1)
                for j in range(NJ):
                    mag = par[:, 0, j:j + 1].broadcast_to([P, SEQ])
                    o = r[:, j % 2, :, :]
                    dve.wait_ge(s["b_ready"], j + 1)
                    st.tell(TT(p1[:, :, :], b[:, j % 2, :, :], tab[:, j, :, :], ALU.mult), s["p1_done"])
                    L(TT(v[:, 0, :], p1[:, 0, :], p1[:, 1, :], ALU.add))
                    if j >= 2:
                        dve.wait_ge(s["q2_done"], j - 1)
                    L(V.tensor_tensor_scan(o[:, 0, :], mag, v[:, 0, :], 0.0, ALU.mult, ALU.add))
                    dve.wait_ge(s["p2_done"], j + 1)
                    L(TT(v[:, 1, :], p2[:, j % 2, 0, :], p2[:, j % 2, 1, :], ALU.subtract))
                    st.tell(V.tensor_tensor_scan(o[:, 1, :], mag, v[:, 1, :], 0.0, ALU.mult, ALU.add), s["r_ready"])
                    if j >= 2:
                        dve.wait_ge(s["y_step"], j - 1)
                    st.tell(TT(q1[:, j % 2, :, :], o, tab[:, j, :, :], ALU.mult), s["q1_done"])
                dve.wait_ge(s["y_step"], NJ)
                for m in range(MT):
                    L(TT(u[:, m, :], u[:, m, :], dd[:, :], ALU.mult))
                    for i in range(2):
                        c = u[:, m, i * 512:(i + 1) * 512]
                        last = TT(c, c, yb[m][i], ALU.add)
                        if i == 0:
                            L(last)
                    st.tell(last, s["y_pre"])


def s5_glu(nc, name, C, proj, yg, glu_w, glu_b, out):
    K = S_W
    KT = K // P
    with Phase(nc, name) as ph:
        yt = ph.sb("yt", [P, MT, K])
        z = ph.sb("z", [P, MT, K])
        gb = ph.sb("gb", [P, K])
        w = ph.sb("w", [P, KT, K])
        ident = ph.sb("ident", [P, P])
        yT = ph.sb("yT", [P, KT, SEQ])
        g = ph.sb("g", [P, MT, K])
        x_in, w_in, zs, full, biased, sig, own, done, stored = (ph.sem(x) for x in (
            "x_in", "w_in", "zs", "full", "biased", "sig", "own", "done", "stored"))
        bank = [[ph.ps(f"bank{m}{i}", [P, 512]) for i in range(2)] for m in range(MT)]
        turner = Turner(nc, ph, ident)
        jobs = [([yt[:, m, (a + i) * P:(a + i + 1) * P] for i in range(4)], yT[:, a:a + 4, m * P:(m + 1) * P], None)
                for m in range(MT) for a in range(0, KT, 4)]
        order = [(i, m) for i in range(2) for m in range(MT)]
        with nc.Block() as block:
            @block.sync
            def _(sp):
                sp.dma_start(yt[:, :, :], yg.rearrange("(m p) n -> p m n", p=P)).then_inc(x_in, 16)
                sp.dma_start(ident[:, :], C["ident"]).then_inc(x_in, 16)
                sp.dma_start(z[:, :, :], proj.rearrange("(m p) n -> p m n", p=P)[:, :, O_SZ:O_SZ + S_W]).then_inc(x_in, 16)
                sp.dma_start(gb[:, :], bcast_rows(glu_b)).then_inc(x_in, 16)
                sp.dma_start(w[:, :, :], glu_w.rearrange("(k p) n -> p k n", p=P)).then_inc(w_in, 16)
                sp.wait_ge(done, 4)
                sp.dma_start(out.rearrange("(m p) n -> p m n", p=P), g[:, :, :]).then_inc(stored, 16)
                sp.wait_ge(stored, 16)

            @block.tensor
            def _(pe):
                pe.wait_ge(x_in, 64)
                turner.turn(pe, jobs)
                turner.all_copied(pe, len(jobs))
                pe.wait_ge(w_in, 16)
                for i, m in order:
                    for k in range(KT):
                        last = nc.tensor.matmul(bank[m][i], yT[:, k, m * P:(m + 1) * P], w[:, k, i * 512:(i + 1) * 512],
                                                start=(k == 0), stop=(k == KT - 1))
                    last.then_inc(full, 1)

            @block.scalar
            def _(act):
                act.wait_ge(x_in, 64)
                turner.copy(act, jobs)
                nc.scalar.activation(z[:, :, :], z[:, :, :], ACT.Silu).then_inc(zs, 1)
                for n, (i, m) in enumerate(order):
                    act.wait_ge(biased, n + 1)
                    c = g[:, m, i * 512:(i + 1) * 512]
                    nc.scalar.activation(c, c, ACT.Sigmoid).then_inc(sig, 1)

            @block.vector
            def _(dve):
                st = Steps(dve, own)
                TT = nc.vector.tensor_tensor
                dve.wait_ge(x_in, 64)
                dve.wait_ge(zs, 1)
                turner.all_copied(dve, len(jobs))
                st.link(TT(yt[:, :, :], yt[:, :, :], z[:, :, :], ALU.mult))
                for n in range(len(order) + 1):
                    if n < len(order):
                        i, m = order[n]
                        c = slice(i * 512, (i + 1) * 512)
                        dve.wait_ge(full, n + 1)
                        st.tell(TT(g[:, m, c], bank[m][i], gb[:, c], ALU.add), biased)
                    if n:
                        i, m = order[n - 1]
                        c = slice(i * 512, (i + 1) * 512)
                        dve.wait_ge(sig, n)
                        st.tell(TT(g[:, m, c], g[:, m, c], yt[:, m, c], ALU.mult), done)


def merge(nc, name, C, proj, branches, w_branch, gate_b, out):
    NBR, K = 3, 1024
    KT, TN = K // P, 512
    with Phase(nc, name) as ph:
        bt = ph.sb("bt", [P, MT, K])
        bT = [ph.sb(f"bT{n}", [P, KT, SEQ]) for n in range(NBR)]
        w = [ph.sb(f"w{n}", [P, KT, TN]) for n in range(NBR)]
        gt = [ph.sb(f"gt{n}", [P, MT, TN]) for n in range(NBR)]
        gb = [ph.sb(f"gb{n}", [P, TN]) for n in range(NBR)]
        mg = ph.sb("mg", [P, MT, TN])
        ident = ph.sb("ident", [P, P])
        const_in, x_in, own, stored = (ph.sem(x) for x in ("const_in", "x_in", "own", "stored"))
        w_full, w_free, acc_full, acc_free, g_full, g_free, biased, sig = ([ph.sem(f"{x}{n}") for n in range(NBR)] for x in (
            "w_full", "w_free", "acc_full", "acc_free", "g_full", "g_free", "biased", "sig"))
        merged = ph.sem("merged")
        acc = [[ph.ps(f"acc{n}{m}", [P, TN]) for m in range(MT)] for n in range(NBR)]
        turner = Turner(nc, ph, ident)
        per = MT * KT // 4
        jobs = [([bt[:, m, (a + i) * P:(a + i + 1) * P] for i in range(4)], bT[n][:, a:a + 4, m * P:(m + 1) * P], (x_in, 16 * (n + 1)))
                for n in range(NBR) for m in range(MT) for a in range(0, KT, 4)]
        projv = proj.rearrange("(m p) n -> p m n", p=P)
        with nc.Block() as block:
            @block.sync
            def _(sp):
                sp.dma_start(ident[:, :], C["ident"]).then_inc(const_in, 16)
                for n in range(NBR):
                    if n:
                        sp.wait_ge(turner.turned, per * n)
                    sp.dma_start(bt[:, :, :], branches[n].rearrange("(m p) n -> p m n", p=P)).then_inc(x_in, 16)
                with sp.Fori(0, D // TN) as c:
                    for n in range(NBR):
                        sp.wait_ge(w_free[n], c + 1)
                        sp.dma_start(w[n][:, :, :], w_branch[n].rearrange("(k p) n -> p k n", p=P)[:, :, bass.ds(c * TN, TN)]).then_inc(w_full[n], 16)

            @block.gpsimd
            def _(pool):
                for n in range(NBR):
                    pool.sem_inc(g_free[n], 1)
                with pool.Fori(0, D // TN) as c:
                    for n in range(NBR):
                        pool.wait_ge(g_free[n], c + 1)
                        pool.dma_start(gt[n][:, :, :], projv[:, :, bass.ds(c * TN + (O_GL + n * D), TN)]).then_inc(g_full[n], 16)
                        pool.dma_start(gb[n][:, :], bcast_rows(gate_b[n])[:, bass.ds(c * TN, TN)]).then_inc(g_full[n], 16)

            @block.tensor
            def _(pe):
                for n in range(NBR):
                    pe.sem_inc(w_free[n], 1)
                pe.wait_ge(const_in, 16)
                turner.turn(pe, jobs)
                turner.all_copied(pe, len(jobs))
                with pe.Fori(0, D // TN) as c:
                    for n in range(NBR):
                        pe.wait_ge(w_full[n], (c + 1) * 16)
                        pe.wait_ge(acc_free[n], c + 1)
                        for k in range(KT):
                            for m in range(MT):
                                last = nc.tensor.matmul(acc[n][m], bT[n][:, k, m * P:(m + 1) * P], w[n][:, k, :],
                                                        start=(k == 0), stop=(k == KT - 1))
                        last.then_inc(acc_full[n], 1)
                        pe.wait_ge(acc_full[n], c + 1)
                        pe.sem_inc(w_free[n], 1)

            @block.scalar
            def _(act):
                turner.copy(act, jobs)
                act.sem_inc(stored, 16)
                with act.Fori(0, D // TN) as c:
                    for n in range(NBR):
                        act.wait_ge(biased[n], c + 1)
                        nc.scalar.activation(gt[n][:, :, :], gt[n][:, :, :], ACT.Sigmoid).then_inc(sig[n], 1)
                    act.wait_ge(merged, c + 1)
                    act.dma_start(out.rearrange("(m p) n -> p m n", p=P)[:, :, bass.ds(c * TN, TN)], mg[:, :, :]).then_inc(stored, 16)
                act.wait_ge(stored, 16 * (D // TN + 1))

            @block.vector
            def _(dve):
                TT = nc.vector.tensor_tensor
                for n in range(NBR):
                    dve.sem_inc(acc_free[n], 1)
                with dve.Fori(0, D // TN) as c:
                    for n in range(NBR):
                        dve.wait_ge(g_full[n], (c + 1) * 32)
                        TT(gt[n][:, :, :], gt[n][:, :, :], gb[n][:, :].unsqueeze(1).broadcast_to([P, MT, TN]), ALU.add).then_inc(biased[n], 1)
                    for n in range(NBR):
                        dve.wait_ge(sig[n], c + 1)
                        dve.wait_ge(acc_full[n], c + 1)
                        if n == 0:
                            dve.wait_ge(stored, (c + 1) * 16)
                        dst = mg if n == 0 else gt[n]
                        for m in range(MT):
                            last = TT(dst[:, m, :], gt[n][:, m, :], acc[n][m], ALU.mult)
                        last.then_inc(own, 1)
                        dve.wait_ge(own, c * (2 * NBR - 1) + (1 if n == 0 else 2 * n))
                        dve.sem_inc(acc_free[n], 1)
                        if n:
                            TT(mg[:, :, :], mg[:, :, :], gt[n][:, :, :], ALU.add).then_inc(own, 1)
                            dve.wait_ge(own, c * (2 * NBR - 1) + 2 * n + 1)
                        dve.sem_inc(g_free[n], 1)
                    dve.sem_inc(merged, 1)


def norm(nc, name, x, g, out):
    with Phase(nc, name) as ph:
        xt = ph.sb("xt", [P, MT, D])
        sq = ph.sb("sq", [P, D])
        gt = ph.sb("gt", [P, D])
        ss = ph.sb("ss", [P, MT])
        rs = ph.sb("rs", [P, MT])
        x_in, squares, mean, root, own, done, stored = (ph.sem(n) for n in ("x_in", "squares", "mean", "root", "own", "done", "stored"))
        with nc.Block() as block:
            @block.sync
            def _(sp):
                sp.dma_start(xt[:, :, :], x.rearrange("(m p) d -> p m d", p=P)).then_inc(x_in, 16)
                sp.dma_start(gt[:, :], bcast_rows(g)).then_inc(x_in, 16)
                for m in range(MT):
                    sp.wait_ge(done, m + 1)
                    sp.dma_start(out[m * P:(m + 1) * P, :], xt[:, m, :]).then_inc(stored, 16)
                sp.wait_ge(stored, 16 * MT)

            @block.scalar
            def _(act):
                act.wait_ge(x_in, 32)
                for m in range(MT):
                    if m:
                        act.wait_ge(squares, m)
                    nc.scalar.activation(sq[:, :], xt[:, m, :], ACT.Square, accum_out=ss[:, m:m + 1]).then_inc(squares, 1)
                act.wait_ge(mean, 1)
                nc.scalar.activation(ss[:, :], rs[:, :], ACT.Sqrt).then_inc(root, 1)

            @block.vector
            def _(dve):
                dve.wait_ge(squares, MT)
                nc.vector.tensor_scalar(rs[:, :], ss[:, :], 1.0 / D, EPS, ALU.mult, ALU.add).then_inc(mean, 1)
                dve.wait_ge(root, 1)
                nc.vector.reciprocal(rs[:, :], ss[:, :]).then_inc(own, 1)
                dve.wait_ge(own, 1)
                for m in range(MT):
                    nc.vector.scalar_tensor_tensor(xt[:, m, :], xt[:, m, :], rs[:, m:m + 1], gt[:, :],
                                                   ALU.mult, ALU.mult).then_inc(done, 1)


def program(nc, a, out):
    def scratch(name, shape):
        return nc.dram_tensor(name, shape, F32).ap()

    x = a["x"][0]
    proj0 = scratch("proj0", [SEQ, a["w_in0"].shape[1]])
    norm_project(nc, "in0", a, x, a["norm0"], a["w_in0"], proj0)
    y0 = scratch("y0", [SEQ, D])
    even_mix(nc, "even", a, proj0, y0)
    x1 = scratch("x1", [SEQ, D])
    gated_project(nc, "out0", a, y0, proj0[:, EVEN_MIX:], a["w_out0"], x, x1)
    proj1 = scratch("proj1", [SEQ, a["w_in1"].shape[1]])
    norm_project(nc, "in1", a, x1, a["norm1"], a["w_in1"], proj1)
    y1 = scratch("y1", [SEQ, D])
    odd_mix(nc, "odd", a, proj1, a["b_f1"], y1)
    x2 = scratch("x2", [SEQ, D])
    gated_project(nc, "out1", a, y1, proj1[:, ODD_MIX:], a["w_out1"], x1, x2)
    x3 = scratch("x3", [SEQ, D])
    norm(nc, "normf", x2, a["norm_f"], x3)
    p2 = {n[:-2]: v[0] for n, v in a.items() if n.endswith("_2") and n != "final_norm_w_2"}
    proj = scratch("proj2", [SEQ, N_IN])
    norm_project(nc, "in2", a, x3, p2["norm_w"], p2["w_in"], proj)
    oa, ob, oc, yg = (scratch(n, [SEQ, 1024]) for n in ("oa", "ob", "oc", "yg"))
    gdn(nc, "gdn", a, proj, p2["gdn_conv_w"], p2["gdn_a_log"], p2["gdn_dt_bias"], p2["gdn_norm_w"], oa)
    rw = [scratch(f"rw_{n}", [SEQ, R_W]) for n in ("al", "be", "ka", "rh", "v", "bonus")]
    carry = scratch("rw_carry", [P, R_W // P])
    rp = {n[5:]: v for n, v in p2.items() if n.startswith("rwkv_")}
    rwkv_prepare(nc, "rwp", a, proj, rp["mu"], rp["w0"], rp["w_up"], rp["a0"], rp["a_up"], rp["k_k"], rp["k_a"],
                 rp["r_k"].rearrange("h d -> (h d)"), *rw, carry)
    rwkv(nc, "rwk", a, proj, *rw, carry, rp["lnx_w"], rp["lnx_b"], ob)
    s5_scan(nc, "s5", a, proj, p2["s5_a_re"], p2["s5_a_im"], p2["s5_log_dt"], p2["s5_b_re"], p2["s5_b_im"],
            p2["s5_c_re"], p2["s5_c_im"], p2["s5_d"], yg)
    s5_glu(nc, "glu", a, proj, yg, p2["s5_glu_w"], p2["s5_glu_b"], oc)
    mg = scratch("merged", [SEQ, D])
    merge(nc, "merge", a, proj, (oa, ob, oc), p2["w_branch"], p2["gate_b"], mg)
    x4 = scratch("x4", [SEQ, D])
    gated_project(nc, "out2", a, mg, None, p2["w_out"], x3, x4)
    norm(nc, "final", x4, a["final_norm_w_2"], out[0])


def constants():
    f = np.float32
    t = np.arange(SEQ)
    c = {"ident": np.eye(P, dtype=f)}
    for n, d in (("", HD), ("i", DI)):
        inv = (f(10000.0) ** (-np.arange(d // 2, dtype=f) / f(d // 2))).astype(f)
        ang = (t.astype(f)[:, None] * inv[None, :]).astype(f)
        c["cos" + n], c["sin" + n] = np.cos(ang).astype(f), np.sin(ang).astype(f)
    dist = t[:, None] - t[None, :]
    before = dist >= 0
    c["causal"] = np.where(before, 0.0, NEG).astype(f)
    times = sum((before & (dist % dil == 0) & (dist // dil <= win // dil)).astype(f)
                for win, dil in ((128, 1), (512, 4), (2048, 16)))
    c["count"] = times.astype(f)
    r = np.arange(P)
    c["before"] = (r[:, None] < r[None, :]).astype(f)
    c["upto"] = (r[:, None] <= r[None, :]).astype(f)
    c["after"] = (r[:, None] >= r[None, :]).astype(f)
    c["low"] = np.where(r[None, :] < r[:, None], 0.0, NEG).astype(f)
    c["upi"] = np.where(r[:, None] <= r[None, :], 0.0, NEG).astype(f)
    joins = [((r[:, None] // b % 2 == 1) & (r[None, :] // b == r[:, None] // b - 1)).astype(f) for b in (1,) + LEVELS]
    c["join1"], c["join1T"] = joins[0], np.ascontiguousarray(joins[0].T)
    c["joins"] = np.concatenate([j[:, r // b % 2 == 0] for j, b in zip(joins[1:], LEVELS)], axis=1)
    c["low1"] = (r[None, :] < r[:, None]).astype(f)
    c["mid_in"] = (c["upto"] - f(0.5)).astype(f)
    c["mid_ex"] = (c["before"] - f(0.5)).astype(f)
    c["half"] = np.full((P, 1), 0.5, f)
    odd = (r // S_C % 2).astype(f)
    c["parity"] = np.stack([1 - odd, odd, odd - 1, -odd], axis=1).astype(f)
    c["ones"] = np.ones((P, P), f)
    c["pick"] = np.repeat(np.eye(8, dtype=f), P, axis=1)
    c["band"] = np.where(times > 0, 0.0, NEG).astype(f)
    return c


def kernel(**inputs):
    from concourse import bacc
    from concourse.bass_utils import run_bass_kernel_spmd

    nc = bacc.Bacc("TRN2", target_bir_lowering=False, num_devices=1)
    arrays, aps = {}, {}
    for name, value in list(inputs.items()) + [("const_" + n, v) for n, v in constants().items()]:
        arrays["in_" + name] = np.ascontiguousarray(value)
        aps[name.removeprefix("const_")] = nc.dram_tensor(
            "in_" + name, arrays["in_" + name].shape, mybir.dt.from_np(arrays["in_" + name].dtype),
            kind="ExternalInput").ap()
    out = nc.dram_tensor("out", (1, SEQ, D), F32, kind="ExternalOutput").ap()
    program(nc, aps, out)
    result = run_bass_kernel_spmd(nc, [arrays], core_ids=[0])
    return result.results[0]["out"]
```

```python
from contextlib import ExitStack

import numpy as np

import concourse.bass as bass
from concourse import mybir

F32 = mybir.dt.float32
F32R = mybir.dt.float32r
ALU = mybir.AluOpType
ACT = mybir.ActivationFunctionType
AX_X = mybir.AxisListType.X
P = 128
SEQ = 256
MT = SEQ // P
D = 2048
EPS = 1e-6
NEG = -1.0e30


class Phase:

    def __init__(self, nc, name):
        self.nc, self.name = nc, name

    def __enter__(self):
        self.stack = ExitStack()
        self.sems = []
        return self

    def sb(self, name, shape, dt=F32):
        return self.stack.enter_context(self.nc.sbuf_tensor(f"{self.name}_{name}", shape, dt))

    def ps(self, name, shape):
        bank = self.stack.enter_context(self.nc.psum_tensor(f"{self.name}_{name}", [P, 512], F32))
        n = int(np.prod(shape[1:]))
        v = bank[0:shape[0], 0:n]
        return v if len(shape) == 2 else v.rearrange("p (a b) -> p a b", a=shape[1])

    def sem(self, name):
        s = self.nc.alloc_semaphore(f"{self.name}_{name}")
        self.sems.append(s)
        return s

    def __exit__(self, *e):
        if e[0] is None:
            self.nc.clear_and_free_semaphores(self.sems)
            self.nc.all_engine_barrier()
        self.stack.close()
        return False


class Chain:

    def __init__(self, eng, sem):
        self.eng, self.sem, self.last = eng, sem, 0

    def step(self, ins):
        self.last += 1
        ins.then_inc(self.sem, 1)
        return self.last

    def settle(self):
        if self.last:
            self.eng.wait_ge(self.sem, self.last)


def bcast_rows(ap, n=P):
    return ap.rearrange("(a w) -> a w", a=1).broadcast_to([n, ap.shape[0]])


TN, Q = 512, 4


class Product:

    def __init__(self, W, out, before=0, rows=None, rows_in=None):
        self.W, self.rows, self.rows_in, self.before = W, rows, rows_in, before
        self.K, self.N = W.shape
        self.tiles = -(-self.N // TN)
        self.Wv = W.rearrange("(k p) n -> p k n", p=P)
        self.outv = None if out is None else out.rearrange("(m p) n -> p m n", p=P)

    def tile(self, t):
        return t % 2, (t + self.before) // 2, t * TN, min(TN, self.N - t * TN)

    def walk(self, eng, one, previous=(None, None), head=None):
        one(self, self.tile(0), *previous)
        if head:
            head()
        pairs = (self.N // TN - 1) // 2 if self.tiles > 4 else 0
        n0 = self.before // 2
        if pairs > 0:
            with eng.Fori(0, pairs) as i:
                one(self, (1, i + n0, i * (2 * TN) + TN, TN), self, (0, i + n0, i * (2 * TN), TN))
                one(self, (0, i + (n0 + 1), i * (2 * TN) + 2 * TN, TN), self, (1, i + n0, i * (2 * TN) + TN, TN))
        for t in range(1 + 2 * pairs, self.tiles):
            one(self, self.tile(t), self, self.tile(t - 1))
        return self, self.tile(self.tiles - 1)


class Gemm:

    def __init__(self, nc, ph, K, products, stage):
        self.nc, self.list = nc, products
        self.KT, self.KQ = K // P, K // P // Q
        self.raw = ph.sb("raw", [P, 2 * Q, self.KQ, TN])
        self.hi = ph.sb("hi", [P, Q, self.KQ, TN], F32R)
        self.lo = ph.sb("lo", [P, Q, self.KQ, TN], F32R)
        self.aT = (ph.sb("aT_hi", [P, self.KT, SEQ], F32R), ph.sb("aT_lo", [P, self.KT, SEQ], F32R))
        self.stage = stage.rearrange("p (s m n) -> p s m n", s=2, m=MT)
        self.acc = [[ph.ps(f"acc{s}{m}", [P, TN]) for m in range(MT)] for s in range(2)]
        self.raw_full = [ph.sem(f"raw_full{r}") for r in range(2 * Q)]
        self.hi_done = [ph.sem(f"hi_done{q}") for q in range(Q)]
        self.lo_done = [ph.sem(f"lo_done{q}") for q in range(Q)]
        self.used = [ph.sem(f"used{q}") for q in range(Q)]
        self.act_staged = [ph.sem(f"act_staged{s}") for s in range(2)]
        self.dve_staged = [ph.sem(f"dve_staged{s}") for s in range(2)]
        self.stored = [ph.sem(f"stored{s}") for s in range(2)]

    def each(self, eng, one, between=None):
        prev = (None, None)
        for i, x in enumerate(self.list):
            prev = x.walk(eng, one, prev, (lambda: between(i - 1)) if i and between else None)
        one(None, None, *prev)

    def load(self, sp):
        def one(x, cur, y, prev):
            if cur is None:
                return
            s, n, c0, w = cur
            for q in range(Q):
                sp.wait_ge(self.lo_done[q], n * 2 + (s + 1))
                sp.dma_start(self.raw[:, s * Q + q, :, 0:w], x.Wv[:, q * self.KQ:(q + 1) * self.KQ, bass.ds(c0, w)]
                             ).then_inc(self.raw_full[s * Q + q], 16)
        self.each(sp, one)

    def tensor(self, pe, turn):
        nc, KT, KQ = self.nc, self.KT, self.KQ

        def one(x, cur, y, prev):
            if cur is None:
                return
            s, n, c0, w = cur
            if x is not y:
                turn(self.list.index(x))
            pe.wait_ge(self.dve_staged[s], n + 1)
            pe.wait_ge(self.act_staged[s], n + 1)
            for q in range(Q):
                pe.wait_ge(self.lo_done[q], n * 2 + (s + 3))
                for k in range(q * KQ, (q + 1) * KQ):
                    for m in range(MT):
                        for a, b, first, end in ((0, self.hi, True, False), (0, self.lo, False, False), (1, self.hi, False, True)):
                            last = nc.tensor.matmul(self.acc[s][m][:, 0:w], self.aT[a][:, k, m * P:(m + 1) * P], b[:, q, k - q * KQ, 0:w],
                                                    start=(k == 0 and first), stop=(k == KT - 1 and end))
                last.then_inc(self.used[q], 1)
        for q in range(Q):
            pe.sem_inc(self.used[q], 1)
        self.each(pe, one)

    def scalar(self, act, between=None, squares=None):
        nc = self.nc

        def one(x, cur, y, prev):
            if cur is not None:
                s, n, c0, w = cur
                for q in range(Q):
                    act.wait_ge(self.raw_full[s * Q + q], (n + 1) * 16)
                    act.wait_ge(self.used[q], n * 2 + (s + 1))
                    nc.scalar.copy(self.hi[:, q, :, 0:w], self.raw[:, s * Q + q, :, 0:w]).then_inc(self.hi_done[q], 1)
            if prev is not None:
                s, n, c0, w = prev
                src = self.stage[:, s, :, 0:w]
                if y.rows is None:
                    act.wait_ge(self.used[Q - 1], n * 2 + (s + 2))
                    act.wait_ge(self.stored[s], (n + 1) * 16)
                    nc.scalar.copy(self.stage[:, s, 0, 0:w], self.acc[s][0][:, 0:w]).then_inc(self.act_staged[s], 1)
                    act.wait_ge(self.act_staged[s], n + 2)
                else:
                    act.sem_inc(self.act_staged[s], 1)
                    src = y.rows[:, :, c0:c0 + w]
                act.wait_ge(self.dve_staged[s], n + 2)
                if y.outv is None:
                    act.sem_inc(self.stored[s], 16)
                else:
                    act.dma_start(y.outv[:, :, bass.ds(c0, w)], src).then_inc(self.stored[s], 16)
                if y.rows is not None and squares:
                    squares(c0 // TN)
        for s in range(2):
            act.sem_inc(self.stored[s], 16)
            act.sem_inc(self.act_staged[s], 1)
        self.each(act, one, between)
        total = self.list[-1].before + self.list[-1].tiles
        for s in range(2):
            act.wait_ge(self.stored[s], 16 * (1 + (total + 1 - s) // 2))

    def vector(self, dve, between=None):
        nc = self.nc

        def one(x, cur, y, prev):
            if cur is not None:
                s, n, c0, w = cur
                for q in range(Q):
                    dve.wait_ge(self.hi_done[q], n * 2 + (s + 1))
                    nc.vector.tensor_tensor(self.lo[:, q, :, 0:w], self.raw[:, s * Q + q, :, 0:w],
                                            self.hi[:, q, :, 0:w].bitcast(F32), ALU.subtract).then_inc(self.lo_done[q], 1)
            if prev is not None:
                s, n, c0, w = prev
                dve.wait_ge(self.used[Q - 1], n * 2 + (s + 2))
                if y.rows is None:
                    dve.wait_ge(self.stored[s], (n + 1) * 16)
                    nc.vector.tensor_copy(self.stage[:, s, 1, 0:w], self.acc[s][1][:, 0:w]).then_inc(self.dve_staged[s], 1)
                else:
                    dve.wait_ge(*y.rows_in)
                    for m in range(MT):
                        r = y.rows[:, m, c0:c0 + w]
                        last = nc.vector.tensor_tensor(r, self.acc[s][m][:, 0:w], r, ALU.add)
                    last.then_inc(self.dve_staged[s], 1)
        self.each(dve, one, between)

    def start(self, dve):
        for q in range(Q):
            dve.sem_inc(self.lo_done[q], 2)
        for s in range(2):
            dve.sem_inc(self.dve_staged[s], 1)


class Steps:

    def __init__(self, eng, sem):
        self.eng, self.own, self.count = eng, sem, {}

    def link(self, ins):
        self.tell(ins, self.own)

    def tell(self, ins, sem, wait=True):
        n = self.count.get(id(sem), 0) + 1
        self.count[id(sem)] = n
        ins.then_inc(sem, 1)
        if wait:
            self.eng.wait_ge(sem, n)


class Turner:

    def __init__(self, nc, ph, ident, name="turn"):
        self.nc, self.ident = nc, ident
        self.bank = [ph.ps(f"{name}{b}", [P, 4, P]) for b in range(2)]
        self.turned = ph.sem(f"{name}_turned")
        self.copied = ph.sem(f"{name}_copied")
        self.hi_copied = ph.sem(f"{name}_hi_copied")
        self.n_pe = self.n_copy = 0

    def turn(self, pe, jobs):
        for srcs, dst, ready in jobs:
            if ready:
                pe.wait_ge(*ready)
            if self.n_pe >= 2:
                pe.wait_ge(self.copied, self.n_pe - 1)
            for j, s in enumerate(srcs):
                rows, cols = s.shape[0], s.free_size()
                last = self.nc.tensor.transpose(self.bank[self.n_pe % 2][0:cols, j, 0:rows], s,
                                                self.ident[0:rows, 0:rows])
            last.then_inc(self.turned, 1)
            self.n_pe += 1

    def copy(self, eng, jobs):
        for srcs, dst, ready in jobs:
            eng.wait_ge(self.turned, self.n_copy + 1)
            rows, cols = srcs[0].shape[0], srcs[0].free_size()
            src = self.bank[self.n_copy % 2][0:cols, 0:len(srcs), 0:rows]
            if eng is self.nc.scalar:
                self.nc.scalar.copy(dst, src).then_inc(self.copied, 1)
            else:
                self.nc.vector.tensor_copy(dst, src).then_inc(self.copied, 1)
            self.n_copy += 1

    def copy_hi(self, act, jobs, base=0):
        for j, (srcs, (hi, lo), ready) in enumerate(jobs, base):
            act.wait_ge(self.turned, j + 1)
            self.nc.scalar.copy(hi, self.bank[j % 2]).then_inc(self.hi_copied, 1)

    def copy_lo(self, dve, jobs, base=0):
        for j, (srcs, (hi, lo), ready) in enumerate(jobs, base):
            dve.wait_ge(self.hi_copied, j + 1)
            self.nc.vector.tensor_tensor(lo, self.bank[j % 2], hi.bitcast(F32), ALU.subtract).then_inc(self.copied, 1)

    def all_copied(self, eng, n):
        eng.wait_ge(self.copied, n)


class SoftmaxHeads:

    def __init__(self, nc, ph, ident, units):
        self.nc, self.ident, self.units = nc, ident, units
        self.lg_ps = [ph.ps(f"lg_ps{b}", [P, SEQ]) for b in range(2)]
        self.pT_ps = [ph.ps(f"pT_ps{b}", [P, MT, P]) for b in range(2)]
        self.o_ps = [ph.ps(f"o_ps{b}", [P, P]) for b in range(2)]
        self.lg = ph.sb("lg", [P, 2, SEQ])
        self.p = ph.sb("p", [P, 3, SEQ])
        self.pT = ph.sb("pT", [P, 2, MT, P])
        self.nmx = ph.sb("nmx", [P, 4])
        self.sm = ph.sb("sm", [P, 4])
        self.rs = ph.sb("rs", [P, 4])
        (self.lg_full, self.lg_masked, self.lg_max, self.p_exp, self.p_counted, self.pT_full, self.pT_copied,
         self.o_full, self.o_recip, self.o_done) = (ph.sem(s) for s in (
             "lg_full", "lg_masked", "lg_max", "p_exp", "p_counted", "pT_full", "pT_copied", "o_full",
             "o_recip", "o_done"))
        self.counted = [sum(1 for x in units[:i + 1] if x.get("count") is not None) for i in range(len(units))]

    def p_ready(self, eng, u):
        if self.units[u].get("count") is not None:
            eng.wait_ge(self.p_counted, self.counted[u])
        else:
            eng.wait_ge(self.p_exp, u + 1)

    def tensor(self, pe):
        nc, U = self.nc, self.units
        for u in range(len(U) + 3):
            if u < len(U):
                x = U[u]
                if x.get("ready"):
                    pe.wait_ge(*x["ready"])
                if u >= 2:
                    pe.wait_ge(self.lg_masked, u - 1)
                more = x.get("extra")
                last = nc.tensor.matmul(self.lg_ps[u % 2][:, 0:x["ns"]], x["q"], x["k"], start=True, stop=not more)
                if more:
                    last = nc.tensor.matmul(self.lg_ps[u % 2][:, 0:x["ns"]], more[0], more[1], start=False, stop=True)
                last.then_inc(self.lg_full, 1)
            v = u - 2
            if 0 <= v < len(U):
                self.p_ready(pe, v)
                if v >= 2:
                    pe.wait_ge(self.pT_copied, v - 1)
                for j in range(U[v]["ns"] // P):
                    last = nc.tensor.transpose(self.pT_ps[v % 2][:, j, :], self.p[:, v % 3, j * P:(j + 1) * P],
                                               self.ident[:, :])
                last.then_inc(self.pT_full, 1)
            w = u - 3
            if 0 <= w < len(U):
                pe.wait_ge(self.pT_copied, w + 1)
                if w >= 2:
                    pe.wait_ge(self.o_done, w - 1)
                n = U[w]["ns"] // P
                for j in range(n):
                    last = nc.tensor.matmul(self.o_ps[w % 2][:, :], self.pT[:, w % 2, j, :], U[w]["v"][j],
                                            start=(j == 0), stop=(j == n - 1))
                last.then_inc(self.o_full, 1)

    def scalar(self, act):
        nc, U = self.nc, self.units
        for u in range(len(U) + 2):
            if u < len(U):
                ns = U[u]["ns"]
                act.wait_ge(self.lg_max, u + 1)
                if u >= 3:
                    act.wait_ge(self.pT_full, u - 2)
                if u >= 4:
                    act.wait_ge(self.o_recip, u - 3)
                nc.scalar.activation(self.p[:, u % 3, 0:ns], self.lg[:, u % 2, 0:ns], ACT.Exp,
                                     bias=self.nmx[:, u % 4:u % 4 + 1],
                                     accum_out=self.sm[:, u % 4:u % 4 + 1]).then_inc(self.p_exp, 1)
            v = u - 2
            if 0 <= v < len(U):
                n = U[v]["ns"] // P
                act.wait_ge(self.pT_full, v + 1)
                if v >= 2:
                    act.wait_ge(self.o_full, v - 1)
                nc.scalar.copy(self.pT[:, v % 2, 0:n, :], self.pT_ps[v % 2][:, 0:n, :]).then_inc(self.pT_copied, 1)

    def vector(self, dve):
        nc, U = self.nc, self.units
        for u in range(len(U) + 3):
            if u < len(U):
                x = U[u]
                ns = x["ns"]
                dve.wait_ge(self.lg_full, u + 1)
                if u >= 2:
                    dve.wait_ge(self.p_exp, u - 1)
                nc.vector.scalar_tensor_tensor(self.lg[:, u % 2, 0:ns], self.lg_ps[u % 2][:, 0:ns], x["scale"],
                                               x["mask"], x.get("op", ALU.mult), ALU.add).then_inc(self.lg_masked, 1)
                dve.wait_ge(self.lg_masked, u + 1)
                nc.vector.tensor_reduce(self.nmx[:, u % 4:u % 4 + 1], self.lg[:, u % 2, 0:ns], AX_X, ALU.max,
                                        negate=True).then_inc(self.lg_max, 1)
            v = u - 1
            if 0 <= v < len(U) and U[v].get("count") is not None:
                ns = U[v]["ns"]
                dve.wait_ge(self.p_exp, v + 1)
                p = self.p[:, v % 3, 0:ns]
                nc.vector.tensor_tensor_reduce(p, p, U[v]["count"], 1.0, 0.0, ALU.mult, ALU.add,
                                               self.sm[:, v % 4:v % 4 + 1]).then_inc(self.p_counted, 1)
            w = u - 3
            if 0 <= w < len(U):
                self.p_ready(dve, w)
                nc.vector.reciprocal(self.rs[:, w % 4:w % 4 + 1], self.sm[:, w % 4:w % 4 + 1]).then_inc(self.o_recip, 1)
                dve.wait_ge(self.o_recip, w + 1)
                dve.wait_ge(self.o_full, w + 1)
                nc.vector.tensor_scalar(U[w]["out"], self.o_ps[w % 2][:, :], self.rs[:, w % 4:w % 4 + 1], None,
                                        ALU.mult).then_inc(self.o_done, 1)


def turn_operand(aT, rows, ready):
    return [([rows[:, m, (4 * g + j) * P:(4 * g + j + 1) * P] for j in range(4)],
             tuple(t[:, 4 * g:4 * g + 4, m * P:(m + 1) * P] for t in aT), (ready, m + 1))
            for m in range(MT) for g in range(aT[0].shape[1] // 4)]


def seam(nc, name, C, x, mixed=None, norms=(), sum_out=None, rows_out=None, projected=None):
    with Phase(nc, name) as ph:
        at = ph.sb("at", [P, MT, D])
        xt = ph.sb("xt", [P, MT, D])
        gw = ph.sb("gw", [P, D])
        ss = ph.sb("ss", [P, MT, D // TN])
        ms = ph.sb("ms", [P, MT])
        rs = ph.sb("rs", [P, MT])
        ident = ph.sb("ident", [P, P])
        x_in, const_in, gw_in, silu, gated, res_in, squares, root, own, scaled, rows_stored = (ph.sem(s) for s in (
            "x_in", "const_in", "gw_in", "silu", "gated", "res_in", "squares", "root", "own", "scaled", "rows_stored"))
        turner = Turner(nc, ph, ident)
        products = []
        if mixed:
            a, gate, W = mixed
            products.append(Product(W, sum_out, rows=xt, rows_in=(res_in, 16)))
        if projected:
            products.append(Product(*projected, before=products[0].tiles if mixed else 0))
        mm = Gemm(nc, ph, D, products, stage=xt[:, 0, :])
        NN = len(norms)
        jobs = []
        if mixed:
            jobs.append(turn_operand(mm.aT, at, gated))
        if projected:
            jobs.append([(srcs, dst, (scaled, MT * (NN - 1) + r)) for srcs, dst, (_, r) in turn_operand(mm.aT, at, scaled)])
        base = [sum(len(x) for x in jobs[:i]) for i in range(len(jobs) + 1)]
        target = lambda n: at if n == NN - 1 else xt
        sq = at[:, 0, 0:TN]

        def rows_left(eng):
            if mixed and sum_out is not None:
                for x in mm.stored:
                    eng.wait_ge(x, 16 * (1 + products[0].tiles // 2))
            if NN > 1:
                eng.wait_ge(rows_stored, 16)
        rowsv = lambda ap: ap.rearrange("(m p) d -> p m d", p=P)

        with nc.Block() as block:
            @block.sync
            def _(sp):
                if mixed:
                    sp.dma_start(at[:, :, :], rowsv(a)).then_inc(x_in, 16)
                    if gate is not None:
                        sp.dma_start(xt[:, :, :], rowsv(gate)).then_inc(x_in, 16)
                    sp.dma_start(ident[:, :], C["ident"]).then_inc(const_in, 16)
                else:
                    sp.dma_start(xt[:, :, :], rowsv(x)).then_inc(x_in, 16)
                    sp.dma_start(ident[:, :], C["ident"]).then_inc(const_in, 16)
                    sp.dma_start(gw[:, :], bcast_rows(norms[0])).then_inc(gw_in, 16)
                mm.load(sp)

            @block.gpsimd
            def _(pool):
                if mixed:
                    pool.wait_ge(gated, MT)
                    pool.dma_start(xt[:, :, :], rowsv(x)).then_inc(res_in, 16)
                for n, g in enumerate(norms):
                    if n:
                        pool.wait_ge(scaled, MT * n)
                        pool.dma_start(rowsv(rows_out), xt[:, :, :]).then_inc(rows_stored, 16)
                    if n or mixed:
                        pool.dma_start(gw[:, :], bcast_rows(g)).then_inc(gw_in, 16)
                if rows_out is not None:
                    if NN == 1:
                        pool.wait_ge(scaled, MT)
                        pool.dma_start(rowsv(rows_out), at[:, :, :]).then_inc(rows_stored, 16)
                    pool.wait_ge(rows_stored, 16)

            @block.tensor
            def _(pe):
                def turn(i):
                    if i == 0:
                        pe.wait_ge(const_in, 16)
                    turner.turn(pe, jobs[i])
                    turner.all_copied(pe, base[i + 1])
                mm.tensor(pe, turn)

            @block.scalar
            def _(act):
                count = [0]

                def square(m, t, n):
                    c = slice(t * TN, (t + 1) * TN)
                    if count[0]:
                        act.wait_ge(squares, count[0])
                    nc.scalar.activation(sq, xt[:, m, c], ACT.Square, accum_out=ss[:, m, t:t + 1]).then_inc(squares, 1)
                    count[0] += 1

                def square_tile(t):
                    for m in range(MT):
                        square(m, t, 0)

                def norm_parts():
                    for n in range(NN):
                        if n:
                            act.wait_ge(scaled, MT * n)
                        if n or not mixed:
                            for t in range(D // TN):
                                square_tile(t)
                        act.wait_ge(own, 4 * n + 2)
                        nc.scalar.activation(rs[:, :], ms[:, :], ACT.Sqrt).then_inc(root, 1)
                    if projected:
                        turner.copy_hi(act, jobs[-1], base[-2])
                        rows_left(act)
                if mixed:
                    if gate is not None:
                        act.wait_ge(x_in, 32)
                        for m in range(MT):
                            nc.scalar.activation(xt[:, m, :], xt[:, m, :], ACT.Silu).then_inc(silu, 1)
                    turner.copy_hi(act, jobs[0])
                    mm.scalar(act, lambda i: norm_parts(), square_tile)
                    if not projected:
                        norm_parts()
                else:
                    act.wait_ge(x_in, 16)
                    norm_parts()
                    mm.scalar(act)

            @block.vector
            def _(dve):
                V = nc.vector

                def norm_parts():
                    for n in range(NN):
                        dve.wait_ge(squares, (n + 1) * MT * (D // TN))
                        V.tensor_reduce(ms[:, :], ss[:, :, :], AX_X, ALU.add).then_inc(own, 1)
                        dve.wait_ge(own, 4 * n + 1)
                        V.tensor_scalar(ms[:, :], ms[:, :], 1.0 / D, EPS, ALU.mult, ALU.add).then_inc(own, 1)
                        dve.wait_ge(root, n + 1)
                        V.reciprocal(rs[:, :], rs[:, :]).then_inc(own, 1)
                        dve.wait_ge(own, 4 * n + 3)
                        dve.wait_ge(gw_in, 16 * (n + 1))
                        for m in range(MT):
                            V.scalar_tensor_tensor(target(n)[:, m, :], xt[:, m, :], rs[:, m:m + 1], gw[:, :],
                                                   ALU.mult, ALU.mult).then_inc(scaled, 1)
                        dve.wait_ge(scaled, MT * (n + 1))
                        dve.sem_inc(own, 1)
                    if projected:
                        turner.copy_lo(dve, jobs[-1], base[-2])
                        rows_left(dve)
                mm.start(dve)
                if mixed:
                    dve.wait_ge(x_in, 16 if gate is None else 32)
                    for m in range(MT):
                        if gate is None:
                            dve.sem_inc(gated, 1)
                        else:
                            dve.wait_ge(silu, m + 1)
                            V.tensor_tensor(at[:, m, :], at[:, m, :], xt[:, m, :], ALU.mult).then_inc(gated, 1)
                    turner.copy_lo(dve, jobs[0])
                    mm.vector(dve, lambda i: norm_parts())
                    if not projected:
                        norm_parts()
                else:
                    norm_parts()
                    mm.vector(dve)


HD = 128
N_A, N_B, N_I, DI = 10, 6, 16, 64
TOPK = min(256, SEQ // 4)
EVEN_MIX = (N_A + 2) * HD + N_I * DI + DI + N_I + 3 * N_B * HD
C_KA = N_A * HD
C_VA = C_KA + HD
C_IQ = C_VA + HD
C_IK = C_IQ + N_I * DI
C_IW = C_IK + DI
C_QB = C_IW + N_I
C_KB = C_QB + N_B * HD
C_VB = C_KB + N_B * HD
TAKEN = -3.0e38


def even_mix(nc, name, C, proj, y):
    SC = float(HD) ** -0.5
    with Phase(nc, name) as ph:
        pr = ph.sb("pr", [P, MT, EVEN_MIX])
        cos = ph.sb("cos", [P, MT, HD // 2])
        sin = ph.sb("sin", [P, MT, HD // 2])
        cosi = ph.sb("cosi", [P, MT, DI // 2])
        sini = ph.sb("sini", [P, MT, DI // 2])
        causal = ph.sb("causal", [P, MT, SEQ])
        band = ph.sb("band", [P, MT, SEQ])
        count = ph.sb("count", [P, MT, SEQ])
        ident = ph.sb("ident", [P, P])
        W = 2 * N_B * HD
        t1 = ph.sb("t1", [P, W // 2])
        t2 = ph.sb("t2", [P, W // 2])
        t3 = ph.sb("t3", [P, W // 2])
        t4 = ph.sb("t4", [P, W // 2])
        ikk = ph.sb("ikk", [P, MT, 2 * DI])
        qkT = ph.sb("qkT", [P, N_A + 1 + 2 * N_B, SEQ])
        iT = ph.sb("iT", [P, N_I // 2 + 1, SEQ])
        relu = ph.sb("relu", [P, 4, SEQ])
        iw = ph.sb("iw", [P, MT, N_I])
        score = ph.sb("score", [P, MT, SEQ])
        top8 = ph.sb("top8", [P, 8])
        sel = ph.sb("sel", [P, MT, SEQ])
        yo = ph.sb("yo", [P, MT, D])
        x_in, const_in, roped, dots_full, dots_relu, added, chosen, own_v, stored = (ph.sem(s) for s in (
            "x_in", "const_in", "roped", "dots_full", "dots_relu", "added", "chosen", "own_v", "stored"))
        turner = Turner(nc, ph, ident)
        prv = proj.rearrange("(m p) n -> p m n", p=P)

        def heads(m, c0, n, w=HD):
            return [pr[:, m, c0 + i * w:c0 + (i + 1) * w] for i in range(n)]

        jobs = []
        for m in range(MT):
            cols = slice(m * P, (m + 1) * P)
            srcs = heads(m, 0, N_A + 1) + heads(m, C_QB, 2 * N_B)
            for g in range(0, len(srcs), 4):
                part = srcs[g:g + 4]
                jobs.append((part, qkT[:, g:g + len(part), cols], (roped, m + 1)))
            srcs = heads(m, C_IQ, N_I // 2) + [ikk[:, m, :]]
            for g in range(0, len(srcs), 4):
                part = srcs[g:g + 4]
                jobs.append((part, iT[:, g:g + len(part), cols], (roped, m + 1)))

        units = []
        for m in range(MT):
            ns = (m + 1) * P
            cols = slice(m * P, (m + 1) * P)
            for h in range(N_B):
                units.append(dict(q=qkT[:, N_A + 1 + h, cols], k=qkT[:, N_A + 1 + N_B + h, 0:ns], ns=ns, scale=SC,
                                  mask=band[:, m, 0:ns], count=count[:, m, 0:ns],
                                  v=[pr[:, j, C_VB + h * HD:C_VB + (h + 1) * HD] for j in range(m + 1)],
                                  out=yo[:, m, (N_A + h) * HD:(N_A + h + 1) * HD]))
        for m in range(MT):
            ns = (m + 1) * P
            cols = slice(m * P, (m + 1) * P)
            for h in range(N_A):
                units.append(dict(q=qkT[:, h, cols], k=qkT[:, N_A, 0:ns], ns=ns, scale=SC,
                                  mask=sel[:, m, 0:ns],
                                  v=[pr[:, j, C_VA:C_VA + HD] for j in range(m + 1)],
                                  out=yo[:, m, h * HD:(h + 1) * HD]))
        soft = SoftmaxHeads(nc, ph, ident, units)
        dots = [(m, h) for m in range(MT) for h in range(N_I)]

        with nc.Block() as block:
            @block.sync
            def _(sp):
                for m in range(MT):
                    sp.dma_start(pr[:, m, :], prv[:, m, 0:EVEN_MIX]).then_inc(x_in, 16)
                for t, c in ((cos, "cos"), (sin, "sin"), (cosi, "cosi"), (sini, "sini"), (causal, "causal"),
                             (band, "band"), (count, "count")):
                    sp.dma_start(t[:, :, :], C[c].rearrange("(m p) n -> p m n", p=P)).then_inc(const_in, 16)
                sp.dma_start(ident[:, :], C["ident"]).then_inc(const_in, 16)
                sp.wait_ge(soft.o_done, len(units))
                sp.dma_start(y.rearrange("(m p) n -> p m n", p=P), yo[:, :, :]).then_inc(stored, 16)
                sp.wait_ge(stored, 16)

            @block.tensor
            def _(pe):
                pe.wait_ge(const_in, 128)
                turner.turn(pe, jobs)
                turner.all_copied(pe, len(jobs))
                for n, (m, h) in enumerate(dots):
                    ns = (m + 1) * P
                    r = slice((h % 2) * DI, (h % 2 + 1) * DI)
                    if n >= 2:
                        pe.wait_ge(dots_relu, n - 1)
                    nc.tensor.matmul(soft.lg_ps[n % 2][:, 0:ns], iT[r, h // 2, m * P:(m + 1) * P],
                                     iT[r, N_I // 2, 0:ns], start=True, stop=True).then_inc(dots_full, 1)
                pe.wait_ge(dots_relu, len(dots))
                pe.wait_ge(chosen, 1)
                soft.tensor(pe)

            @block.scalar
            def _(act):
                turner.copy(act, jobs)
                for n, (m, h) in enumerate(dots):
                    ns = (m + 1) * P
                    act.wait_ge(dots_full, n + 1)
                    if n >= 4:
                        act.wait_ge(added, n - 3)
                    nc.scalar.activation(relu[:, n % 4, 0:ns], soft.lg_ps[n % 2][:, 0:ns], ACT.Relu,
                                         scale=float(DI) ** -0.5).then_inc(dots_relu, 1)
                soft.scalar(act)

            @block.vector
            def _(dve):
                st = Steps(dve, own_v)
                V = nc.vector
                dve.wait_ge(x_in, 16 * MT)
                dve.wait_ge(const_in, 128)
                for m in range(MT):
                    for c0, n, w, co, si in ((0, N_A + 1, HD, cos, sin), (C_QB, 2 * N_B, HD, cos, sin),
                                             (C_IQ, N_I + 1, DI, cosi, sini)):
                        hw = w // 2
                        x = pr[:, m, c0:c0 + n * w].rearrange("p (h d) -> p h d", h=n)
                        a, b = x[:, :, 0:hw], x[:, :, hw:w]
                        cb = co[:, m, :].unsqueeze(1).broadcast_to([P, n, hw])
                        sb_ = si[:, m, :].unsqueeze(1).broadcast_to([P, n, hw])
                        tv = [t[:, 0:n * hw].rearrange("p (h d) -> p h d", h=n) for t in (t1, t2, t3, t4)]
                        V.tensor_tensor(tv[0], a, cb, ALU.mult)
                        V.tensor_tensor(tv[1], b, sb_, ALU.mult)
                        V.tensor_tensor(tv[2], b, cb, ALU.mult)
                        st.link(V.tensor_tensor(tv[3], a, sb_, ALU.mult))
                        V.tensor_tensor(a, tv[0], tv[1], ALU.subtract)
                        st.link(V.tensor_tensor(b, tv[2], tv[3], ALU.add))
                    V.tensor_scalar(iw[:, m, :], pr[:, m, C_IW:C_IW + N_I], float(N_I) ** -0.5, None, ALU.mult)
                    st.tell(V.tensor_copy(ikk[:, m, :].rearrange("p (a d) -> p a d", a=2),
                                          pr[:, m, C_IK:C_IK + DI].unsqueeze(1).broadcast_to([P, 2, DI])), roped)
                for n, (m, h) in enumerate(dots):
                    ns = (m + 1) * P
                    dve.wait_ge(dots_relu, n + 1)
                    if h == 0:
                        i = V.tensor_scalar(score[:, m, 0:ns], relu[:, n % 4, 0:ns], iw[:, m, 0:1], None, ALU.mult)
                    else:
                        i = V.scalar_tensor_tensor(score[:, m, 0:ns], relu[:, n % 4, 0:ns], iw[:, m, h:h + 1],
                                                   score[:, m, 0:ns], ALU.mult, ALU.add)
                    st.tell(i, added)
                for m in range(MT):
                    ns = (m + 1) * P
                    s = score[:, m, 0:ns]
                    st.link(V.tensor_tensor(s, s, causal[:, m, 0:ns], ALU.add))
                    for _ in range(TOPK // 8):
                        st.link(V.max(top8[:, :], s))
                        st.link(V.match_replace(s, top8[:, :], s, TAKEN))
                    st.link(V.tensor_scalar(s, s, TAKEN / 2, None, ALU.is_lt))
                    st.link(V.tensor_scalar(s, s, -NEG, NEG, ALU.mult, ALU.add))
                    st.link(V.tensor_tensor(sel[:, m, 0:ns], s, causal[:, m, 0:ns], ALU.add))
                dve.sem_inc(chosen, 1)
                soft.vector(dve)


N_C, N_D = 8, 8
C_QC, C_KC, C_VC = 0, N_C * HD, 2 * N_C * HD
C_QD, C_KD, C_VD = 3 * N_C * HD, 3 * N_C * HD + N_D * HD, 3 * N_C * HD + 2 * N_D * HD
C_FL = 3 * (N_C + N_D) * HD
ODD_MIX = C_FL + N_D


def odd_mix(nc, name, C, proj, b_f, y):
    SC = float(HD) ** -0.5
    ZW = SEQ + P
    NB = 2
    with Phase(nc, name) as ph:
        pr = ph.sb("pr", [P, MT, ODD_MIX])
        qkT = ph.sb("qkT", [P, 2 * N_C + 2 * N_D, SEQ])
        causal = ph.sb("causal", [P, MT, SEQ])
        before = ph.sb("before", [P, P])
        upto = ph.sb("upto", [P, P])
        after = ph.sb("after", [P, P])
        ones = ph.sb("ones", [P, P])
        pick = ph.sb("pick", [N_D, N_D, P])
        ident = ph.sb("ident", [P, P])
        bf = ph.sb("bf", [P, N_D])
        lf = ph.sb("lf", [P, MT, N_D])
        e1 = ph.sb("e1", [P, MT, N_D])
        cum = ph.sb("cum", [P, MT, N_D])
        ncT = ph.sb("ncT", [N_D, SEQ])
        z = ph.sb("z", [P, 2, ZW])
        az = ph.sb("az", [P, 2, ZW])
        ez = ph.sb("ez", [P, 2, ZW])
        ls = ph.sb("ls", [P, 2, ZW])
        w = ph.sb("w", [P, 2, ZW])
        yo = ph.sb("yo", [P, MT, D])
        (x_in, const_in, ready, pre, abs_, exp_, cum_full, cum_done, z_full, z_out, l_abs, l_exp, l_ln, l_done,
         r_full, w_arg, w_exp, w_done, oc_full, oc_done, own_v, stored, scaled, z_copied) = (ph.sem(s) for s in (
             "x_in", "const_in", "ready", "pre", "abs", "exp", "cum_full", "cum_done", "z_full", "z_out", "l_abs",
             "l_exp", "l_ln", "l_done", "r_full", "w_arg", "w_exp", "w_done", "oc_full", "oc_done", "own_v",
             "stored", "scaled", "z_copied"))
        turner = Turner(nc, ph, ident)
        srcs0 = [C_QC + i * HD for i in range(2 * N_C)] + [C_QD + i * HD for i in range(2 * N_D)]
        jobs = []
        for m in range(MT):
            for g in range(0, len(srcs0), 4):
                jobs.append(([pr[:, m, c:c + HD] for c in srcs0[g:g + 4]],
                             qkT[:, g:g + 4, m * P:(m + 1) * P], (scaled, m + 1)))
        units = []
        for m in range(MT):
            ns = (m + 1) * P
            for h in range(N_D):
                units.append(dict(q=qkT[:, 2 * N_C + h, m * P:(m + 1) * P], k=qkT[:, 2 * N_C + N_D + h, 0:ns],
                                  ns=ns, scale=cum[:, m, h:h + 1], op=ALU.add, mask=causal[:, m, 0:ns],
                                  extra=(pick[:, h, :], ncT[:, 0:ns]),
                                  v=[pr[:, j, C_VD + h * HD:C_VD + (h + 1) * HD] for j in range(m + 1)],
                                  out=yo[:, m, (N_C + h) * HD:(N_C + h + 1) * HD]))
        soft = SoftmaxHeads(nc, ph, ident, units)
        zb, rb, ob = soft.lg_ps, soft.pT_ps, soft.o_ps
        with nc.Block() as block:
            @block.sync
            def _(sp):
                for m in range(MT):
                    sp.dma_start(pr[:, m, :], proj.rearrange("(m p) n -> p m n", p=P)[:, m, 0:ODD_MIX]).then_inc(x_in, 16)
                sp.dma_start(bf[:, :], bcast_rows(b_f)).then_inc(const_in, 16)
                sp.dma_start(causal[:, :, :], C["causal"].rearrange("(m p) n -> p m n", p=P)).then_inc(const_in, 16)
                for t, c in ((before, "before"), (upto, "upto"), (after, "after"), (ones, "ones"), (ident, "ident")):
                    sp.dma_start(t[:, :], C[c]).then_inc(const_in, 16)
                sp.dma_start(pick[:, :, :], C["pick"].rearrange("a (b c) -> a b c", b=N_D)).then_inc(const_in, 16)
                sp.wait_ge(soft.o_done, len(units))
                sp.wait_ge(oc_done, MT * N_C)
                sp.dma_start(y.rearrange("(m p) n -> p m n", p=P), yo[:, :, :]).then_inc(stored, 16)
                sp.wait_ge(stored, 16)

            @block.tensor
            def _(pe):
                pe.wait_ge(const_in, 128)
                turner.turn(pe, jobs)
                turner.all_copied(pe, len(jobs))
                pe.wait_ge(ready, 1)
                nc.tensor.matmul(rb[0][:, 0, 0:N_D], upto[:, :], lf[:, 0, :], start=True, stop=True)
                nc.tensor.matmul(rb[0][:, 1, 0:N_D], ones[:, :], lf[:, 0, :], start=True, stop=False)
                nc.tensor.matmul(rb[0][:, 1, 0:N_D], upto[:, :], lf[:, 1, :], start=False, stop=True).then_inc(cum_full, 1)
                pe.wait_ge(cum_done, 1)
                for m in range(MT):
                    last = nc.tensor.transpose(ob[0].tensor[0:N_D, m * P:(m + 1) * P], cum[:, m, :], ident[:, :])
                last.then_inc(cum_full, 1)
                pe.wait_ge(cum_done, 2)
                for i in range(N_C + 2):
                    h = i
                    if h < N_C:
                        q, k = qkT[:, h, :], qkT[:, N_C + h, :]
                        b = zb[h % 2].tensor
                        if h >= 2:
                            pe.wait_ge(z_copied, h - 1)
                        nc.tensor.matmul(b[:, 0:SEQ], k[:, 0:P], q, start=True, stop=True)
                        nc.tensor.matmul(b[:, SEQ:ZW], k[:, P:SEQ], q[:, P:SEQ], start=True, stop=True).then_inc(z_full, 1)
                    h = i - 1
                    if 0 <= h < N_C:
                        pe.wait_ge(l_done, h + 1)
                        b = rb[h % 2].tensor
                        if h >= 2:
                            pe.wait_ge(w_arg, h - 1)
                        l = ls[:, h % 2, :]
                        nc.tensor.matmul(b[:, 0:P], after[:, :], l[:, 0:P], start=True, stop=True)
                        nc.tensor.matmul(b[:, P:SEQ], after[:, :], l[:, P:SEQ], start=True, stop=False)
                        nc.tensor.matmul(b[:, P:SEQ], ones[:, :], l[:, SEQ:ZW], start=False, stop=True)
                        nc.tensor.matmul(b[:, SEQ:ZW], after[:, :], l[:, SEQ:ZW], start=True, stop=True).then_inc(r_full, 1)
                    h = i - 2
                    if 0 <= h < N_C:
                        pe.wait_ge(w_done, h + 1)
                        b = ob[h % 2].tensor
                        if h >= 2:
                            pe.wait_ge(oc_done, MT * (h - 1))
                        ww = w[:, h % 2, :]
                        v = [pr[:, j, C_VC + h * HD:C_VC + (h + 1) * HD] for j in range(MT)]
                        nc.tensor.matmul(b[:, 0:HD], ww[:, 0:P], v[0], start=True, stop=True)
                        nc.tensor.matmul(b[:, HD:2 * HD], ww[:, P:SEQ], v[0], start=True, stop=False)
                        nc.tensor.matmul(b[:, HD:2 * HD], ww[:, SEQ:ZW], v[1], start=False, stop=True).then_inc(oc_full, 1)
                pe.wait_ge(oc_done, MT * N_C)
                pe.wait_ge(w_arg, N_C)
                soft.tensor(pe)

            @block.scalar
            def _(act):
                A = nc.scalar.activation
                turner.copy(act, jobs)
                act.wait_ge(pre, 1)
                A(e1[:, :, :], lf[:, :, :], ACT.Abs).then_inc(abs_, 1)
                act.wait_ge(abs_, 1)
                A(e1[:, :, :], e1[:, :, :], ACT.Exp, scale=-1.0).then_inc(exp_, 1)
                act.wait_ge(exp_, 1)
                A(e1[:, :, :], e1[:, :, :], ACT.Ln, bias=1.0).then_inc(abs_, 1)
                for i in range(N_C + 1):
                    h = i
                    if h < N_C:
                        s = h % 2
                        act.wait_ge(z_full, h + 1)
                        act.wait_ge(z_copied, h + 1)
                        if h >= 2:
                            act.wait_ge(l_done, h - 1)
                        A(az[:, s, :], z[:, s, :], ACT.Abs).then_inc(l_abs, 1)
                        act.wait_ge(l_abs, h + 1)
                        A(ez[:, s, :], az[:, s, :], ACT.Exp, scale=-1.0).then_inc(l_exp, 1)
                        act.wait_ge(l_exp, h + 1)
                        A(ez[:, s, :], ez[:, s, :], ACT.Ln, bias=1.0).then_inc(l_ln, 1)
                    h = i - 1
                    if 0 <= h < N_C:
                        s = h % 2
                        act.wait_ge(w_arg, h + 1)
                        A(w[:, s, :], w[:, s, :], ACT.Exp).then_inc(w_exp, 1)
                soft.scalar(act)

            @block.vector
            def _(dve):
                st = Steps(dve, own_v)
                V = nc.vector
                dve.wait_ge(x_in, 16 * MT)
                dve.wait_ge(const_in, 128)
                for m in range(MT):
                    c = pr[:, m, C_QC:C_QC + N_C * HD]
                    V.tensor_scalar(c, c, SC, None, ALU.mult)
                    c = pr[:, m, C_QD:C_QD + N_D * HD]
                    st.tell(V.tensor_scalar(c, c, SC, None, ALU.mult), scaled)
                st.tell(V.tensor_tensor(lf[:, :, :], pr[:, :, C_FL:C_FL + N_D], bf[:, :].unsqueeze(1).broadcast_to([P, MT, N_D]), ALU.add), pre)
                dve.wait_ge(abs_, 2)
                st.tell(V.scalar_tensor_tensor(lf[:, :, :], lf[:, :, :], 0.0, e1[:, :, :], ALU.min, ALU.subtract), ready)
                dve.wait_ge(cum_full, 1)
                st.tell(V.tensor_copy(cum[:, :, :], rb[0][:, :, 0:N_D]), cum_done)
                dve.wait_ge(cum_full, 2)
                st.tell(V.tensor_scalar(ncT[:, :], ob[0].tensor[0:N_D, 0:SEQ], -1.0, None, ALU.mult), cum_done)
                for i in range(N_C + 3):
                    h = i
                    if h < N_C:
                        s = h % 2
                        dve.wait_ge(z_full, h + 1)
                        if h >= 2:
                            dve.wait_ge(w_exp, h - 1)
                        st.tell(V.tensor_copy(z[:, s, :], zb[s].tensor[:, 0:ZW]), z_copied)
                        if h >= 2:
                            dve.wait_ge(r_full, h - 1)
                        st.link(V.tensor_scalar(ls[:, s, :], z[:, s, :], -1.0, 0.0, ALU.mult, ALU.min))
                        dve.wait_ge(l_ln, h + 1)
                        st.link(V.tensor_tensor(ls[:, s, :], ls[:, s, :], ez[:, s, :], ALU.subtract))
                        d0, d1 = ls[:, s, 0:P], ls[:, s, SEQ:ZW]
                        V.tensor_tensor(d0, d0, before[:, :], ALU.mult)
                        st.tell(V.tensor_tensor(d1, d1, before[:, :], ALU.mult), l_done)
                    h = i - 1
                    if 0 <= h < N_C:
                        s = h % 2
                        dve.wait_ge(r_full, h + 1)
                        if h >= 2:
                            dve.wait_ge(oc_full, h - 1)
                        st.tell(V.tensor_tensor(w[:, s, :], rb[s].tensor[:, 0:ZW], z[:, s, :], ALU.add), w_arg)
                        dve.wait_ge(w_exp, h + 1)
                        d0, d1 = w[:, s, 0:P], w[:, s, SEQ:ZW]
                        V.tensor_tensor(d0, d0, before[:, :], ALU.mult)
                        st.tell(V.tensor_tensor(d1, d1, before[:, :], ALU.mult), w_done)
                    h = i - 2
                    if 0 <= h < N_C:
                        dve.wait_ge(oc_full, h + 1)
                        for m in range(MT):
                            st.tell(V.tensor_copy(yo[:, m, h * HD:(h + 1) * HD], ob[h % 2].tensor[:, m * HD:(m + 1) * HD]), oc_done)
                soft.vector(dve)


G_H, G_W = 8, 1024
R_H, R_D, R_W, R_LORA = 16, 64, 1024, 96
R_FEAT = 3 * R_W + 2 * R_LORA
S_W, S_G, S_C, S_N = 1024, 64, 16, 64
O_GZ = 3 * G_W
O_GB = O_GZ + G_W
O_GA = O_GB + G_H
O_RF = O_GA + G_H
O_RZ = O_RF + R_FEAT
O_SU = O_RZ + R_W
O_SZ = O_SU + S_W
O_GL = O_SZ + S_W
N_IN = O_GL + 3 * D
QUAD = 4
LEVELS = (2, 4, 8, 16, 32, 64)


class Inverter:

    def __init__(self, nc, ph, joins, banks):
        self.nc, self.joins = nc, joins
        self.xb, self.yb, self.tb = banks[0:2], banks[2:4], banks[4:6]
        self.x = ph.sb("inv_x", [P, 2, QUAD * P // 2])
        self.x_full, self.x_done, self.y_full, self.y_done, self.t_full, self.t_done = (ph.sem(s) for s in (
            "inv_x_full", "inv_x_done", "inv_y_full", "inv_y_done", "inv_t_full", "inv_t_done"))

    def tensor(self, pe, rnd, lT, m, mT, ident):
        nc, L, HW = self.nc, len(LEVELS), P // 2
        for l, b in enumerate(LEVELS):
            step = lambda i: (rnd * L + l) * 2 + i
            for i in range(2):
                n = step(i)
                if l:
                    pe.wait_ge(self.y_done, n - 1)
                for h in range(QUAD):
                    c = slice(h * P, (h + 1) * P)
                    even = m[i][:, c].rearrange("p (n two b) -> p n two b", two=2, b=b)[:, :, 0, :]
                    last = nc.tensor.matmul(self.xb[i][:, h * HW:(h + 1) * HW].rearrange("p (n b) -> p n b", b=b),
                                            lT[i][:, c], even, start=True, stop=True)
                last.then_inc(self.x_full, 1)
            for i in range(2):
                n = step(i)
                pe.wait_ge(self.x_done, n + 1)
                if l:
                    pe.wait_ge(self.t_done, n - 1)
                for h in range(QUAD):
                    hc = slice(h * HW, (h + 1) * HW)
                    last = nc.tensor.matmul(self.yb[i][:, hc], mT[i][:, h * P:(h + 1) * P], self.x[:, i, hc], start=True, stop=True)
                last.then_inc(self.y_full, 1)
            for i in range(2):
                pe.wait_ge(self.y_done, step(i) + 1)
                for h in range(QUAD):
                    c = slice(h * P, (h + 1) * P)
                    last = nc.tensor.transpose(self.tb[i][:, c], m[i][:, c], ident)
                last.then_inc(self.t_full, 1)

    def vector(self, dve, rnd, m):
        V, L, HW = self.nc.vector, len(LEVELS), P // 2
        for l, b in enumerate(LEVELS):
            for i in range(2):
                dve.wait_ge(self.x_full, (rnd * L + l) * 2 + i + 1)
                j = self.joins[:, l, :].unsqueeze(1).broadcast_to([P, QUAD, HW])
                V.tensor_tensor(self.x[:, i, :].rearrange("p (h s) -> p h s", h=QUAD),
                                self.xb[i][:, 0:QUAD * HW].rearrange("p (h s) -> p h s", h=QUAD), j, ALU.mult).then_inc(self.x_done, 1)
            for i in range(2):
                dve.wait_ge(self.y_full, (rnd * L + l) * 2 + i + 1)
                even = m[i].rearrange("p (n two b) -> p n two b", two=2, b=b)[:, :, 0, :]
                V.tensor_tensor(even, even, self.yb[i][:, 0:QUAD * HW].rearrange("p (n b) -> p n b", b=b),
                                ALU.subtract).then_inc(self.y_done, 1)

    def scalar(self, act, rnd, mT):
        for l in range(len(LEVELS)):
            for i in range(2):
                act.wait_ge(self.t_full, (rnd * len(LEVELS) + l) * 2 + i + 1)
                self.nc.scalar.copy(mT[i], self.tb[i]).then_inc(self.t_done, 1)

    def finished(self, eng, rnd):
        eng.wait_ge(self.t_done, 2 * len(LEVELS) * (rnd + 1))


def heads4(ap):
    return ap.rearrange("p (h s) -> p h s", h=QUAD)


def gdn(nc, name, C, proj, conv_w, a_log, dt_bias, norm_w, out):
    H, CH = G_H, MT
    NQ = H // QUAD
    with Phase(nc, name) as ph:
        NCT = 3 * G_W // P
        cwr = ph.sb("cwr", [4 * NCT, P])
        cw = ph.sb("cw", [P, 4, NCT])
        cv = ph.sb("cv", [P, 4, 2, SEQ])
        tmp = ph.sb("tmp", [P, G_W])
        qkv = ph.sb("qkv", [P, 3, MT, G_W])
        z = ph.sb("z", [P, MT, G_W])
        ba = ph.sb("ba", [P, MT, 2 * H])
        par = ph.sb("par", [P, 2 * H])
        nw = ph.sb("nw", [P, HD])
        ss = ph.sb("ss", [P, 2 * MT, H])
        rt = ph.sb("rt", [P, 2 * MT, H])
        beta = ph.sb("beta", [P, MT, H])
        g = ph.sb("g", [P, MT, H])
        gt = ph.sb("gt", [P, MT, H])
        gc = ph.sb("gc", [P, MT, H])
        eg = ph.sb("eg", [P, MT, H])
        kd = ph.sb("kd", [P, MT, H])
        gcT = ph.sb("gcT", [H, MT, P])
        ident = ph.sb("ident", [P, P])
        upto = ph.sb("upto", [P, P])
        ones = ph.sb("ones", [P, P])
        low = ph.sb("low", [P, P])
        upi = ph.sb("upi", [P, P])
        join1 = ph.sb("join1", [P, P])
        joins = ph.sb("joins", [P, len(LEVELS), P // 2])
        join1T = ph.sb("join1T", [P, P])
        pick = ph.sb("pick", [H, H, P])
        qT = ph.sb("qT", [P, H, SEQ])
        kT = ph.sb("kT", [P, H, SEQ])
        Q4 = QUAD * P
        el = ph.sb("el", [P, 2, Q4])
        eu = ph.sb("eu", [P, 2, Q4])
        L = ph.sb("L", [P, 2, Q4])
        LT = ph.sb("LT", [P, 2, Q4])
        AT = ph.sb("AT", [P, 2, Q4])
        M = ph.sb("M", [P, 2, Q4])
        MTt = ph.sb("MTt", [P, 2, Q4])
        S = ph.sb("S", [P, Q4])
        X = ph.sb("X", [P, Q4])
        vn = ph.sb("vn", [P, Q4])
        y = ph.sb("y", [P, MT, G_W])
        names = ("tap_in", "q_in", "k_in", "v_in", "z_in", "x_in", "const_in", "conv", "silu", "squared", "ssum", "root", "unit", "own_v",
                 "own_a", "g_in", "g_a", "g_ready", "gc_full", "gc_done", "gcT_full", "gcT_done", "gb_full", "diff",
                 "decay", "kk_full", "kq_full", "l_done", "lT_full", "lT_done", "at_done", "ks_full", "x_done",
                 "vn_full", "vn_done", "o_full", "o_done", "s_full", "s_done", "y_rt", "y_rt_a", "stored", "e_in",
                 "e_a", "first_tap", "cw_full", "cw_done", "flip_full", "back_full", "back_done", "zs", "y_ready")
        s = {n: ph.sem(n) for n in names}
        part_in = [s["q_in"], s["k_in"], s["v_in"]]
        bank = [ph.ps(f"bank{i}", [P, 512]) for i in range(6)]
        turner = Turner(nc, ph, ident)
        inv = Inverter(nc, ph, joins, bank)
        NU = NCT // 2
        IN_BANKS = 4
        jobs = []
        for m in range(MT):
            for src, dst in ((0, qT), (1, kT)):
                for a in range(0, H, 4):
                    jobs.append(([qkv[:, src, m, (a + i) * P:(a + i + 1) * P] for i in range(4)],
                                 dst[:, a:a + 4, m * P:(m + 1) * P], (s["unit"], 1)))
        CONSTS = ((upto, "upto"), (ones, "ones"), (low, "low"), (upi, "upi"), (join1, "join1"), (join1T, "join1T"))

        with nc.Block() as block:
            @block.sync
            def _(sp):
                sp.dma_start(ba[:, :, :], proj.rearrange("(m p) n -> p m n", p=P)[:, :, O_GB:O_GB + 2 * H]).then_inc(s["x_in"], 16)
                sp.dma_start(par[:, 0:H], bcast_rows(a_log)).then_inc(s["x_in"], 16)
                sp.dma_start(par[:, H:2 * H], bcast_rows(dt_bias)).then_inc(s["x_in"], 16)
                for p in range(3):
                    sp.dma_start(qkv[:, p, :, :], proj.rearrange("(m p) n -> p m n", p=P)[:, :, p * G_W:(p + 1) * G_W]).then_inc(part_in[p], 16)
                    if p == 0:
                        sp.dma_start(ident[:, :], C["ident"]).then_inc(s["tap_in"], 16)
                        sp.dma_start(cwr[:, :], conv_w.rearrange("j (c p) -> (j c) p", p=P)).then_inc(s["tap_in"], 16)
                sp.dma_start(nw[:, :], bcast_rows(norm_w)).then_inc(s["z_in"], 16)
                sp.dma_start(z[:, :, :], proj.rearrange("(m p) n -> p m n", p=P)[:, :, O_GZ:O_GZ + G_W]).then_inc(s["z_in"], 16)
                sp.wait_ge(s["y_ready"], 1)
                sp.dma_start(out.rearrange("(m p) n -> p m n", p=P), y[:, :, :]).then_inc(s["stored"], 16)
                sp.wait_ge(s["stored"], 16)

            @block.gpsimd
            def _(pool):
                for t, c in CONSTS:
                    pool.dma_start(t[:, :], C[c]).then_inc(s["const_in"], 16)
                pool.dma_start(joins[:, :, :], C["joins"].rearrange("p (a b) -> p a b", b=P // 2)).then_inc(s["const_in"], 16)
                pool.dma_start(pick[:, :, :], C["pick"].rearrange("a (b c) -> a b c", b=H)).then_inc(s["const_in"], 16)

            @block.scalar
            def _(act):
                A = nc.scalar.activation
                own = Steps(act, s["own_a"])
                act.wait_ge(s["g_in"], 1)
                own.link(A(gt[:, :, :], g[:, :, :], ACT.Abs))
                own.link(A(gt[:, :, :], gt[:, :, :], ACT.Exp, scale=-1.0))
                own.link(A(par[:, 0:H], par[:, 0:H], ACT.Exp))
                own.link(A(beta[:, :, :], ba[:, :, 0:H], ACT.Exp, scale=-1.0))
                own.tell(A(gt[:, :, :], gt[:, :, :], ACT.Ln, bias=1.0), s["g_a"])
                act.wait_ge(s["cw_done"], 1)
                for u in range(NU + 3):
                    if u < NU:
                        act.wait_ge(s["flip_full"], u + 1)
                        if u >= 4:
                            act.wait_ge(s["back_full"], u - 3)
                        for c in range(2):
                            A(cv[:, u % 4, c, :], bank[2 + u % IN_BANKS][:, c * SEQ:(c + 1) * SEQ], ACT.Copy,
                              scale=cw[:, 3, 2 * u + c:2 * u + c + 1]).then_inc(s["first_tap"], 1)
                    if 1 <= u < NU + 1:
                        act.wait_ge(s["conv"], u)
                        A(cv[:, (u - 1) % 4, :, :], cv[:, (u - 1) % 4, :, :], ACT.Silu).then_inc(s["silu"], 1)
                    if u >= 3:
                        v = u - 3
                        act.wait_ge(s["back_full"], v + 1)
                        p, c0 = v * 2 * P // G_W, v * 2 * P % G_W
                        nc.scalar.copy(qkv[:, p, :, c0:c0 + 2 * P], turner.bank[v % 2][:, :, :].rearrange("p (m c) t -> p m (c t)", m=MT)).then_inc(s["back_done"], 1)
                act.wait_ge(s["z_in"], 32)
                A(z[:, :, :], z[:, :, :], ACT.Silu).then_inc(s["zs"], 1)
                act.wait_ge(s["ssum"], 1)
                A(rt[:, :, :], ss[:, :, :], ACT.Sqrt).then_inc(s["root"], 1)
                act.wait_ge(s["e_in"], 1)
                own.link(A(eg[:, :, :], gc[:, :, :], ACT.Exp))
                A(kd[:, :, :], kd[:, :, :], ACT.Exp).then_inc(s["e_a"], 1)
                turner.copy(act, jobs)
                for q in range(NQ):
                    for m in range(MT):
                        n = q * MT + m
                        act.wait_ge(s["diff"], 2 * n + 1)
                        A(el[:, m, :], el[:, m, :], ACT.Exp).then_inc(s["decay"], 1)
                        act.wait_ge(s["diff"], 2 * n + 2)
                        A(eu[:, m, :], eu[:, m, :], ACT.Exp).then_inc(s["decay"], 1)
                    inv.scalar(act, q, [MTt[:, m, :] for m in range(MT)])
                act.wait_ge(s["y_rt"], 1)
                A(rt[:, 0:MT, :], ss[:, 0:MT, :], ACT.Sqrt).then_inc(s["y_rt_a"], 1)

            @block.tensor
            def _(pe):
                T = nc.tensor
                pe.wait_ge(s["tap_in"], 32)
                T.transpose(bank[1][:, 0:4 * NCT], cwr[:, :], ident[0:4 * NCT, 0:4 * NCT]).then_inc(s["cw_full"], 1)
                for u in range(NU + 2):
                    if u < NU:
                        pe.wait_ge(part_in[u * 2 * P // G_W], 16)
                        if u >= IN_BANKS:
                            pe.wait_ge(s["conv"], u - IN_BANKS + 1)
                        for c in range(2):
                            for m in range(MT):
                                ch = (2 * u + c) * P
                                last = T.transpose(bank[2 + u % IN_BANKS][:, c * SEQ + m * P:c * SEQ + (m + 1) * P],
                                                   qkv[:, ch // G_W, m, ch % G_W:ch % G_W + P], ident[:, :])
                        last.then_inc(s["flip_full"], 1)
                    if u >= 2:
                        v = u - 2
                        pe.wait_ge(s["silu"], v + 1)
                        if v >= 2:
                            pe.wait_ge(s["back_done"], v - 1)
                        for m in range(MT):
                            for c in range(2):
                                last = T.transpose(turner.bank[v % 2][:, m * 2 + c, :], cv[:, v % 4, c, m * P:(m + 1) * P], ident[:, :])
                        last.then_inc(s["back_full"], 1)
                pe.wait_ge(s["const_in"], 128)
                pe.wait_ge(s["g_ready"], 1)
                for m in range(MT):
                    T.matmul(bank[0][:, m * H:(m + 1) * H], upto[:, :], g[:, m, :], start=True, stop=True)
                    last = T.matmul(bank[0][:, (MT + m) * H:(MT + m + 1) * H], ones[:, :], g[:, m, :], start=True, stop=True)
                last.then_inc(s["gc_full"], 1)
                pe.wait_ge(s["gc_done"], 1)
                for m in range(MT):
                    last = T.transpose(bank[1][0:H, m * P:(m + 1) * P], gc[:, m, :], ident[:, :])
                last.then_inc(s["gcT_full"], 1)
                turner.turn(pe, jobs)
                turner.all_copied(pe, len(jobs))
                pe.wait_ge(s["gcT_done"], 1)
                for q in range(NQ):
                    for m in range(MT):
                        n = q * MT + m
                        c = slice(m * P, (m + 1) * P)
                        if n:
                            pe.wait_ge(s["diff"], 2 * n)
                        for h in range(QUAD):
                            last = T.matmul(bank[0][:, h * P:(h + 1) * P], pick[:, q * QUAD + h, :], gcT[:, m, :], start=True, stop=True)
                        last.then_inc(s["gb_full"], 1)
                        if q and m == 0:
                            inv.finished(pe, q - 1)
                            pe.wait_ge(s["o_done"], q * MT)
                            pe.wait_ge(s["s_done"], q)
                        if n:
                            pe.wait_ge(s["l_done"], n)
                            pe.wait_ge(s["at_done"], n)
                            pe.wait_ge(s["lT_done"], n)
                        for h in range(QUAD):
                            k = kT[:, q * QUAD + h, c]
                            last = T.matmul(bank[1][:, h * P:(h + 1) * P], k, k, start=True, stop=True)
                        last.then_inc(s["kk_full"], 1)
                        for h in range(QUAD):
                            last = T.matmul(bank[2][:, h * P:(h + 1) * P], kT[:, q * QUAD + h, c], qT[:, q * QUAD + h, c], start=True, stop=True)
                        last.then_inc(s["kq_full"], 1)
                        pe.wait_ge(s["l_done"], n + 1)
                        for h in range(QUAD):
                            last = T.transpose(bank[3][:, h * P:(h + 1) * P], L[:, m, h * P:(h + 1) * P], ident[:, :])
                        last.then_inc(s["lT_full"], 1)
                    pe.wait_ge(s["lT_done"], (q + 1) * MT)
                    pe.wait_ge(s["at_done"], (q + 1) * MT)
                    sets = [[t[:, m, :] for m in range(MT)] for t in (LT, M, MTt)]
                    inv.tensor(pe, q, *sets, ident[:, :])
                    inv.finished(pe, q)
                    for m in range(MT):
                        n = q * MT + m
                        c = slice(m * P, (m + 1) * P)
                        if m:
                            pe.wait_ge(s["s_done"], q + 1)
                            for h in range(QUAD):
                                last = T.matmul(bank[0][:, h * P:(h + 1) * P], kT[:, q * QUAD + h, c], S[:, h * P:(h + 1) * P], start=True, stop=True)
                            last.then_inc(s["ks_full"], 1)
                        pe.wait_ge(s["x_done"], n + 1)
                        for h in range(QUAD):
                            hc = slice(h * P, (h + 1) * P)
                            last = T.matmul(bank[1][:, hc], MTt[:, m, hc], X[:, hc], start=True, stop=True)
                        last.then_inc(s["vn_full"], 1)
                        pe.wait_ge(s["vn_done"], n + 1)
                        if m == 0:
                            for h in range(QUAD):
                                hc = slice(h * P, (h + 1) * P)
                                last = T.matmul(bank[2][:, hc], qkv[:, 1, m, (q * QUAD + h) * P:(q * QUAD + h + 1) * P], vn[:, hc], start=True, stop=True)
                            last.then_inc(s["s_full"], 1)
                        else:
                            for h in range(QUAD):
                                hc = slice(h * P, (h + 1) * P)
                                T.matmul(bank[3][:, hc], qT[:, q * QUAD + h, c], S[:, hc], start=True, stop=True)
                        for h in range(QUAD):
                            hc = slice(h * P, (h + 1) * P)
                            last = T.matmul(bank[4][:, hc], AT[:, m, hc], vn[:, hc], start=True, stop=True)
                        last.then_inc(s["o_full"], 1)

            @block.vector
            def _(dve):
                V = nc.vector
                st = Steps(dve, s["own_v"])
                W = G_W
                dve.wait_ge(s["x_in"], 48)
                dt = par[:, H:2 * H].unsqueeze(1).broadcast_to([P, MT, H])
                ea = par[:, 0:H].unsqueeze(1).broadcast_to([P, MT, H])
                st.tell(V.tensor_tensor(g[:, :, :], ba[:, :, H:2 * H], dt, ALU.add), s["g_in"])
                dve.wait_ge(s["cw_full"], 1)
                st.tell(V.tensor_copy(cw[:, :, :], bank[1][:, 0:4 * NCT].rearrange("p (j c) -> p j c", j=4)), s["cw_done"])
                for u in range(NU):
                    dve.wait_ge(s["first_tap"], 2 * u + 2)
                    for back in range(1, 4):
                        for c in range(2):
                            o = cv[:, u % 4, c, back:SEQ]
                            last = V.scalar_tensor_tensor(o, bank[2 + u % IN_BANKS][:, c * SEQ:(c + 1) * SEQ - back],
                                                          cw[:, 3 - back, 2 * u + c:2 * u + c + 1], o, ALU.mult, ALU.add)
                            if back == 3 and c == 1:
                                st.tell(last, s["conv"], wait=False)
                            elif c == 1:
                                st.link(last)
                dve.wait_ge(s["g_a"], 1)
                st.link(V.scalar_tensor_tensor(g[:, :, :], g[:, :, :], 0.0, gt[:, :, :], ALU.max, ALU.add))
                st.tell(V.scalar_tensor_tensor(g[:, :, :], g[:, :, :], -1.0, ea, ALU.mult, ALU.mult), s["g_ready"])
                st.link(V.tensor_scalar(beta[:, :, :], beta[:, :, :], 1.0, None, ALU.add))
                st.link(V.reciprocal(beta[:, :, :], beta[:, :, :]))
                dve.wait_ge(s["gc_full"], 1)
                st.tell(V.tensor_copy(gc[:, :, :], bank[0][:, 0:MT * H].rearrange("p (m h) -> p m h", m=MT)), s["gc_done"])
                st.tell(V.tensor_tensor(kd[:, :, :], bank[0][:, MT * H:2 * MT * H].rearrange("p (m h) -> p m h", m=MT), gc[:, :, :], ALU.subtract), s["e_in"])
                dve.wait_ge(s["gcT_full"], 1)
                st.tell(V.tensor_copy(gcT[:, :, :], bank[1][0:H, 0:SEQ].rearrange("p (m t) -> p m t", m=MT)), s["gcT_done"])
                for p in range(2):
                    dve.wait_ge(s["back_done"], NU // 3 * (p + 1))
                    for m in range(MT):
                        c = qkv[:, p, m, :]
                        st.link(V.tensor_tensor(tmp[:, :], c, c, ALU.mult))
                        st.link(V.tensor_reduce(ss[:, 2 * m + p, :], tmp[:, :].rearrange("p (h d) -> p h d", h=H), AX_X, ALU.add))
                st.tell(V.tensor_scalar(ss[:, :, :], ss[:, :, :], 1e-6, None, ALU.add), s["ssum"])
                dve.wait_ge(s["root"], 1)
                st.link(V.reciprocal(rt[:, :, :], rt[:, :, :]))
                for m in range(MT):
                    r = rt[:, 2 * m, :]
                    st.link(V.tensor_scalar(r, r, float(HD) ** -0.5, None, ALU.mult))
                    for p in range(2):
                        c = qkv[:, p, m, :].rearrange("p (h d) -> p h d", h=H)
                        last = V.tensor_tensor(c, c, rt[:, 2 * m + p, :].unsqueeze(2).broadcast_to([P, H, HD]), ALU.mult)
                        st.link(last)
                dve.sem_inc(s["unit"], 1)
                dve.wait_ge(s["back_done"], NU)
                turner.all_copied(dve, len(jobs))
                dve.wait_ge(s["e_a"], 1)
                dve.wait_ge(s["const_in"], 128)
                c = qkv[:, 1, 0, :].rearrange("p (h d) -> p h d", h=H)
                st.link(V.tensor_tensor(c, c, kd[:, 0, :].unsqueeze(2).broadcast_to([P, H, HD]), ALU.mult))
                for q in range(NQ):
                    hs = slice(q * QUAD, (q + 1) * QUAD)
                    for m in range(MT):
                        n = q * MT + m
                        col = gc[:, m, hs].unsqueeze(2).broadcast_to([P, QUAD, P])
                        lo, up, lm, am = heads4(el[:, m, :]), heads4(eu[:, m, :]), heads4(L[:, m, :]), heads4(AT[:, m, :])
                        bc = lambda t: t.unsqueeze(1).broadcast_to([P, QUAD, P])
                        dve.wait_ge(s["gb_full"], n + 1)
                        b0 = heads4(bank[0])
                        st.link(V.tensor_tensor(lo, col, b0, ALU.subtract))
                        st.link(V.tensor_tensor(up, b0, col, ALU.subtract))
                        st.tell(V.tensor_tensor(lo, lo, bc(low[:, :]), ALU.add), s["diff"])
                        st.tell(V.tensor_tensor(up, up, bc(upi[:, :]), ALU.add), s["diff"])
                        dve.wait_ge(s["decay"], 2 * n + 1)
                        st.link(V.tensor_tensor(lo, lo, beta[:, m, hs].unsqueeze(2).broadcast_to([P, QUAD, P]), ALU.mult))
                        dve.wait_ge(s["kk_full"], n + 1)
                        if q:
                            inv.finished(dve, q - 1)
                        st.tell(V.tensor_tensor(lm, heads4(bank[1]), lo, ALU.mult), s["l_done"])
                        dve.wait_ge(s["decay"], 2 * n + 2)
                        dve.wait_ge(s["kq_full"], n + 1)
                        st.tell(V.tensor_tensor(am, heads4(bank[2]), up, ALU.mult), s["at_done"])
                        mm, mt, lt = heads4(M[:, m, :]), heads4(MTt[:, m, :]), heads4(LT[:, m, :])
                        st.link(V.tensor_tensor(mm, lm, bc(join1[:, :]), ALU.mult))
                        st.link(V.tensor_tensor(mm, bc(ident[:, :]), mm, ALU.subtract))
                        dve.wait_ge(s["lT_full"], n + 1)
                        st.link(V.tensor_copy(lt, heads4(bank[3])))
                        st.link(V.tensor_tensor(mt, lt, bc(join1T[:, :]), ALU.mult))
                        st.tell(V.tensor_tensor(mt, bc(ident[:, :]), mt, ALU.subtract), s["lT_done"])
                    inv.vector(dve, q, [M[:, m, :] for m in range(MT)])
                    inv.finished(dve, q)
                    for m in range(MT):
                        n = q * MT + m
                        hb = lambda t: t[:, m, hs].unsqueeze(2).broadcast_to([P, QUAD, HD])
                        v = heads4(qkv[:, 2, m, q * QUAD * HD:(q + 1) * QUAD * HD])
                        x = heads4(X[:, :])
                        if m:
                            dve.wait_ge(s["ks_full"], q + 1)
                            st.link(V.tensor_tensor(x, heads4(bank[0]), hb(eg), ALU.mult))
                            st.link(V.tensor_tensor(x, v, x, ALU.subtract))
                            st.tell(V.tensor_tensor(x, x, hb(beta), ALU.mult), s["x_done"])
                        else:
                            st.tell(V.tensor_tensor(x, v, hb(beta), ALU.mult), s["x_done"])
                        dve.wait_ge(s["vn_full"], n + 1)
                        if n:
                            dve.wait_ge(s["o_full"], n)
                        st.tell(V.tensor_copy(vn[:, :], bank[1]), s["vn_done"])
                        yy = heads4(y[:, m, q * QUAD * HD:(q + 1) * QUAD * HD])
                        if m == 0:
                            dve.wait_ge(s["s_full"], q + 1)
                            st.tell(V.tensor_copy(S[:, :], bank[2]), s["s_done"])
                            dve.wait_ge(s["o_full"], n + 1)
                            st.tell(V.tensor_copy(yy, heads4(bank[4])), s["o_done"])
                        else:
                            dve.wait_ge(s["o_full"], n + 1)
                            st.link(V.tensor_tensor(x, heads4(bank[3]), hb(eg), ALU.mult))
                            st.tell(V.tensor_tensor(yy, x, heads4(bank[4]), ALU.add), s["o_done"])
                for m in range(MT):
                    st.link(V.tensor_tensor(tmp[:, :], y[:, m, :], y[:, m, :], ALU.mult))
                    st.link(V.tensor_reduce(ss[:, m, :], tmp[:, :].rearrange("p (h d) -> p h d", h=H), AX_X, ALU.add))
                st.tell(V.tensor_scalar(ss[:, 0:MT, :], ss[:, 0:MT, :], 1.0 / HD, EPS, ALU.mult, ALU.add), s["y_rt"])
                dve.wait_ge(s["y_rt_a"], 1)
                st.link(V.reciprocal(rt[:, 0:MT, :], rt[:, 0:MT, :]))
                dve.wait_ge(s["zs"], 1)
                dve.wait_ge(s["z_in"], 32)
                for m in range(MT):
                    yv = y[:, m, :].rearrange("p (h d) -> p h d", h=H)
                    st.link(V.tensor_tensor(yv, yv, rt[:, m, :].unsqueeze(2).broadcast_to([P, H, HD]), ALU.mult))
                    st.link(V.tensor_tensor(yv, yv, nw[:, :].unsqueeze(1).broadcast_to([P, H, HD]), ALU.mult))
                    st.link(V.tensor_tensor(y[:, m, :], y[:, m, :], z[:, m, :], ALU.mult))
                dve.sem_inc(s["y_ready"], 1)


def rwkv_prepare(nc, name, C, proj, mu, w0, w_up, a0, a_up, k_k, k_a, r_k, al, be, ka, rh, vv, bonus, carry):
    NF = R_FEAT
    W = R_W
    HB = [(0, 512), (512, 1024)]
    with Phase(nc, name) as ph:
        ft = ph.sb("ft", [P, MT, NF])
        pv = ph.sb("pv", [P, MT, NF])
        mub = ph.sb("mub", [P, NF])
        prm = ph.sb("prm", [P, 5, W])
        ups = ph.sb("ups", [R_LORA, 2, W])
        ident = ph.sb("ident", [P, P])
        mid_in = ph.sb("mid_in", [P, P])
        mid_ex = ph.sb("mid_ex", [P, P])
        half = ph.sb("half", [P, 1])
        lw = ph.sb("lw", [P, MT, W])
        a = ph.sb("a", [P, W])
        kk = ph.sb("kk", [P, W])
        t1 = ph.sb("t1", [P, W])
        t2 = ph.sb("t2", [P, W])
        ei = ph.sb("ei", [P, W])
        ni = ph.sb("ni", [P, W])
        ee = ph.sb("ee", [P, W])
        outs = ph.sb("outs", [P, 5, W])
        lT = ph.sb("lT", [R_LORA, MT, 2, P])
        ss = ph.sb("ss", [P, R_H])
        rt = ph.sb("rt", [P, R_H])
        cr = ph.sb("cr", [P, W // P])
        names = ("x_in", "const_in", "zeroed", "mixed_r", "mixed", "tanh", "pre_full", "w_pre", "a_pre", "w_sig",
                 "a_sig", "lw_ready", "c_full", "c_read", "cr_full", "cr_done", "sumsq", "root", "own_v", "own_a",
                 "outs_ready", "stored", "v_stored", "own_p")
        s = {n: ph.sem(n) for n in names}
        bank = [ph.ps(f"bank{i}", [P, 512]) for i in range(6)]
        turner = Turner(nc, ph, ident)
        jobs = [([ft[:, m, 3 * W:3 * W + R_LORA], ft[:, m, 3 * W + R_LORA:NF]], lT[:, m, :, :], (s["tanh"], m + 1))
                for m in range(MT)]
        PR = proj[:, O_RF:O_RF + NF]
        with nc.Block() as block:
            @block.sync
            def _(sp):
                sp.dma_start(ft[:, :, :], PR.rearrange("(m p) n -> p m n", p=P)).then_inc(s["x_in"], 16)
                sp.dma_start(pv[1:P, 0, :], PR[0:P - 1, :]).then_inc(s["x_in"], 16)
                sp.dma_start(pv[:, 1, :], PR[P - 1:SEQ - 1, :]).then_inc(s["x_in"], 16)
                sp.dma_start(mub[:, :], bcast_rows(mu)).then_inc(s["x_in"], 16)
                for t, c in ((ident, "ident"), (mid_in, "mid_in"), (mid_ex, "mid_ex"), (half, "half")):
                    sp.dma_start(t[:, :], C[c]).then_inc(s["const_in"], 16)
                for i, w in enumerate((w0, a0, k_k, k_a, r_k)):
                    sp.dma_start(prm[:, i, :], bcast_rows(w)).then_inc(s["const_in"], 16)
                sp.dma_start(ups[:, 0, :], w_up).then_inc(s["const_in"], 16)
                sp.dma_start(ups[:, 1, :], a_up).then_inc(s["const_in"], 16)
                for m in range(MT):
                    sp.wait_ge(s["outs_ready"], m + 1)
                    for i, o in enumerate((al, be, ka, rh, bonus)):
                        sp.dma_start(o[m * P:(m + 1) * P, :], outs[:, i, :]).then_inc(s["stored"], 16)
                    sp.wait_ge(s["stored"], 80 * (m + 1))
                    sp.dma_start(vv[m * P:(m + 1) * P, :], ft[:, m, 2 * W:3 * W]).then_inc(s["v_stored"], 16)
                sp.wait_ge(s["cr_done"], 1)
                sp.dma_start(carry, cr[:, :]).then_inc(s["v_stored"], 16)
                sp.wait_ge(s["v_stored"], 48)

            @block.gpsimd
            def _(pool):
                G = nc.gpsimd
                st = Steps(pool, s["own_p"])
                G.memset(pv[0:1, 0, :], 0.0).then_inc(s["zeroed"], 1)
                pool.wait_ge(s["zeroed"], 1)
                pool.wait_ge(s["x_in"], 64)
                for m in range(MT):
                    f, p_ = ft[:, m, 0:W], pv[:, m, 0:W]
                    st.link(G.tensor_tensor(p_, p_, f, ALU.subtract))
                    st.link(G.tensor_tensor(p_, p_, mub[:, 0:W], ALU.mult))
                    st.tell(G.tensor_tensor(f, f, p_, ALU.add), s["mixed_r"])

            @block.scalar
            def _(act):
                A = nc.scalar.activation
                st = Steps(act, s["own_a"])
                for m in range(MT):
                    act.wait_ge(s["mixed"], m + 1)
                    w = ft[:, m, 3 * W:3 * W + R_LORA]
                    A(w, w, ACT.Tanh).then_inc(s["tanh"], 1)
                turner.copy(act, jobs)
                for m in range(MT):
                    act.wait_ge(s["w_pre"], m + 1)
                    A(lw[:, m, :], lw[:, m, :], ACT.Sigmoid).then_inc(s["w_sig"], 1)
                    act.wait_ge(s["a_pre"], m + 1)
                    A(a[:, :], a[:, :], ACT.Sigmoid).then_inc(s["a_sig"], 1)
                    act.wait_ge(s["sumsq"], m + 1)
                    A(rt[:, :], ss[:, :], ACT.Sqrt).then_inc(s["root"], 1)
                    act.wait_ge(s["c_full"], m + 1)
                    if m:
                        act.wait_ge(s["outs_ready"], m)
                    for i, (c0, c1) in enumerate(HB):
                        A(ei[:, c0:c1], bank[i], ACT.Exp)
                        A(ni[:, c0:c1], bank[i], ACT.Exp, scale=-1.0)
                        last = A(ee[:, c0:c1], bank[2 + i], ACT.Exp)
                    st.tell(last, s["c_read"])
                act.wait_ge(s["cr_full"], 1)
                A(cr[:, :], bank[4][:, 0:W // P], ACT.Exp).then_inc(s["cr_done"], 1)

            @block.tensor
            def _(pe):
                T = nc.tensor
                pe.wait_ge(s["const_in"], 16 * 11)
                turner.turn(pe, jobs)
                turner.all_copied(pe, len(jobs))
                for m in range(MT):
                    if m:
                        pe.wait_ge(s["c_read"], m)
                    for i, (c0, c1) in enumerate(HB):
                        T.matmul(bank[i], lT[:, m, 0, :], ups[:, 0, c0:c1], start=True, stop=True)
                        last = T.matmul(bank[2 + i], lT[:, m, 1, :], ups[:, 1, c0:c1], start=True, stop=True)
                    last.then_inc(s["pre_full"], 1)
                    pe.wait_ge(s["a_pre"], m + 1)
                    pe.wait_ge(s["lw_ready"], m + 1)
                    for i, (c0, c1) in enumerate(HB):
                        T.matmul(bank[i], mid_in[:, :], lw[:, m, c0:c1], start=True, stop=True)
                        last = T.matmul(bank[2 + i], mid_ex[:, :], lw[:, m, c0:c1], start=True, stop=True)
                    last.then_inc(s["c_full"], 1)
                for p_ in range(W // P):
                    for m in range(MT):
                        last = T.matmul(bank[4][:, p_:p_ + 1], lw[:, m, p_ * P:(p_ + 1) * P], half[:, :],
                                        start=(m == 0), stop=(m == MT - 1))
                last.then_inc(s["cr_full"], 1)

            @block.vector
            def _(dve):
                V = nc.vector
                st = Steps(dve, s["own_v"])
                dve.wait_ge(s["x_in"], 64)
                dve.wait_ge(s["zeroed"], 1)
                for m in range(MT):
                    f, p_ = ft[:, m, W:NF], pv[:, m, W:NF]
                    st.link(V.tensor_tensor(p_, p_, f, ALU.subtract))
                    st.link(V.tensor_tensor(p_, p_, mub[:, W:NF], ALU.mult))
                    st.tell(V.tensor_tensor(f, f, p_, ALU.add), s["mixed"])
                dve.wait_ge(s["const_in"], 16 * 11)
                byh = lambda t: t.rearrange("p (h d) -> p h d", h=R_H)
                each = lambda t: t.unsqueeze(2).broadcast_to([P, R_H, R_D])
                for m in range(MT):
                    r, k, v = (ft[:, m, i * W:(i + 1) * W] for i in range(3))
                    dve.wait_ge(s["pre_full"], m + 1)
                    for i, (c0, c1) in enumerate(HB):
                        last = V.tensor_tensor(lw[:, m, c0:c1], bank[i], prm[:, 0, c0:c1], ALU.add)
                    st.tell(last, s["w_pre"])
                    for i, (c0, c1) in enumerate(HB):
                        last = V.tensor_tensor(a[:, c0:c1], bank[2 + i], prm[:, 1, c0:c1], ALU.add)
                    st.tell(last, s["a_pre"])
                    dve.wait_ge(s["w_sig"], m + 1)
                    st.tell(V.tensor_scalar(lw[:, m, :], lw[:, m, :], -float(np.exp(-0.5)), None, ALU.mult), s["lw_ready"])
                    st.link(V.tensor_tensor(kk[:, :], k, prm[:, 2, :], ALU.mult))
                    st.link(V.tensor_tensor(t1[:, :], kk[:, :], kk[:, :], ALU.mult))
                    st.link(V.tensor_reduce(ss[:, :], byh(t1[:, :]), AX_X, ALU.add))
                    st.tell(V.tensor_scalar(ss[:, :], ss[:, :], 1e-6, None, ALU.add), s["sumsq"])
                    dve.wait_ge(s["a_sig"], m + 1)
                    st.link(V.scalar_tensor_tensor(t1[:, :], a[:, :], 1.0, prm[:, 3, :], ALU.subtract, ALU.mult))
                    st.link(V.scalar_tensor_tensor(k, t1[:, :], 1.0, k, ALU.add, ALU.mult))
                    dve.wait_ge(s["root"], m + 1)
                    st.link(V.reciprocal(rt[:, :], rt[:, :]))
                    st.link(V.tensor_tensor(byh(kk[:, :]), byh(kk[:, :]), each(rt[:, :]), ALU.mult))
                    st.link(V.tensor_tensor(t1[:, :], kk[:, :], a[:, :], ALU.mult))
                    dve.wait_ge(s["mixed_r"], m + 1)
                    if m:
                        dve.wait_ge(s["stored"], 80 * m)
                    st.link(V.tensor_tensor(t2[:, :], r, k, ALU.mult))
                    st.link(V.tensor_tensor(t2[:, :], t2[:, :], prm[:, 4, :], ALU.mult))
                    st.link(V.tensor_reduce(ss[:, :], byh(t2[:, :]), AX_X, ALU.add))
                    st.link(V.tensor_tensor(byh(outs[:, 4, :]), byh(v), each(ss[:, :]), ALU.mult))
                    dve.wait_ge(s["c_read"], m + 1)
                    V.tensor_tensor(outs[:, 0, :], kk[:, :], ee[:, :], ALU.mult)
                    V.tensor_tensor(outs[:, 1, :], t1[:, :], ni[:, :], ALU.mult)
                    V.tensor_tensor(outs[:, 2, :], k, ni[:, :], ALU.mult)
                    st.tell(V.tensor_tensor(outs[:, 3, :], r, ei[:, :], ALU.mult), s["outs_ready"])


def rwkv(nc, name, C, proj, al, be, ka, rh, vv, bonus, carry, lnx_w, lnx_b, out):
    W, CH = R_W, MT
    NQ = R_H // QUAD
    Q4 = QUAD * P
    VC = QUAD * R_D
    with Phase(nc, name) as ph:
        tok = {n: ph.sb(n, [P, MT, W]) for n in ("be", "ka", "vv")}
        src = ph.sb("src", [P, 2, W])
        tT = {n: ph.sb(n + "T", [P, W // P, SEQ]) for n in ("al", "be", "ka", "rh")}
        z = ph.sb("z", [P, MT, W])
        bn = ph.sb("bn", [P, MT, W])
        lnw = ph.sb("lnw", [P, 2, W])
        cr = ph.sb("cr", [P, W // P])
        ident = ph.sb("ident", [P, P])
        low1 = ph.sb("low1", [P, P])
        up1 = ph.sb("up1", [P, P])
        upi1 = ph.sb("upi1", [P, P])
        join1 = ph.sb("join1", [P, P])
        joins = ph.sb("joins", [P, len(LEVELS), P // 2])
        join1T = ph.sb("join1T", [P, P])
        NT = ph.sb("NT", [P, 2, Q4])
        PT = ph.sb("PT", [P, 2, Q4])
        QT = ph.sb("QT", [P, 2, Q4])
        RT = ph.sb("RT", [P, 2, Q4])
        M = ph.sb("M", [P, 2, Q4])
        MTt = ph.sb("MTt", [P, 2, Q4])
        Hs = ph.sb("Hs", [P, QUAD // 2, P])
        X = ph.sb("X", [P, VC])
        nS = ph.sb("nS", [P, VC])
        y = ph.sb("y", [P, MT, W])
        sm = ph.sb("sm", [P, 2, R_H])
        rt = ph.sb("rt", [P, R_H])
        names = ("x_in", "src_in", "const_in", "turned", "n_full", "t_full", "m_done", "mT_done", "nT_done", "r_done", "p_done",
                 "q_done", "x_full", "x_done", "s_full", "s_done", "y_full", "y_done", "h_full", "h_done", "own_v",
                 "var", "root", "zs", "y_ready", "stored")
        s = {n: ph.sem(n) for n in names}
        bank = [ph.ps(f"bank{i}", [P, 512]) for i in range(6)]
        turner = Turner(nc, ph, ident)
        inv = Inverter(nc, ph, joins, bank)
        jobs = []
        for m in range(MT):
            for n, t, ready in (("be", tok["be"][:, m, :], None), ("ka", tok["ka"][:, m, :], None),
                                ("al", src[:, 0, :], (s["src_in"], 32 * (m + 1))), ("rh", src[:, 1, :], None)):
                for g in range(0, W // P, 4):
                    jobs.append(([t[:, (g + i) * P:(g + i + 1) * P] for i in range(4)],
                                 tT[n][:, g:g + 4, m * P:(m + 1) * P], ready))
        CONSTS = ((ident, "ident"), (low1, "low1"), (up1, "before"), (upi1, "upto"), (join1, "join1"), (join1T, "join1T"))
        row = lambda e: slice(e * R_D, (e + 1) * R_D)

        with nc.Block() as block:
            @block.sync
            def _(sp):
                for t, c in CONSTS:
                    sp.dma_start(t[:, :], C[c]).then_inc(s["const_in"], 16)
                sp.dma_start(joins[:, :, :], C["joins"].rearrange("p (a b) -> p a b", b=P // 2)).then_inc(s["const_in"], 16)
                for n, d in (("be", be), ("ka", ka), ("vv", vv)):
                    sp.dma_start(tok[n][:, :, :], d.rearrange("(m p) n -> p m n", p=P)).then_inc(s["x_in"], 16)
                sp.dma_start(cr[:, :], carry).then_inc(s["x_in"], 16)
                sp.dma_start(bn[:, :, :], bonus.rearrange("(m p) n -> p m n", p=P)).then_inc(s["x_in"], 16)
                sp.dma_start(z[:, :, :], proj.rearrange("(m p) n -> p m n", p=P)[:, :, O_RZ:O_RZ + W]).then_inc(s["x_in"], 16)
                sp.dma_start(lnw[:, 0, :], bcast_rows(lnx_w)).then_inc(s["x_in"], 16)
                sp.dma_start(lnw[:, 1, :], bcast_rows(lnx_b)).then_inc(s["x_in"], 16)
                for m in range(MT):
                    if m:
                        sp.wait_ge(turner.turned, len(jobs) // MT)
                    sp.dma_start(src[:, 0, :], al[m * P:(m + 1) * P, :]).then_inc(s["src_in"], 16)
                    sp.dma_start(src[:, 1, :], rh[m * P:(m + 1) * P, :]).then_inc(s["src_in"], 16)
                sp.wait_ge(s["y_ready"], 1)
                sp.dma_start(out.rearrange("(m p) n -> p m n", p=P), y[:, :, :]).then_inc(s["stored"], 16)
                sp.wait_ge(s["stored"], 16)

            @block.scalar
            def _(act):
                A = nc.scalar.activation
                turner.copy(act, jobs)
                act.wait_ge(s["x_in"], 128)
                A(z[:, :, :], z[:, :, :], ACT.Silu).then_inc(s["zs"], 1)
                for q in range(NQ):
                    inv.scalar(act, q, [MTt[:, m, :] for m in range(MT)])
                for m in range(MT):
                    act.wait_ge(s["var"], m + 1)
                    A(rt[:, :], sm[:, 1, :], ACT.Sqrt).then_inc(s["root"], 1)

            @block.tensor
            def _(pe):
                T = nc.tensor
                pe.wait_ge(s["const_in"], 112)
                pe.wait_ge(s["x_in"], 128)
                turner.turn(pe, jobs)
                turner.all_copied(pe, len(jobs))
                for q in range(NQ):
                    def products(b, lhs, rhss, m):
                        for j, rhs in enumerate(rhss):
                            for g in range(QUAD // 2):
                                for e in range(2):
                                    pair = q * QUAD // 2 + g
                                    c = slice(m * P, (m + 1) * P)
                                    o = (2 * j + g) * P
                                    last = T.matmul(bank[b + e][:, o:o + P], tT[lhs][row(e), pair, c],
                                                    tT[rhs][row(e), pair, c], start=True, stop=True)
                        last.then_inc(s["n_full"], 1)
                    for m in range(MT):
                        n = q * MT + m
                        if m:
                            for d in ("m_done", "mT_done", "nT_done", "r_done", "p_done", "q_done"):
                                pe.wait_ge(s[d], n)
                        products(0, "al", ("be",), m)
                        products(2, "be", ("al", "rh"), m)
                        products(4, "ka", ("al", "rh"), m)
                    for d in ("m_done", "mT_done", "nT_done", "r_done", "p_done", "q_done"):
                        pe.wait_ge(s[d], (q + 1) * MT)
                    inv.tensor(pe, q, *[[t[:, m, :] for m in range(MT)] for t in (NT, M, MTt)], ident[:, :])
                    inv.finished(pe, q)
                    for m in range(MT):
                        n = q * MT + m
                        c = slice(m * P, (m + 1) * P)
                        vr = lambda h: slice(h * R_D, (h + 1) * R_D)
                        vq = lambda h: tok["vv"][:, m, (q * QUAD + h) * R_D:(q * QUAD + h + 1) * R_D]
                        if m:
                            pe.wait_ge(s["h_done"], q + 1)
                        def from_state(b, t, g):
                            T.matmul(bank[b][:, g * P:(g + 1) * P], tT[t][:, q * QUAD // 2 + g, c], Hs[:, g, :], start=True, stop=False)

                        for g in range(QUAD // 2):
                            if m:
                                from_state(0, "al", g)
                            for h in (2 * g, 2 * g + 1):
                                last = T.matmul(bank[0][:, vr(h)], PT[:, m, h * P:(h + 1) * P], vq(h), start=(m == 0), stop=(m == 0 or h % 2 == 1))
                        last.then_inc(s["x_full"], 1)
                        pe.wait_ge(s["x_done"], n + 1)
                        for h in range(QUAD):
                            last = T.matmul(bank[1][:, vr(h)], MTt[:, m, h * P:(h + 1) * P], X[:, vr(h)], start=True, stop=True)
                        last.then_inc(s["s_full"], 1)
                        pe.wait_ge(s["s_done"], n + 1)
                        for g in range(QUAD // 2):
                            if m:
                                from_state(2, "rh", g)
                            for h in (2 * g, 2 * g + 1):
                                hc = slice(h * P, (h + 1) * P)
                                T.matmul(bank[2][:, vr(h)], QT[:, m, hc], vq(h), start=(m == 0), stop=False)
                                last = T.matmul(bank[2][:, vr(h)], RT[:, m, hc], nS[:, vr(h)], start=False, stop=(m == 0 or h % 2 == 1))
                        last.then_inc(s["y_full"], 1)
                        if m == 0:
                            for g in range(QUAD // 2):
                                pair = q * QUAD // 2 + g
                                pc = slice(pair * P, (pair + 1) * P)
                                T.matmul(bank[3][:, g * P:(g + 1) * P], tok["ka"][:, m, pc], tok["vv"][:, m, pc], start=True, stop=False)
                                last = T.matmul(bank[3][:, g * P:(g + 1) * P], tok["be"][:, m, pc], nS[:, g * P:(g + 1) * P], start=False, stop=True)
                            last.then_inc(s["h_full"], 1)
                    pe.wait_ge(s["y_done"], (q + 1) * MT)

            @block.vector
            def _(dve):
                V = nc.vector
                st = Steps(dve, s["own_v"])
                dve.wait_ge(s["x_in"], 128)
                dve.wait_ge(s["const_in"], 112)
                bc = lambda t: t.unsqueeze(1).broadcast_to([P, QUAD, P])
                st.link(V.memset(Hs[:, :, :], 0.0))
                for q in range(NQ):
                    for m in range(MT):
                        n = q * MT + m
                        mm, mt = heads4(M[:, m, :]), heads4(MTt[:, m, :])
                        half = lambda b, j: bank[b][:, 2 * j * P:2 * (j + 1) * P].rearrange("p (h s) -> p h s", h=2)
                        two = lambda t: t.unsqueeze(1).broadcast_to([P, 2, P])
                        dve.wait_ge(s["n_full"], 3 * n + 1)
                        for e in range(2):
                            last = V.tensor_tensor(mm[:, e::2, :], half(e, 0), two(join1[:, :]), ALU.mult)
                        st.link(last)
                        st.tell(V.tensor_tensor(mm, bc(ident[:, :]), mm, ALU.subtract), s["m_done"])
                        for b, parts in ((2, ((NT, up1, "nT_done"), (RT, upi1, "r_done"))), (4, ((PT, up1, "p_done"), (QT, upi1, "q_done")))):
                            dve.wait_ge(s["n_full"], 3 * n + 1 + b // 2)
                            for j, (dst, mask, done) in enumerate(parts):
                                for e in range(2):
                                    last = V.tensor_tensor(heads4(dst[:, m, :])[:, e::2, :], half(b + e, j), two(mask[:, :]), ALU.mult)
                                st.tell(last, s[done])
                        st.link(V.tensor_tensor(mt, heads4(NT[:, m, :]), bc(join1T[:, :]), ALU.mult))
                        st.tell(V.tensor_tensor(mt, bc(ident[:, :]), mt, ALU.subtract), s["mT_done"])
                    inv.vector(dve, q, [M[:, m, :] for m in range(MT)])
                    for m in range(MT):
                        n = q * MT + m
                        dve.wait_ge(s["x_full"], n + 1)
                        st.tell(V.tensor_copy(X[:, :], bank[0][:, 0:VC]), s["x_done"])
                        dve.wait_ge(s["s_full"], n + 1)
                        st.tell(V.tensor_scalar(nS[:, :], bank[1][:, 0:VC], -1.0, None, ALU.mult), s["s_done"])
                        dve.wait_ge(s["y_full"], n + 1)
                        st.tell(V.tensor_copy(y[:, m, q * VC:(q + 1) * VC], bank[2][:, 0:VC]), s["y_done"])
                        if m == 0:
                            dve.wait_ge(s["h_full"], q + 1)
                            for g in range(QUAD // 2):
                                pair = q * QUAD // 2 + g
                                for e in range(2):
                                    st.link(V.tensor_scalar(Hs[row(e), g, row(e)], bank[3][row(e), g * P + e * R_D:g * P + (e + 1) * R_D],
                                                            cr[row(e), pair:pair + 1], None, ALU.mult))
                            dve.sem_inc(s["h_done"], 1)
                dve.wait_ge(s["zs"], 1)
                for m in range(MT):
                    byh = lambda t: t.rearrange("p (h d) -> p h d", h=R_H)
                    each = lambda t: t.unsqueeze(2).broadcast_to([P, R_H, R_D])
                    ym, sq = y[:, m, :], src[:, 0, :]
                    st.link(V.tensor_reduce(sm[:, 0, :], byh(ym), AX_X, ALU.add))
                    st.link(V.tensor_scalar(sm[:, 0, :], sm[:, 0, :], 1.0 / R_D, None, ALU.mult))
                    st.link(V.tensor_tensor(byh(ym), byh(ym), each(sm[:, 0, :]), ALU.subtract))
                    st.link(V.tensor_tensor(sq, ym, ym, ALU.mult))
                    st.link(V.tensor_reduce(sm[:, 1, :], byh(sq), AX_X, ALU.add))
                    st.tell(V.tensor_scalar(sm[:, 1, :], sm[:, 1, :], 1.0 / R_D, 64e-5, ALU.mult, ALU.add), s["var"])
                    dve.wait_ge(s["root"], m + 1)
                    st.link(V.reciprocal(rt[:, :], rt[:, :]))
                    st.link(V.tensor_tensor(byh(ym), byh(ym), each(rt[:, :]), ALU.mult))
                    st.link(V.tensor_tensor(ym, ym, lnw[:, 0, :], ALU.mult))
                    st.link(V.tensor_tensor(ym, ym, lnw[:, 1, :], ALU.add))
                    st.link(V.tensor_tensor(ym, ym, bn[:, m, :], ALU.add))
                    st.link(V.tensor_tensor(ym, ym, z[:, m, :], ALU.mult))
                dve.sem_inc(s["y_ready"], 1)


TWO_PI = 2.0 * np.pi
PI_1 = 6.28125
PI_2 = float(np.float32(TWO_PI - PI_1))
PI_3 = float(TWO_PI - PI_1 - PI_2)
ROUND = 1.5 * 2.0 ** 23


def s5_scan(nc, name, C, proj, a_re, a_im, log_dt, b_re, b_im, c_re, c_im, d, out):
    NJ = S_G // 2
    JJ = S_W // P
    PC = 2 * S_C
    with Phase(nc, name) as ph:
        are = ph.sb("are", [NJ, 2, S_N])
        aim = ph.sb("aim", [NJ, 2, S_N])
        ldt = ph.sb("ldt", [NJ, 2])
        prm = ph.sb("prm", [NJ, 5, P])
        w1 = ph.sb("w1", [NJ, P])
        w2 = ph.sb("w2", [NJ, P])
        w3 = ph.sb("w3", [NJ, P])
        w4 = ph.sb("w4", [NJ, P])
        par = ph.sb("par", [P, 5, NJ])
        pw = ph.sb("pw", [P, 2, NJ])
        pw2 = ph.sb("pw2", [P, 2, NJ])
        bre = ph.sb("bre", [P, NJ, S_C])
        bim = ph.sb("bim", [P, NJ, S_C])
        bt = ph.sb("bt", [P, 2, NJ, S_C])
        bp = ph.sb("bp", [P, 2, NJ, PC])
        BT = ph.sb("BT", [P, 2, JJ, P])
        cc = ph.sb("cc", [P, 2, JJ, S_N])
        cp = ph.sb("cp", [P, 3, JJ, P])
        CT = ph.sb("CT", [P, 3, JJ, P])
        parity = ph.sb("parity", [P, 4])
        ident = ph.sb("ident", [P, P])
        u = ph.sb("u", [P, MT, S_W])
        dd = ph.sb("dd", [P, S_W])
        uT = ph.sb("uT", [P, JJ, SEQ])
        tab = ph.sb("tab", [P, NJ, 2, SEQ])
        ta = ph.sb("ta", [P, 2, NJ * P // 4])
        tb = ph.sb("tb", [P, 2, NJ * P // 4])
        b = ph.sb("b", [P, 2, 2, SEQ])
        p1 = ph.sb("p1", [P, 2, SEQ])
        p2 = ph.sb("p2", [P, 2, 2, SEQ])
        v = ph.sb("v", [P, 2, SEQ])
        r = ph.sb("r", [P, 2, 2, SEQ])
        q1 = ph.sb("q1", [P, 2, 2, SEQ])
        q2 = ph.sb("q2", [P, 2, 2, SEQ])
        names = ("par_in", "x_in", "const_in", "own_v", "own_a", "own_p", "dt", "wdt", "mag", "angle", "sines", "prm_ready",
                 "bc_ready", "level", "table_v", "table_p", "bu_full", "b_ready", "p1_done", "p2_done", "r_ready",
                 "q1_done", "q2_done", "y_step", "y_pre", "y_out", "stored", "power")
        s = {n: ph.sem(n) for n in names}
        bu = [ph.ps(f"bu{i}", [P, 2, SEQ]) for i in range(2)]
        yb = [[ph.ps(f"y{m}{i}", [P, 512]) for i in range(2)] for m in range(MT)]
        turner = Turner(nc, ph, ident)
        jobs_u = [([u[:, m, (g + i) * P:(g + i + 1) * P] for i in range(4)], uT[:, g:g + 4, m * P:(m + 1) * P], None)
                  for m in range(MT) for g in range(0, JJ, 4)]
        jobs_p = [([prm[:, i, :] for i in g], par[:, g[0]:g[-1] + 1, :], (s["prm_ready"], 1)) for g in ((0, 1, 2, 3), (4,))]
        jobs_c = [([cp[:, k, g + i, :] for i in range(4)], CT[:, k, g:g + 4, :], (s["bc_ready"], 1)) for k in range(3) for g in range(0, JJ, 4)]
        flat = lambda k: bp[:, k, :, :].rearrange("p j c -> p (j c)")
        jobs_b = [([flat(k)[:, (g + i) * P:(g + i + 1) * P] for i in range(4)], BT[:, k, g:g + 4, :], (s["bc_ready"], 2)) for k in range(2) for g in range(0, JJ, 4)]
        early, late = jobs_u + jobs_p, jobs_c + jobs_b
        levels = [1, 2, 4, 8, 16, 32, 64, 128]
        swap = lambda t: t[:, ::-1, :]

        def double(eng, G, st, n, which, scratch_a, scratch_b):
            for h0 in range(0, NJ, NJ // 4 if n > 32 else NJ):
                h1 = h0 + (NJ // 4 if n > 32 else NJ)
                nj = h1 - h0
                A, B = (t[:, 0:nj * n].rearrange("p (j n) -> p j n", j=nj) for t in (scratch_a, scratch_b))
                co, si = (tab[:, h0:h1, k, 0:n] for k in range(2))
                pc, ps_ = (pw[:, k, h0:h1].unsqueeze(2).broadcast_to([P, nj, n]) for k in range(2))
                x, y_ = (co, si) if which == 0 else (si, co)
                st.link(G.tensor_tensor(A, x, pc, ALU.mult))
                st.link(G.tensor_tensor(B, y_, ps_, ALU.mult))
                st.link(G.tensor_tensor(tab[:, h0:h1, which, n:2 * n], A, B, ALU.subtract if which == 0 else ALU.add))

        with nc.Block() as block:
            @block.sync
            def _(sp):
                sp.dma_start(are[:, :, :], a_re.rearrange("(j e) n -> j e n", e=2)).then_inc(s["par_in"], 16)
                sp.dma_start(aim[:, :, :], a_im.rearrange("(j e) n -> j e n", e=2)).then_inc(s["par_in"], 16)
                sp.dma_start(ldt[:, :], log_dt.rearrange("(j e) -> j e", e=2)).then_inc(s["par_in"], 16)
                sp.dma_start(ident[:, :], C["ident"]).then_inc(s["const_in"], 16)
                sp.dma_start(u[:, :, :], proj.rearrange("(m p) n -> p m n", p=P)[:, :, O_SU:O_SU + S_W]).then_inc(s["const_in"], 16)
                sp.dma_start(parity[:, :], C["parity"]).then_inc(s["x_in"], 16)
                sp.dma_start(bre[:, :, :], b_re.rearrange("(j e) n c -> (e n) j c", e=2)).then_inc(s["x_in"], 16)
                sp.dma_start(bim[:, :, :], b_im.rearrange("(j e) n c -> (e n) j c", e=2)).then_inc(s["x_in"], 16)
                sp.dma_start(cc[:, 0, :, :], c_re.rearrange("(j r) c n -> (r c) j n", r=8)).then_inc(s["x_in"], 16)
                sp.dma_start(cc[:, 1, :, :], c_im.rearrange("(j r) c n -> (r c) j n", r=8)).then_inc(s["x_in"], 16)
                sp.dma_start(dd[:, :], bcast_rows(d)).then_inc(s["x_in"], 16)
                for m in range(MT):
                    sp.wait_ge(s["y_out"], m + 1)
                    sp.dma_start(out[m * P:(m + 1) * P, :], u[:, m, :]).then_inc(s["stored"], 16)
                sp.wait_ge(s["stored"], 16 * MT)

            @block.tensor
            def _(pe):
                T = nc.tensor
                pe.wait_ge(s["const_in"], 32)
                turner.turn(pe, early)
                turner.turn(pe, late)
                turner.all_copied(pe, len(early) + len(late))
                for i in range(NJ + 2):
                    j = i
                    if j < NJ:
                        if j >= 2:
                            pe.wait_ge(s["b_ready"], j - 1)
                        rw = slice((j % 4) * PC, (j % 4 + 1) * PC)
                        for k in range(2):
                            last = T.matmul(bu[j % 2][:, k, :], BT[rw, k, j // 4, :], uT[rw, j // 4, :], start=True, stop=True,
                                            tile_position=((j % 4) * PC, 0))
                        last.then_inc(s["bu_full"], 1)
                    j = i - 2
                    if j >= 0:
                        pe.wait_ge(s["q1_done"], j + 1)
                        pe.wait_ge(s["q2_done"], j + 1)
                        w = slice((j % 4) * PC, (j % 4 + 1) * PC)
                        for m in range(MT):
                            o = yb[m][j // 16][:, (j % 16) * PC:(j % 16 + 1) * PC]
                            terms = ((q1, 0, 0), (q1, 1, 1), (q2, 0, 2), (q2, 1, 2))
                            for k, (q, part, c) in enumerate(terms):
                                last = T.matmul(o, q[:, j % 2, part, m * P:(m + 1) * P], CT[:, c, j // 4, w],
                                                start=(k == 0), stop=(k == 3))
                        last.then_inc(s["y_step"], 1)

            @block.scalar
            def _(act):
                A = nc.scalar.activation
                act.wait_ge(s["par_in"], 48)
                A(ldt[:, :], ldt[:, :], ACT.Exp).then_inc(s["dt"], 1)
                act.wait_ge(s["wdt"], 1)
                A(prm[:, 0, :], w1[:, :], ACT.Exp).then_inc(s["mag"], 1)
                act.wait_ge(s["angle"], 1)
                A(prm[:, 2, :], w3[:, :], ACT.Sin).then_inc(s["sines"], 1)
                A(prm[:, 1, :], w4[:, :], ACT.Sin).then_inc(s["sines"], 1)
                turner.copy(act, early)
                turner.copy(act, late)
                for j in range(NJ):
                    act.wait_ge(s["bu_full"], j + 1)
                    if j >= 2:
                        act.wait_ge(s["p1_done"], j - 1)
                        act.wait_ge(s["p2_done"], j - 1)
                    nc.scalar.copy(b[:, j % 2, :, :], bu[j % 2]).then_inc(s["b_ready"], 1)
                for m in range(MT):
                    act.wait_ge(s["y_pre"], m + 1)
                    A(u[:, m, :], u[:, m, :], ACT.Gelu_apprx_tanh).then_inc(s["y_out"], 1)

            @block.gpsimd
            def _(pool):
                G = nc.gpsimd
                st = Steps(pool, s["own_p"])
                for i, n in enumerate(levels):
                    pool.wait_ge(s["level"], i + 1)
                    double(pool, G, st, n, 1, tb[:, 0, :], tb[:, 1, :])
                    pool.sem_inc(s["table_p"], 1)
                pool.wait_ge(s["table_v"], len(levels))
                for i in range(NJ + 1):
                    j = i
                    if j < NJ:
                        pool.wait_ge(s["b_ready"], j + 1)
                        if j >= 2:
                            pool.wait_ge(s["r_ready"], j - 1)
                        G.tensor_tensor(p2[:, j % 2, :, :], swap(b[:, j % 2, :, :]), tab[:, j, :, :], ALU.mult).then_inc(s["p2_done"], 1)
                    j = i - 1
                    if j >= 0:
                        pool.wait_ge(s["r_ready"], j + 1)
                        if j >= 2:
                            pool.wait_ge(s["y_step"], j - 1)
                        G.tensor_tensor(q2[:, j % 2, :, :], swap(r[:, j % 2, :, :]), tab[:, j, :, :], ALU.mult).then_inc(s["q2_done"], 1)

            @block.vector
            def _(dve):
                V = nc.vector
                st = Steps(dve, s["own_v"])
                L = st.link
                TT, TS = V.tensor_tensor, V.tensor_scalar
                two = lambda t: t.rearrange("j (e n) -> j e n", e=2)
                dtb = ldt[:, :].unsqueeze(2).broadcast_to([NJ, 2, S_N])
                dve.wait_ge(s["dt"], 1)
                st.tell(TT(two(w1[:, :]), are[:, :, :], dtb, ALU.mult), s["wdt"])
                L(TT(two(w2[:, :]), aim[:, :, :], dtb, ALU.mult))
                L(TS(w4[:, :], w2[:, :], 1.0 / TWO_PI, ROUND, ALU.mult, ALU.add))
                L(TS(w4[:, :], w4[:, :], -ROUND, None, ALU.add))
                L(V.scalar_tensor_tensor(w3[:, :], w4[:, :], -PI_1, w2[:, :], ALU.mult, ALU.add))
                L(V.scalar_tensor_tensor(w3[:, :], w4[:, :], -PI_2, w3[:, :], ALU.mult, ALU.add))
                L(V.scalar_tensor_tensor(w3[:, :], w4[:, :], -PI_3, w3[:, :], ALU.mult, ALU.add))
                L(TS(w3[:, :], w3[:, :], 3.1415925, -3.1415925, ALU.min, ALU.max))
                L(V.scalar_tensor_tensor(w4[:, :], w3[:, :], -1.0, w3[:, :], ALU.mult, ALU.max))
                st.tell(TS(w4[:, :], w4[:, :], -1.0, float(np.pi / 2), ALU.mult, ALU.add), s["angle"])
                dve.wait_ge(s["mag"], 1)
                dve.wait_ge(s["sines"], 2)
                ar, ai = are[:, :, :].rearrange("j e n -> j (e n)"), aim[:, :, :].rearrange("j e n -> j (e n)")
                x, y_, den, t = w1[:, :], w2[:, :], w3[:, :], w4[:, :]
                L(TT(x, prm[:, 0, :], prm[:, 1, :], ALU.mult))
                L(TS(x, x, -1.0, None, ALU.add))
                L(TT(y_, prm[:, 0, :], prm[:, 2, :], ALU.mult))
                L(TT(den, ar, ar, ALU.mult))
                L(TT(t, ai, ai, ALU.mult))
                L(TT(den, den, t, ALU.add))
                L(V.reciprocal(den, den))
                for k, (m1, m2, op) in enumerate(((ar, ai, ALU.add), (ai, ar, ALU.subtract))):
                    o = prm[:, 3 + k, :]
                    L(TT(t, x, m1, ALU.mult))
                    L(TT(o, y_, m2, ALU.mult))
                    L(TT(o, o, t, op))
                    last = TT(o, o, den, ALU.mult)
                    L(last)
                dve.sem_inc(s["prm_ready"], 1)
                dve.wait_ge(s["x_in"], 96)
                for k, (src, sign) in enumerate(((0, 0), (0, 2), (1, 2))):
                    for e in range(2):
                        last = TS(cp[:, k, :, e * S_N:(e + 1) * S_N], cc[:, src, :, :], parity[:, sign + e:sign + e + 1], None, ALU.mult)
                        L(last)
                dve.sem_inc(s["bc_ready"], 1)
                turner.all_copied(dve, len(early))
                cr, ci = (par[:, 3 + k, :].unsqueeze(2).broadcast_to([P, NJ, S_C]) for k in range(2))
                L(V.memset(bp[:, :, :, :], 0.0))
                for k, (m1, m2, op) in enumerate(((bre, bim, ALU.subtract), (bim, bre, ALU.add))):
                    L(TT(bt[:, 0, :, :], m1[:, :, :], cr, ALU.mult))
                    L(TT(bt[:, 1, :, :], m2[:, :, :], ci, ALU.mult))
                    for e in range(2):
                        rw = slice(e * S_N, (e + 1) * S_N)
                        L(TT(bp[rw, k, :, e * S_C:(e + 1) * S_C], bt[rw, 0, :, :], bt[rw, 1, :, :], op))
                dve.sem_inc(s["bc_ready"], 1)
                V.memset(tab[:, :, 0, 0:1], 1.0)
                V.memset(tab[:, :, 1, 0:1], 0.0)
                L(V.tensor_copy(pw[:, :, :], par[:, 1:3, :]))
                for i, n in enumerate(levels):
                    dve.sem_inc(s["level"], 1)
                    double(dve, V, st, n, 0, ta[:, 0, :], ta[:, 1, :])
                    dve.wait_ge(s["table_p"], i + 1)
                    if i < len(levels) - 1:
                        L(TT(pw2[:, :, :], pw[:, :, :], pw[:, :, :], ALU.mult))
                        L(TT(pw[:, 1, :], pw[:, 0, :], pw[:, 1, :], ALU.mult))
                        L(TS(pw[:, 1, :], pw[:, 1, :], 2.0, None, ALU.mult))
                        L(TT(pw[:, 0, :], pw2[:, 0, :], pw2[:, 1, :], ALU.subtract))
                    dve.sem_inc(s["table_v"], 1)
                for j in range(NJ):
                    mag = par[:, 0, j:j + 1].broadcast_to([P, SEQ])
                    o = r[:, j % 2, :, :]
                    dve.wait_ge(s["b_ready"], j + 1)
                    st.tell(TT(p1[:, :, :], b[:, j % 2, :, :], tab[:, j, :, :], ALU.mult), s["p1_done"])
                    L(TT(v[:, 0, :], p1[:, 0, :], p1[:, 1, :], ALU.add))
                    if j >= 2:
                        dve.wait_ge(s["q2_done"], j - 1)
                    L(V.tensor_tensor_scan(o[:, 0, :], mag, v[:, 0, :], 0.0, ALU.mult, ALU.add))
                    dve.wait_ge(s["p2_done"], j + 1)
                    L(TT(v[:, 1, :], p2[:, j % 2, 0, :], p2[:, j % 2, 1, :], ALU.subtract))
                    st.tell(V.tensor_tensor_scan(o[:, 1, :], mag, v[:, 1, :], 0.0, ALU.mult, ALU.add), s["r_ready"])
                    if j >= 2:
                        dve.wait_ge(s["y_step"], j - 1)
                    st.tell(TT(q1[:, j % 2, :, :], o, tab[:, j, :, :], ALU.mult), s["q1_done"])
                dve.wait_ge(s["y_step"], NJ)
                for m in range(MT):
                    L(TT(u[:, m, :], u[:, m, :], dd[:, :], ALU.mult))
                    for i in range(2):
                        c = u[:, m, i * 512:(i + 1) * 512]
                        last = TT(c, c, yb[m][i], ALU.add)
                        if i == 0:
                            L(last)
                    st.tell(last, s["y_pre"])


def s5_glu(nc, name, C, proj, yg, glu_w, glu_b, out):
    K = S_W
    KT, Q = K // P, 4
    KQ = KT // Q
    with Phase(nc, name) as ph:
        yt = ph.sb("yt", [P, MT, K])
        z = ph.sb("z", [P, MT, K])
        gb = ph.sb("gb", [P, K])
        w = ph.sb("w", [P, KT, K])
        ident = ph.sb("ident", [P, P])
        w_hi = ph.sb("w_hi", [P, KT, K], F32R)
        w_lo = ph.sb("w_lo", [P, KT, K], F32R)
        yT = (ph.sb("yT_hi", [P, KT, SEQ], F32R), ph.sb("yT_lo", [P, KT, SEQ], F32R))
        g = ph.sb("g", [P, MT, K])
        x_in, hi_done, lo_done, zs, full, biased, sig, own, done, stored = (ph.sem(x) for x in (
            "x_in", "hi_done", "lo_done", "zs", "full", "biased", "sig", "own", "done", "stored"))
        w_in = [ph.sem(f"w_in{q}") for q in range(Q)]
        bank = [[ph.ps(f"bank{m}{i}", [P, 512]) for i in range(2)] for m in range(MT)]
        turner = Turner(nc, ph, ident)
        jobs = [([yt[:, m, (a + i) * P:(a + i + 1) * P] for i in range(4)], tuple(t[:, a:a + 4, m * P:(m + 1) * P] for t in yT), None)
                for m in range(MT) for a in range(0, KT, 4)]
        order = [(i, m) for i in range(2) for m in range(MT)]
        with nc.Block() as block:
            @block.sync
            def _(sp):
                sp.dma_start(yt[:, :, :], yg.rearrange("(m p) n -> p m n", p=P)).then_inc(x_in, 16)
                sp.dma_start(ident[:, :], C["ident"]).then_inc(x_in, 16)
                sp.dma_start(z[:, :, :], proj.rearrange("(m p) n -> p m n", p=P)[:, :, O_SZ:O_SZ + S_W]).then_inc(x_in, 16)
                sp.dma_start(gb[:, :], bcast_rows(glu_b)).then_inc(x_in, 16)
                for q in range(Q):
                    ks = slice(q * KQ, (q + 1) * KQ)
                    sp.dma_start(w[:, ks, :], glu_w.rearrange("(k p) n -> p k n", p=P)[:, ks, :]).then_inc(w_in[q], 16)
                sp.wait_ge(done, 4)
                sp.dma_start(out.rearrange("(m p) n -> p m n", p=P), g[:, :, :]).then_inc(stored, 16)
                sp.wait_ge(stored, 16)

            @block.tensor
            def _(pe):
                pe.wait_ge(x_in, 64)
                turner.turn(pe, jobs)
                turner.all_copied(pe, len(jobs))
                for q in range(Q):
                    pe.wait_ge(lo_done, q + 1)
                    for i, m in order:
                        for k in range(q * KQ, (q + 1) * KQ):
                            for a, b, first, end in ((yT[0], w_hi, True, False), (yT[0], w_lo, False, False), (yT[1], w_hi, False, True)):
                                last = nc.tensor.matmul(bank[m][i], a[:, k, m * P:(m + 1) * P], b[:, k, i * 512:(i + 1) * 512],
                                                        start=(k == 0 and first), stop=(k == KT - 1 and end))
                        if q == Q - 1:
                            last.then_inc(full, 1)

            @block.scalar
            def _(act):
                act.wait_ge(x_in, 64)
                turner.copy_hi(act, jobs)
                for q in range(Q):
                    ks = slice(q * KQ, (q + 1) * KQ)
                    act.wait_ge(w_in[q], 16)
                    nc.scalar.copy(w_hi[:, ks, :], w[:, ks, :]).then_inc(hi_done, 1)
                nc.scalar.activation(z[:, :, :], z[:, :, :], ACT.Silu).then_inc(zs, 1)
                for n, (i, m) in enumerate(order):
                    act.wait_ge(biased, n + 1)
                    c = g[:, m, i * 512:(i + 1) * 512]
                    nc.scalar.activation(c, c, ACT.Sigmoid).then_inc(sig, 1)

            @block.vector
            def _(dve):
                st = Steps(dve, own)
                TT = nc.vector.tensor_tensor
                dve.wait_ge(x_in, 64)
                turner.copy_lo(dve, jobs)
                for q in range(Q):
                    ks = slice(q * KQ, (q + 1) * KQ)
                    dve.wait_ge(hi_done, q + 1)
                    TT(w_lo[:, ks, :], w[:, ks, :], w_hi[:, ks, :].bitcast(F32), ALU.subtract).then_inc(lo_done, 1)
                dve.wait_ge(zs, 1)
                st.link(TT(yt[:, :, :], yt[:, :, :], z[:, :, :], ALU.mult))
                for n in range(len(order) + 1):
                    if n < len(order):
                        i, m = order[n]
                        c = slice(i * 512, (i + 1) * 512)
                        dve.wait_ge(full, n + 1)
                        st.tell(TT(g[:, m, c], bank[m][i], gb[:, c], ALU.add), biased)
                    if n:
                        i, m = order[n - 1]
                        c = slice(i * 512, (i + 1) * 512)
                        dve.wait_ge(sig, n)
                        st.tell(TT(g[:, m, c], g[:, m, c], yt[:, m, c], ALU.mult), done)


def merge(nc, name, C, proj, branches, w_branch, gate_b, out):
    NBR, K = 3, 1024
    KT, TN, NS = K // P, 512, 3
    KH = KT // 2
    TILES = D // TN
    with Phase(nc, name) as ph:
        bt = ph.sb("bt", [P, 2, MT, K])
        aT = [tuple(ph.sb(f"bT{n}_{x}", [P, KT, SEQ], F32R) for x in ("hi", "lo")) for n in range(NBR)]
        raw = ph.sb("raw", [P, 2 * NBR, KH, TN])
        hi = ph.sb("hi", [P, NS, KH, TN], F32R)
        lo = ph.sb("lo", [P, NS, KH, TN], F32R)
        gt = [ph.sb(f"gt{n}", [P, MT, TN]) for n in range(NBR)]
        gb = [ph.sb(f"gb{n}", [P, TN]) for n in range(NBR)]
        mg = ph.sb("mg", [P, MT, TN])
        ident = ph.sb("ident", [P, P])
        const_in, own, merged, stored = (ph.sem(x) for x in ("const_in", "own", "merged", "stored"))
        b_in, acc_free, g_full, g_free, biased, sig = ([ph.sem(f"{x}{n}") for n in range(NBR)] for x in (
            "b_in", "acc_free", "g_full", "g_free", "biased", "sig"))
        raw_full = [ph.sem(f"raw_full{u}") for u in range(2 * NBR)]
        hi_done = [ph.sem(f"hi_done{x}") for x in range(NS)]
        lo_done = [ph.sem(f"lo_done{x}") for x in range(NS)]
        used = [ph.sem(f"used{x}") for x in range(NS)]
        acc = [[ph.ps(f"acc{n}{m}", [P, TN]) for m in range(MT)] for n in range(NBR)]
        turner = Turner(nc, ph, ident)
        per = MT * KT // 4
        jobs = [([bt[:, n % 2, m, (a + i) * P:(a + i + 1) * P] for i in range(4)],
                 tuple(t[:, a:a + 4, m * P:(m + 1) * P] for t in aT[n]), (b_in[n], 16))
                for n in range(NBR) for m in range(MT) for a in range(0, KT, 4)]
        projv = proj.rearrange("(m p) n -> p m n", p=P)
        uses = lambda c, u: c * 2 + u // NS

        with nc.Block() as block:
            def tiles(eng, prepare, gate):
                prepare(0, 0)
                with eng.Fori(0, TILES - 1) as c:
                    for n in range(NBR):
                        prepare(*((c, n + 1) if n + 1 < NBR else (c + 1, 0)))
                        gate(c, n)
                for n in range(NBR):
                    if n + 1 < NBR:
                        prepare(TILES - 1, n + 1)
                    gate(TILES - 1, n)

            @block.sync
            def _(sp):
                def load(c, n):
                    for h in range(2):
                        u = 2 * n + h
                        sp.wait_ge(lo_done[u % NS], uses(c, u) + 1)
                        sp.dma_start(raw[:, u, :, :], w_branch[n].rearrange("(k p) n -> p k n", p=P)[
                            :, h * KH:(h + 1) * KH, bass.ds(c * TN, TN)]).then_inc(raw_full[u], 16)
                sp.dma_start(ident[:, :], C["ident"]).then_inc(const_in, 16)
                for n in range(NBR):
                    if n == 2:
                        sp.wait_ge(turner.turned, per)
                    sp.dma_start(bt[:, n % 2, :, :], branches[n].rearrange("(m p) n -> p m n", p=P)).then_inc(b_in[n], 16)
                tiles(sp, load, lambda c, n: None)

            @block.gpsimd
            def _(pool):
                for n in range(NBR):
                    pool.sem_inc(g_free[n], 1)
                with pool.Fori(0, TILES) as c:
                    for n in range(NBR):
                        pool.wait_ge(g_free[n], c + 1)
                        pool.dma_start(gt[n][:, :, :], projv[:, :, bass.ds(c * TN + (O_GL + n * D), TN)]).then_inc(g_full[n], 16)
                        pool.dma_start(gb[n][:, :], bcast_rows(gate_b[n])[:, bass.ds(c * TN, TN)]).then_inc(g_full[n], 16)

            @block.tensor
            def _(pe):
                def products(c, n):
                    pe.wait_ge(acc_free[n], c + 1)
                    for h in range(2):
                        u = 2 * n + h
                        pe.wait_ge(lo_done[u % NS], uses(c, u) + 3)
                        for k in range(KH):
                            for m in range(MT):
                                for a, b, first, end in ((0, hi, True, False), (0, lo, False, False), (1, hi, False, True)):
                                    last = nc.tensor.matmul(acc[n][m], aT[n][a][:, h * KH + k, m * P:(m + 1) * P], b[:, u % NS, k, :],
                                                            start=(h == 0 and k == 0 and first),
                                                            stop=(h == 1 and k == KH - 1 and end))
                        last.then_inc(used[u % NS], 1)
                for x in used:
                    pe.sem_inc(x, 1)
                pe.wait_ge(const_in, 16)
                turner.turn(pe, jobs)
                turner.all_copied(pe, len(jobs))
                tiles(pe, products, lambda c, n: None)

            @block.scalar
            def _(act):
                def split(c, n):
                    for h in range(2):
                        u = 2 * n + h
                        act.wait_ge(raw_full[u], (c + 1) * 16)
                        act.wait_ge(used[u % NS], uses(c, u) + 1)
                        nc.scalar.copy(hi[:, u % NS, :, :], raw[:, u, :, :]).then_inc(hi_done[u % NS], 1)
                    act.wait_ge(biased[n], c + 1)
                    nc.scalar.activation(gt[n][:, :, :], gt[n][:, :, :], ACT.Sigmoid).then_inc(sig[n], 1)

                def store(c, n):
                    if n == NBR - 1:
                        act.wait_ge(merged, c + 1)
                        act.dma_start(out.rearrange("(m p) n -> p m n", p=P)[:, :, bass.ds(c * TN, TN)], mg[:, :, :]).then_inc(stored, 16)
                turner.copy_hi(act, jobs)
                act.sem_inc(stored, 16)
                tiles(act, split, store)
                act.wait_ge(stored, 16 * (TILES + 1))

            @block.vector
            def _(dve):
                TT = nc.vector.tensor_tensor

                def split(c, n):
                    dve.wait_ge(g_full[n], (c + 1) * 32)
                    TT(gt[n][:, :, :], gt[n][:, :, :], gb[n][:, :].unsqueeze(1).broadcast_to([P, MT, TN]), ALU.add).then_inc(biased[n], 1)
                    for h in range(2):
                        u = 2 * n + h
                        dve.wait_ge(hi_done[u % NS], uses(c, u) + 1)
                        TT(lo[:, u % NS, :, :], raw[:, u, :, :], hi[:, u % NS, :, :].bitcast(F32), ALU.subtract).then_inc(lo_done[u % NS], 1)

                def gate(c, n):
                    dve.wait_ge(sig[n], c + 1)
                    u = 2 * n + 1
                    dve.wait_ge(used[u % NS], uses(c, u) + 2)
                    if n == 0:
                        dve.wait_ge(stored, (c + 1) * 16)
                    dst = mg if n == 0 else gt[n]
                    for m in range(MT):
                        last = TT(dst[:, m, :], gt[n][:, m, :], acc[n][m], ALU.mult)
                    last.then_inc(own, 1)
                    dve.wait_ge(own, c * (2 * NBR - 1) + (1 if n == 0 else 2 * n))
                    dve.sem_inc(acc_free[n], 1)
                    if n:
                        TT(mg[:, :, :], mg[:, :, :], gt[n][:, :, :], ALU.add).then_inc(own, 1)
                        dve.wait_ge(own, c * (2 * NBR - 1) + 2 * n + 1)
                    dve.sem_inc(g_free[n], 1)
                    if n == NBR - 1:
                        dve.sem_inc(merged, 1)
                for x in lo_done:
                    dve.sem_inc(x, 2)
                for x in acc_free:
                    dve.sem_inc(x, 1)
                turner.copy_lo(dve, jobs)
                tiles(dve, split, gate)


def program(nc, a, out):
    def scratch(name, shape):
        return nc.dram_tensor(name, shape, F32).ap()

    x = a["x"][0]
    proj0 = scratch("proj0", [SEQ, a["w_in0"].shape[1]])
    seam(nc, "in0", a, x, norms=[a["norm0"]], projected=(a["w_in0"], proj0))
    y0 = scratch("y0", [SEQ, D])
    even_mix(nc, "even", a, proj0, y0)
    x1 = scratch("x1", [SEQ, D])
    proj1 = scratch("proj1", [SEQ, a["w_in1"].shape[1]])
    seam(nc, "in1", a, x, (y0, proj0[:, EVEN_MIX:], a["w_out0"]), [a["norm1"]], x1, projected=(a["w_in1"], proj1))
    y1 = scratch("y1", [SEQ, D])
    odd_mix(nc, "odd", a, proj1, a["b_f1"], y1)
    x3 = scratch("x3", [SEQ, D])
    p2 = {n[:-2]: v[0] for n, v in a.items() if n.endswith("_2") and n != "final_norm_w_2"}
    proj = scratch("proj2", [SEQ, N_IN])
    seam(nc, "in2", a, x1, (y1, proj1[:, ODD_MIX:], a["w_out1"]), [a["norm_f"], p2["norm_w"]], rows_out=x3,
         projected=(p2["w_in"], proj))
    oa, ob, oc, yg = (scratch(n, [SEQ, 1024]) for n in ("oa", "ob", "oc", "yg"))
    gdn(nc, "gdn", a, proj, p2["gdn_conv_w"], p2["gdn_a_log"], p2["gdn_dt_bias"], p2["gdn_norm_w"], oa)
    rw = [scratch(f"rw_{n}", [SEQ, R_W]) for n in ("al", "be", "ka", "rh", "v", "bonus")]
    carry = scratch("rw_carry", [P, R_W // P])
    rp = {n[5:]: v for n, v in p2.items() if n.startswith("rwkv_")}
    rwkv_prepare(nc, "rwp", a, proj, rp["mu"], rp["w0"], rp["w_up"], rp["a0"], rp["a_up"], rp["k_k"], rp["k_a"],
                 rp["r_k"].rearrange("h d -> (h d)"), *rw, carry)
    rwkv(nc, "rwk", a, proj, *rw, carry, rp["lnx_w"], rp["lnx_b"], ob)
    s5_scan(nc, "s5", a, proj, p2["s5_a_re"], p2["s5_a_im"], p2["s5_log_dt"], p2["s5_b_re"], p2["s5_b_im"],
            p2["s5_c_re"], p2["s5_c_im"], p2["s5_d"], yg)
    s5_glu(nc, "glu", a, proj, yg, p2["s5_glu_w"], p2["s5_glu_b"], oc)
    mg = scratch("merged", [SEQ, D])
    merge(nc, "merge", a, proj, (oa, ob, oc), p2["w_branch"], p2["gate_b"], mg)
    seam(nc, "out2", a, x3, (mg, None, p2["w_out"]), [a["final_norm_w_2"]], rows_out=out[0])


def constants():
    f = np.float32
    t = np.arange(SEQ)
    c = {"ident": np.eye(P, dtype=f)}
    for n, d in (("", HD), ("i", DI)):
        inv = (f(10000.0) ** (-np.arange(d // 2, dtype=f) / f(d // 2))).astype(f)
        ang = (t.astype(f)[:, None] * inv[None, :]).astype(f)
        c["cos" + n], c["sin" + n] = np.cos(ang).astype(f), np.sin(ang).astype(f)
    dist = t[:, None] - t[None, :]
    before = dist >= 0
    c["causal"] = np.where(before, 0.0, NEG).astype(f)
    times = sum((before & (dist % dil == 0) & (dist // dil <= win // dil)).astype(f)
                for win, dil in ((128, 1), (512, 4), (2048, 16)))
    c["count"] = times.astype(f)
    r = np.arange(P)
    c["before"] = (r[:, None] < r[None, :]).astype(f)
    c["upto"] = (r[:, None] <= r[None, :]).astype(f)
    c["after"] = (r[:, None] >= r[None, :]).astype(f)
    c["low"] = np.where(r[None, :] < r[:, None], 0.0, NEG).astype(f)
    c["upi"] = np.where(r[:, None] <= r[None, :], 0.0, NEG).astype(f)
    joins = [((r[:, None] // b % 2 == 1) & (r[None, :] // b == r[:, None] // b - 1)).astype(f) for b in (1,) + LEVELS]
    c["join1"], c["join1T"] = joins[0], np.ascontiguousarray(joins[0].T)
    c["joins"] = np.concatenate([j[:, r // b % 2 == 0] for j, b in zip(joins[1:], LEVELS)], axis=1)
    c["low1"] = (r[None, :] < r[:, None]).astype(f)
    c["mid_in"] = (c["upto"] - f(0.5)).astype(f)
    c["mid_ex"] = (c["before"] - f(0.5)).astype(f)
    c["half"] = np.full((P, 1), 0.5, f)
    odd = (r // S_C % 2).astype(f)
    c["parity"] = np.stack([1 - odd, odd, odd - 1, -odd], axis=1).astype(f)
    c["ones"] = np.ones((P, P), f)
    c["pick"] = np.repeat(np.eye(8, dtype=f), P, axis=1)
    c["band"] = np.where(times > 0, 0.0, NEG).astype(f)
    return c


def kernel(**inputs):
    from concourse import bacc
    from concourse.bass_utils import run_bass_kernel_spmd

    nc = bacc.Bacc("TRN2", target_bir_lowering=False, num_devices=1)
    arrays, aps = {}, {}
    for name, value in list(inputs.items()) + [("const_" + n, v) for n, v in constants().items()]:
        arrays["in_" + name] = np.ascontiguousarray(value)
        aps[name.removeprefix("const_")] = nc.dram_tensor(
            "in_" + name, arrays["in_" + name].shape, mybir.dt.from_np(arrays["in_" + name].dtype),
            kind="ExternalInput").ap()
    out = nc.dram_tensor("out", (1, SEQ, D), F32, kind="ExternalOutput").ap()
    program(nc, aps, out)
    result = run_bass_kernel_spmd(nc, [arrays], core_ids=[0])
    return result.results[0]["out"]
```
